# Optimizing a Trainium2 kernel written in Bass

```python
import math
import jax
import jax.numpy as jnp
from jax import lax
import numpy as np

D_MODEL = 1024
BATCH = 1
SEQ = 1024
DEPTH = 1
DEC_BATCH = 8
DEC_SEQ = 4
PAST_LEN = 8192
PAGE_SIZE = 128

SSM_D_INNER = 1536
SSM_HEAD_DIM = 64
SSM_HEADS = SSM_D_INNER // SSM_HEAD_DIM
SSM_GROUPS = 4
SSM_HEADS_PER_GROUP = SSM_HEADS // SSM_GROUPS
SSM_STATE = 128
SSM_CONV = 4
SSM_CHUNK = 128
SSM_CONV_DIM = SSM_D_INNER + 2 * SSM_GROUPS * SSM_STATE
GM_WIDTH = 512
GM_GROUPS = 4
GM_GROUP_DIM = GM_WIDTH // GM_GROUPS
GM_CHUNK = 128
IN_DIM = SSM_D_INNER + SSM_CONV_DIM + SSM_HEADS + 2 * GM_WIDTH
MEM_LEN = 256
MEM_HEADS = 4
MEM_HEAD_DIM = D_MODEL // MEM_HEADS
MOE_GROUPS = 4
MOE_EXPERTS_PER_GROUP = 4
MOE_EXPERTS = MOE_GROUPS * MOE_EXPERTS_PER_GROUP
MOE_TOP_K = 2
MOE_D_FF = 512
MOE_BLOCK = 128
NORM_EPS = 1e-6

kernel_name = 'hybrid_ssd_gmlp_hmoe_decode_step'

def rmsnorm(x, g):
    xf = x.astype(jnp.float32)
    xf = xf * lax.rsqrt(jnp.mean(xf * xf, axis=-1, keepdims=True) + NORM_EPS)
    return (xf * g.astype(jnp.float32)).astype(x.dtype)

def layernorm(x, g, b):
    xf = x.astype(jnp.float32)
    xc = xf - jnp.mean(xf, axis=-1, keepdims=True)
    var = jnp.mean(xc * xc, axis=-1, keepdims=True)
    return (xc * lax.rsqrt(var + NORM_EPS) * g.astype(jnp.float32) + b.astype(jnp.float32)).astype(x.dtype)

def gated_rmsnorm(y, z, g):
    yz = y.astype(jnp.float32) * jax.nn.silu(z.astype(jnp.float32))
    shp = yz.shape
    yz = yz.reshape(shp[:-1] + (SSM_GROUPS, SSM_D_INNER // SSM_GROUPS))
    yz = yz * lax.rsqrt(jnp.mean(yz * yz, axis=-1, keepdims=True) + NORM_EPS)
    return (yz.reshape(shp) * g.astype(jnp.float32)).astype(z.dtype)

def causal_depthwise_conv(xbc, prev, w, b):
    xpad = jnp.concatenate([prev.astype(xbc.dtype), xbc], axis=1)
    out = lax.conv_general_dilated(
        xpad, w[:, None, :].astype(xbc.dtype), window_strides=(1,), padding='VALID',
        dimension_numbers=('NWC', 'WIO', 'NWC'), feature_group_count=SSM_CONV_DIM)
    return out + b.astype(xbc.dtype), xpad[:, xpad.shape[1] - (SSM_CONV - 1):]

def ssd_scan(x, dt, a, bmat, cmat, h0):
    bsz, L = x.shape[:2]
    cs = SSM_CHUNK if L % SSM_CHUNK == 0 else L
    nc = L // cs
    G, R, P, N = SSM_GROUPS, SSM_HEADS_PER_GROUP, SSM_HEAD_DIM, SSM_STATE
    xf = x.astype(jnp.float32).reshape(bsz, nc, cs, G, R, P)
    dtc = dt.reshape(bsz, nc, cs, G, R)
    bc = bmat.astype(jnp.float32).reshape(bsz, nc, cs, G, N)
    cc = cmat.astype(jnp.float32).reshape(bsz, nc, cs, G, N)
    acs_l = jnp.cumsum(dtc * a.reshape(G, R), axis=2)
    acs = jnp.moveaxis(acs_l, 2, -1)
    xdt = xf * dtc[..., None]
    tril = jnp.tril(jnp.ones((cs, cs), dtype=bool))
    seg = acs[..., :, None] - acs[..., None, :]
    decay = jnp.exp(jnp.where(tril, seg, -jnp.inf))
    cb = jnp.einsum('bclgn,bcsgn->bcgls', cc, bc)
    att = cb[:, :, :, None] * decay
    y_diag = jnp.einsum('bcgrls,bcsgrp->bclgrp', att, xdt)
    decay_to_end = jnp.exp(acs_l[:, :, -1:] - acs_l)
    states = jnp.einsum('bclgn,bclgrp->bcgrpn', bc, xdt * decay_to_end[..., None])
    chunk_decay = jnp.exp(acs_l[:, :, -1])

    def step(h, inp):
        st, dec = inp
        return h * dec[..., None, None] + st, h

    h_init = h0.astype(jnp.float32).reshape(bsz, G, R, P, N)
    h_last, h_starts = lax.scan(step, h_init, (jnp.moveaxis(states, 1, 0), jnp.moveaxis(chunk_decay, 1, 0)))
    h_starts = jnp.moveaxis(h_starts, 0, 1)
    y_off = jnp.einsum('bclgn,bcgrpn->bclgrp', cc, h_starts) * jnp.exp(acs_l)[..., None]
    y = (y_diag + y_off).reshape(bsz, L, SSM_HEADS, P)
    return y, h_last.reshape(bsz, SSM_HEADS, P, N)

def spatial_gating(u, v, ws, bs):
    bsz, L, _ = v.shape
    nc = -(-L // GM_CHUNK)
    lp_ = nc * GM_CHUNK
    vp = jnp.pad(v, ((0, 0), (0, lp_ - L), (0, 0))).reshape(bsz, nc, GM_CHUNK, GM_GROUPS, GM_GROUP_DIM)
    w_causal = jnp.where(jnp.tril(jnp.ones((GM_CHUNK, GM_CHUNK), dtype=bool)), ws, 0.0).astype(v.dtype)
    s = jnp.einsum('gts,bcsgk->bctgk', w_causal, vp) + bs.T[:, :, None].astype(v.dtype)
    s = s.reshape(bsz, lp_, GM_WIDTH)[:, :L]
    return u * s

def hier_moe(x, w_rg, b_rg, w_re, b_re, w_eg, w_eu, w_ed):
    shp = x.shape
    xt = x.reshape(-1, D_MODEL)
    T = xt.shape[0]
    lg = (xt @ w_rg).astype(jnp.float32) + b_rg.astype(jnp.float32)
    pg = jax.nn.softmax(lg, axis=-1)
    gid = jnp.argmax(lg, axis=-1).astype(jnp.int32)
    gw = jnp.take_along_axis(pg, gid[:, None], axis=1)[:, 0]
    le = (xt @ w_re).astype(jnp.float32).reshape(T, MOE_GROUPS, MOE_EXPERTS_PER_GROUP) + b_re.astype(jnp.float32)
    le_sel = jnp.take_along_axis(le, gid[:, None, None], axis=1)[:, 0]
    top_v, top_i = lax.top_k(le_sel, MOE_TOP_K)
    wts = gw[:, None] * jax.nn.softmax(top_v, axis=-1)
    eid = gid[:, None] * MOE_EXPERTS_PER_GROUP + top_i.astype(jnp.int32)
    flat_e = eid.reshape(-1)
    flat_tok = jnp.repeat(jnp.arange(T, dtype=jnp.int32), MOE_TOP_K)
    flat_w = wts.reshape(-1)
    order = jnp.argsort(flat_e)
    se, stok, sw = flat_e[order], flat_tok[order], flat_w[order]
    counts = jax.ops.segment_sum(jnp.ones_like(flat_e), flat_e, num_segments=MOE_EXPERTS)
    starts = jnp.cumsum(counts) - counts
    padded = (counts + MOE_BLOCK - 1) // MOE_BLOCK * MOE_BLOCK
    pad_ends = jnp.cumsum(padded)
    pad_starts = pad_ends - padded
    dest = pad_starts[se] + jnp.arange(T * MOE_TOP_K, dtype=jnp.int32) - starts[se]
    n_blocks = -(-(T * MOE_TOP_K) // MOE_BLOCK) + MOE_EXPERTS
    n_slots = n_blocks * MOE_BLOCK
    slot_tok = jnp.full((n_slots,), T, dtype=jnp.int32).at[dest].set(stok)
    slot_w = jnp.zeros((n_slots,), jnp.float32).at[dest].set(sw)
    block_e = jnp.minimum(
        jnp.searchsorted(pad_ends, jnp.arange(n_blocks, dtype=jnp.int32) * MOE_BLOCK, side='right'),
        MOE_EXPERTS - 1)
    x_pad = jnp.concatenate([xt, jnp.zeros((1, D_MODEL), xt.dtype)], axis=0)

    def expert_block(args):
        toks, e = args
        xb = x_pad[toks]
        h = jax.nn.silu(xb @ w_eg[e]) * (xb @ w_eu[e])
        return h @ w_ed[e]

    out = lax.map(expert_block, (slot_tok.reshape(n_blocks, MOE_BLOCK), block_e)).reshape(n_slots, D_MODEL)
    y = jnp.zeros((T + 1, D_MODEL), jnp.float32).at[slot_tok].add(out.astype(jnp.float32) * slot_w[:, None])
    return y[:T].astype(x.dtype).reshape(shp)

def memory_kv(mem, g, wk, wv):
    mn = rmsnorm(mem, g)
    b, m = mem.shape[:2]
    k = (mn @ wk).reshape(b, m, MEM_HEADS, MEM_HEAD_DIM)
    v = (mn @ wv).reshape(b, m, MEM_HEADS, MEM_HEAD_DIM)
    return k, v

def cross_attend(xn, k, v, wq, wo):
    b, L = xn.shape[:2]
    q = (xn @ wq).reshape(b, L, MEM_HEADS, MEM_HEAD_DIM)
    s = jnp.einsum('blhd,bmhd->bhlm', q, k.astype(q.dtype)).astype(jnp.float32) * (MEM_HEAD_DIM ** -0.5)
    p = jax.nn.softmax(s, axis=-1).astype(q.dtype)
    o = jnp.einsum('bhlm,bmhd->blhd', p, v.astype(q.dtype)).reshape(b, L, D_MODEL)
    return o @ wo

def mixer_block(xn, conv_prev, h0, lp):
    bsz, L = xn.shape[:2]
    proj = xn @ lp['w_in']
    s1 = SSM_D_INNER
    s2 = s1 + SSM_CONV_DIM
    s3 = s2 + SSM_HEADS
    z, xbc, dt_raw, gm = proj[..., :s1], proj[..., s1:s2], proj[..., s2:s3], proj[..., s3:]
    xbc, conv_new = causal_depthwise_conv(xbc, conv_prev, lp['conv_w'], lp['conv_b'])
    xbc = jax.nn.silu(xbc)
    nb = SSM_GROUPS * SSM_STATE
    xs = xbc[..., :SSM_D_INNER].reshape(bsz, L, SSM_HEADS, SSM_HEAD_DIM)
    bm = xbc[..., SSM_D_INNER:SSM_D_INNER + nb].reshape(bsz, L, SSM_GROUPS, SSM_STATE)
    cm = xbc[..., SSM_D_INNER + nb:].reshape(bsz, L, SSM_GROUPS, SSM_STATE)
    dt = jax.nn.softplus(dt_raw.astype(jnp.float32) + lp['dt_bias'].astype(jnp.float32))
    a = -jnp.exp(lp['a_log'].astype(jnp.float32))
    y, h_new = ssd_scan(xs, dt, a, bm, cm, h0)
    y = y + lp['d_skip'].astype(jnp.float32)[:, None] * xs.astype(jnp.float32)
    y = gated_rmsnorm(y.reshape(bsz, L, SSM_D_INNER), z, lp['ssm_norm'])
    a_out = y @ lp['w_a_proj']
    gm = jax.nn.gelu(gm, approximate=False)
    u, v = gm[..., :GM_WIDTH], gm[..., GM_WIDTH:]
    v = layernorm(v, lp['gm_ln_g'], lp['gm_ln_b'])
    b_out = spatial_gating(u, v, lp['gm_ws'], lp['gm_bs']) @ lp['w_b_proj']
    gates = jax.nn.sigmoid(xn @ lp['w_gate'] + lp['b_gate'])
    merged = gates[..., :D_MODEL] * a_out + gates[..., D_MODEL:] * b_out
    return merged @ lp['w_out'], conv_new, h_new, v

def decoder_layer(x, mem_k, mem_v, conv_prev, h0, lp):
    out, conv_new, h_new, v_rows = mixer_block(rmsnorm(x, lp['norm_mix']), conv_prev, h0, lp)
    x = x + out
    x = x + cross_attend(rmsnorm(x, lp['norm_mem']), mem_k, mem_v, lp['w_mem_q'], lp['w_mem_o'])
    x = x + hier_moe(rmsnorm(x, lp['norm_ffn']), lp['w_router_group'], lp['b_router_group'],
                     lp['w_router_expert'], lp['b_router_expert'],
                     lp['w_expert_gate'], lp['w_expert_up'], lp['w_expert_down'])
    return x, conv_new, h_new, v_rows

def setup_inputs(seed: int = 0) -> dict:
    key = jax.random.key(seed)
    ks = iter(jax.random.split(key, 48))

    def nrm(shape, scale):
        return scale * jax.random.normal(next(ks), shape, jnp.float32)

    dt0 = jnp.exp(jax.random.uniform(next(ks), (DEPTH, SSM_HEADS), jnp.float32,
                                     minval=math.log(1e-3), maxval=math.log(1e-1)))
    dt_bias = dt0 + jnp.log(-jnp.expm1(-dt0))
    a_log = jnp.log(jax.random.uniform(next(ks), (DEPTH, SSM_HEADS), jnp.float32, minval=1.0, maxval=16.0))
    return {
        'x_prompt': nrm((BATCH, SEQ, D_MODEL), 1.0),
        'x_sample': nrm((DEC_BATCH, DEC_SEQ, D_MODEL), 1.0),
        'mem_prompt': nrm((BATCH, MEM_LEN, D_MODEL), 1.0),
        'state_ssm': nrm((DEPTH, DEC_BATCH, SSM_HEADS, SSM_HEAD_DIM, SSM_STATE), 0.3),
        'state_conv': nrm((DEPTH, DEC_BATCH, SSM_CONV - 1, SSM_CONV_DIM), 1.0),
        'cache_mem_k': nrm((DEPTH, DEC_BATCH, MEM_LEN, MEM_HEADS, MEM_HEAD_DIM), 1.0),
        'cache_mem_v': nrm((DEPTH, DEC_BATCH, MEM_LEN, MEM_HEADS, MEM_HEAD_DIM), 1.0),
        'norm_mix': 1.0 + nrm((DEPTH, D_MODEL), 0.05),
        'w_in': nrm((DEPTH, D_MODEL, IN_DIM), D_MODEL ** -0.5),
        'conv_w': nrm((DEPTH, SSM_CONV, SSM_CONV_DIM), 0.5),
        'conv_b': nrm((DEPTH, SSM_CONV_DIM), 0.02),
        'dt_bias': dt_bias,
        'a_log': a_log,
        'd_skip': 1.0 + nrm((DEPTH, SSM_HEADS), 0.1),
        'ssm_norm': 1.0 + nrm((DEPTH, SSM_D_INNER), 0.05),
        'w_a_proj': nrm((DEPTH, SSM_D_INNER, D_MODEL), SSM_D_INNER ** -0.5),
        'gm_ln_g': 1.0 + nrm((DEPTH, GM_WIDTH), 0.05),
        'gm_ln_b': nrm((DEPTH, GM_WIDTH), 0.02),
        'gm_ws': nrm((DEPTH, GM_GROUPS, GM_CHUNK, GM_CHUNK), GM_CHUNK ** -0.5),
        'gm_bs': 1.0 + nrm((DEPTH, GM_GROUPS, GM_CHUNK), 0.1),
        'w_b_proj': nrm((DEPTH, GM_WIDTH, D_MODEL), GM_WIDTH ** -0.5),
        'w_gate': nrm((DEPTH, D_MODEL, 2 * D_MODEL), D_MODEL ** -0.5),
        'b_gate': nrm((DEPTH, 2 * D_MODEL), 0.1),
        'w_out': nrm((DEPTH, D_MODEL, D_MODEL), D_MODEL ** -0.5),
        'norm_mem': 1.0 + nrm((DEPTH, D_MODEL), 0.05),
        'norm_memkv': 1.0 + nrm((DEPTH, D_MODEL), 0.05),
        'w_mem_q': nrm((DEPTH, D_MODEL, D_MODEL), D_MODEL ** -0.5),
        'w_mem_k': nrm((DEPTH, D_MODEL, D_MODEL), D_MODEL ** -0.5),
        'w_mem_v': nrm((DEPTH, D_MODEL, D_MODEL), D_MODEL ** -0.5),
        'w_mem_o': nrm((DEPTH, D_MODEL, D_MODEL), D_MODEL ** -0.5),
        'norm_ffn': 1.0 + nrm((DEPTH, D_MODEL), 0.05),
        'w_router_group': nrm((DEPTH, D_MODEL, MOE_GROUPS), D_MODEL ** -0.5),
        'b_router_group': nrm((DEPTH, MOE_GROUPS), 0.01),
        'w_router_expert': nrm((DEPTH, D_MODEL, MOE_EXPERTS), D_MODEL ** -0.5),
        'b_router_expert': nrm((DEPTH, MOE_GROUPS, MOE_EXPERTS_PER_GROUP), 0.01),
        'w_expert_gate': nrm((DEPTH, MOE_EXPERTS, D_MODEL, MOE_D_FF), D_MODEL ** -0.5),
        'w_expert_up': nrm((DEPTH, MOE_EXPERTS, D_MODEL, MOE_D_FF), D_MODEL ** -0.5),
        'w_expert_down': nrm((DEPTH, MOE_EXPERTS, MOE_D_FF, D_MODEL), MOE_D_FF ** -0.5),
        'norm_final': 1.0 + nrm((D_MODEL,), 0.05),
    }

def reference(x_prompt, x_sample, mem_prompt, state_ssm, state_conv, cache_mem_k, cache_mem_v,
              norm_mix, w_in, conv_w, conv_b, dt_bias, a_log, d_skip, ssm_norm, w_a_proj,
              gm_ln_g, gm_ln_b, gm_ws, gm_bs, w_b_proj, w_gate, b_gate, w_out,
              norm_mem, norm_memkv, w_mem_q, w_mem_k, w_mem_v, w_mem_o,
              norm_ffn, w_router_group, b_router_group, w_router_expert, b_router_expert,
              w_expert_gate, w_expert_up, w_expert_down, norm_final):
    xp, xs = x_prompt, x_sample
    bp = x_prompt.shape[0]
    ssm_p, conv_p, mk_p, mv_p = [], [], [], []
    ssm_s, conv_s, gv_s = [], [], []
    for l in range(DEPTH):
        lp = {
            'norm_mix': norm_mix[l], 'w_in': w_in[l], 'conv_w': conv_w[l], 'conv_b': conv_b[l],
            'dt_bias': dt_bias[l], 'a_log': a_log[l], 'd_skip': d_skip[l], 'ssm_norm': ssm_norm[l],
            'w_a_proj': w_a_proj[l], 'gm_ln_g': gm_ln_g[l], 'gm_ln_b': gm_ln_b[l], 'gm_ws': gm_ws[l],
            'gm_bs': gm_bs[l], 'w_b_proj': w_b_proj[l], 'w_gate': w_gate[l], 'b_gate': b_gate[l],
            'w_out': w_out[l], 'norm_mem': norm_mem[l], 'w_mem_q': w_mem_q[l], 'w_mem_o': w_mem_o[l],
            'norm_ffn': norm_ffn[l], 'w_router_group': w_router_group[l],
            'b_router_group': b_router_group[l], 'w_router_expert': w_router_expert[l],
            'b_router_expert': b_router_expert[l], 'w_expert_gate': w_expert_gate[l],
            'w_expert_up': w_expert_up[l], 'w_expert_down': w_expert_down[l],
        }
        k_p, v_p = memory_kv(mem_prompt, norm_memkv[l], w_mem_k[l], w_mem_v[l])
        conv0 = jnp.zeros((bp, SSM_CONV - 1, SSM_CONV_DIM), xp.dtype)
        h0 = jnp.zeros((bp, SSM_HEADS, SSM_HEAD_DIM, SSM_STATE), jnp.float32)
        xp, c_new, h_new, _ = decoder_layer(xp, k_p, v_p, conv0, h0, lp)
        ssm_p.append(h_new)
        conv_p.append(c_new)
        mk_p.append(k_p)
        mv_p.append(v_p)
        xs, c_new_s, h_new_s, v_rows_s = decoder_layer(xs, cache_mem_k[l], cache_mem_v[l],
                                                       state_conv[l], state_ssm[l], lp)
        ssm_s.append(h_new_s)
        conv_s.append(c_new_s)
        gv_s.append(v_rows_s)
    y_prompt = rmsnorm(xp, norm_final)
    y_sample = rmsnorm(xs, norm_final)
    return (y_prompt, y_sample,
            jnp.stack(ssm_p), jnp.stack(conv_p), jnp.stack(mk_p), jnp.stack(mv_p),
            jnp.stack(ssm_s), jnp.stack(conv_s), jnp.stack(gv_s))


_drawn_inputs = setup_inputs


def setup_inputs(seed=0):
    import zlib

    import numpy as np

    out = dict(_drawn_inputs(seed))
    spreads = {}
    factors = {'gm_ln_b': 2.973, 'norm_mem': 4.994, 'b_router_group': 22.803, 'b_router_expert': 5.43}
    for name, (base, spread) in spreads.items():
        noise = np.random.default_rng([zlib.crc32(name.encode()), seed]).standard_normal(out[name].shape)
        drawn = base * np.exp(spread * noise) if base else spread * noise
        out[name] = jnp.asarray(drawn.astype(out[name].dtype))
    for name, factor in factors.items():
        out[name] = (out[name] * factor).astype(out[name].dtype)
    return out
```

```python
from contextlib import ExitStack

import numpy as np

import concourse.bass as bass
import concourse.mybir as mybir
from concourse.alu_op_type import AluOpType as ALU

ACT = mybir.ActivationFunctionType
AX = mybir.AxisListType.X
F32 = mybir.dt.float32
I32 = mybir.dt.int32
U32 = mybir.dt.uint32

P = 128
BANK = 512
D = 1024
SEQ = 1024
NB, LS = 8, 4
NS = NB * LS
T = SEQ + NS
NC = SEQ // P
NT = NC + 1
TP = NT * P
DK = D // P
H, HD, G, R, N = 24, 64, 4, 6, 128
DI = H * HD
GW = R * HD
CONV = 4
CD = DI + 2 * G * N
CF = CD // P
XF = DI // P
GM = 512
GMF = GM // P
ML, MH, MD = 256, 4, 256
MT = ML // P
NG, EPG = 4, 4
NE = NG * EPG
FF = 512
FK = FF // P
EPS = 1e-6
COL_XBC, COL_DT = DI, DI + CD
COL_U = COL_DT + H
COL_V = COL_U + GM
SLAB = T // 3
NBLK = (2 * T + P - 1) // P + NE
NBLK += NBLK % 2
NSLOT = NBLK * P
SCALE = MD ** -0.5
BIG = 1.0e30


class Chain:

    def __init__(self, eng, sem, base=0):
        self.eng, self.sem, self.base, self.n = eng, sem, base, 0

    def done(self, ins):
        self.n += 1
        ins.then_inc(self.sem, 1)
        self.eng.wait_ge(self.sem, self.base + self.n)


def mid(ap, n):
    return ap.unsqueeze(1).to_broadcast([ap.shape[0], n, ap.shape[1]])


def last(ap, n):
    return ap.unsqueeze(2).to_broadcast([ap.shape[0], ap.shape[1], n])


class Prog:

    def __init__(self, nc, d, out, stages):
        self.nc, self.d, self.out, self.stages = nc, d, out, stages
        self.ctx = ExitStack()
        self.names, self.sems, self.n_out = [], [], 0

    def sb(self, name, shape, dt=F32, ctx=None):
        if name in self.names:
            name = f"{name}_{len(self.names)}"
        self.names.append(name)
        return (ctx or self.ctx).enter_context(self.nc.sbuf_tensor(name, list(shape), dt))

    def stored(self):
        self.n_out += 1
        return 16

    def sem(self, name):
        s = self.nc.alloc_semaphore(name)
        self.sems.append(s)
        return s

    def renew_semaphores(self):
        self.nc.clear_and_free_semaphores(self.sems)
        self.nc.all_engine_barrier()
        self.sems = []


VEC_A = CONV * CF + CF
VEC = {"norm_mix": 0, "norm_mem": 8, "norm_memkv": 16, "norm_ffn": 24, "b_gate": 32, "ssm_norm": 48}
VEC_B = 60


def stage_constants(g):
    nc, d = g.nc, g.d
    ps = g.psum
    with ExitStack() as ctx:
        va = g.sb("va", [VEC_A, P], ctx=ctx)
        vb = g.sb("vb", [VEC_B, P], ctx=ctx)
        sc = g.sb("sc_rows", [3 * NB, CD], ctx=ctx)
        alog = g.sb("alog", [P, H], ctx=ctx)
        s_vec = g.sem("c_vec_loaded")
        s_row = g.sem("c_rows_loaded")
        s_alog = g.sem("c_alog_loaded")
        s_one = g.sem("c_ones")
        s_msk = g.sem("c_masks")
        s_tr = g.sem("c_vec_turned")
        s_tr2 = g.sem("c_state_turned")
        s_ev = g.sem("c_evacuated")
        s_exp = g.sem("c_exp")
        block = ctx.enter_context(nc.Block("constants"))

        @block.sync
        def _(sp):
            for i, (name, n) in enumerate((("conv_w", CONV * CF), ("conv_b", CF))):
                sp.dma_start(va[i * CONV * CF:i * CONV * CF + n, :],
                             g.flat[name].rearrange("(a b) -> a b", b=P)).then_inc(s_vec, 16)
            for name, at in VEC.items():
                n = g.flat[name].shape[0] // P
                sp.dma_start(vb[at:at + n, :], g.flat[name].rearrange("(a b) -> a b", b=P)).then_inc(s_vec, 16)
            sp.dma_start(sc[:], d["state_conv"][0].rearrange("b r c -> (b r) c")).then_inc(s_vec, 16)
            sp.dma_start(alog[:], d["a_log"][0].partition_broadcast(P)).then_inc(s_alog, 16)
            for dst, name in ((g.dtb[:], "dt_bias"), (g.dskip[:], "d_skip"), (g.lng[:], "gm_ln_g"),
                              (g.lnb[:], "gm_ln_b"), (g.bs[:].rearrange("p g t -> p (g t)"), "gm_bs")):
                sp.dma_start(dst, g.flat[name].partition_broadcast(P)).then_inc(s_row, 16)
            sp.wait_ge(s_row, 16 * 5)

        @block.gpsimd
        def _(pool):
            nc.gpsimd.memset(g.ones[:], 1.0).then_inc(s_one, 1)
            nc.gpsimd.memset(g.mhalf[:], -0.5)
            nc.gpsimd.memset(g.eps[:], EPS)
            nc.gpsimd.memset(g.colmask[:], 1.0)
            nc.gpsimd.memset(g.rowmask[:], 1.0).then_inc(s_one, 1)
            pool.wait_ge(s_one, 2)
            sel = nc.gpsimd.affine_select
            one, sq = g.ones, [[1, P]]
            sel(g.ident[:], one[:], sq, ALU.is_equal, 0.0, 0, -1)
            sel(g.tri[:], one[:], sq, ALU.is_ge, 0.0, 0, -1)
            sel(g.stri[:], one[:], sq, ALU.is_gt, 0.0, 0, -1)
            quad = [[LS, NB], [0, LS]]
            sel(g.same[:], one[0:NS, 0:NS], [[-LS, NB], [0, LS]], ALU.is_ge, 0.0, 0, 1).then_inc(s_msk, 1)
            sel(g.colmask[:], g.colmask[:], [[-LS, NB], [1, NS]], ALU.is_ge, 0.0, 0, 0).then_inc(s_msk, 1)
            sel(g.rowmask[:], g.rowmask[:], [[-LS, NB]], ALU.is_ge, 0.0, 0, 1).then_inc(s_msk, 1)
            pool.wait_ge(s_msk, 3)
            sel(g.same[:], g.same[:], quad, ALU.is_ge, 0.0, LS - 1, -1).then_inc(s_msk, 1)
            sel(g.colmask[:], g.colmask[:], [[LS, NB], [-1, NS]], ALU.is_ge, 0.0, LS - 1, 0)
            sel(g.rowmask[:], g.rowmask[:], [[LS, NB]], ALU.is_ge, 0.0, LS - 1, -1)
            pool.wait_ge(s_msk, 4)
            sel(g.btri[:], g.same[:], [[1, NS]], ALU.is_ge, 0.0, 0, -1).then_inc(s_msk, 1)

        @block.tensor
        def _(pe):
            pe.wait_ge(s_msk, 5)
            pe.wait_ge(s_vec, 16 * 9)
            nc.tensor.transpose(ps[:, 0, 0:VEC_A], va[:], g.ident[0:VEC_A, 0:VEC_A])
            nc.tensor.transpose(ps[:, 1, 0:VEC_B], vb[:], g.ident[0:VEC_B, 0:VEC_B]).then_inc(s_tr, 1)
            for f in range(CF):
                tr = nc.tensor.transpose(ps[:, 2, f * 3 * NB:(f + 1) * 3 * NB], sc[:, f * P:(f + 1) * P],
                                         g.ident[0:3 * NB, 0:3 * NB])
            tr.then_inc(s_tr2, 1)

        @block.scalar
        def _(act):
            act.wait_ge(s_alog, 16)
            nc.scalar.activation(alog[:], alog[:], ACT.Exp).then_inc(s_exp, 1)

        @block.vector
        def _(dve):
            dve.wait_ge(s_exp, 1)
            nc.vector.tensor_scalar(g.aneg[:], alog[:], -1.0, None, ALU.mult)
            dve.wait_ge(s_tr, 1)
            nc.vector.tensor_copy(g.veca[:], ps[:, 0, 0:VEC_A])
            nc.vector.tensor_copy(g.vecb[:], ps[:, 1, 0:VEC_B])
            dve.wait_ge(s_tr2, 1)
            nc.vector.tensor_copy(g.cst[:].rearrange("p f r -> p (f r)"), ps[:, 2, 0:CF * 3 * NB]).then_inc(s_ev, 1)


def stage_norm(g, tag, x, gain, dst, tiles, x_dram=None, rows_dram=None):
    nc, ps = g.nc, g.psum
    RING = 3
    assert tiles % RING == 0 or tiles < RING
    ring = min(RING, tiles)
    with ExitStack() as ctx:
        xn = g.sb("n_xn", [P, ring, D], ctx=ctx)
        ss = g.sb("n_ss", [P, tiles], ctx=ctx)
        ms = g.sb("n_ms", [P, tiles], ctx=ctx)
        rstd = g.sb("n_rstd", [P, tiles], ctx=ctx)
        xg = g.sb("n_xg", [P, ring, D], ctx=ctx) if rows_dram else None
        s_x = g.sem(tag + "_x_loaded")
        s_zero = g.sem(tag + "_x_padded")
        s_sq = g.sem(tag + "_squares")
        s_ms = g.sem(tag + "_means")
        s_rstd = g.sem(tag + "_rstd")
        s_xn = g.sem(tag + "_xn_ready")
        s_tr = g.sem(tag + "_turned")
        s_free = g.sem(tag + "_psum_free")
        s_xfree = g.sem(tag + "_xn_free")
        s_xg = g.sem(tag + "_xg_ready")
        s_xgf = [g.sem(f"{tag}_xg_stored{i}") for i in range(ring)] if rows_dram else None
        block = ctx.enter_context(nc.Block(tag))

        @block.sync
        def _(sp):
            if x_dram:
                for i, (dst_ap, src) in enumerate(x_dram):
                    if i:
                        sp.wait_ge(s_zero, 1)
                    sp.dma_start(dst_ap, src).then_inc(s_x, 16)
            if rows_dram:
                with sp.Fori(0, tiles // ring) as i:
                    for q in range(ring):
                        sp.wait_ge(s_xg, i * ring + q + 1)
                        sp.dma_start(rows_dram[0].rearrange("(t p) n -> t p n", p=P)[i * ring + q],
                                     xg[:, q, :]).then_inc(s_xgf[q], 16)
                for q in range(ring):
                    sp.wait_ge(s_xgf[q], 16 * (tiles // ring))

        @block.gpsimd
        def _(pool):
            if tiles == NT and x_dram:
                nc.gpsimd.memset(x[:, NT - 1, :], 0.0).then_inc(s_zero, 1)
            pool.wait_ge(s_sq, tiles)
            nc.gpsimd.tensor_scalar(ms[:], ss[:], 1.0 / D, EPS, ALU.mult, ALU.add).then_inc(s_ms, 1)
            pool.wait_ge(s_ms, 1)
            nc.gpsimd.tensor_tensor(rstd[:], ms[:], g.mhalf[:, 0:tiles], ALU.pow).then_inc(s_rstd, 1)
            if rows_dram:
                with pool.Fori(0, tiles // ring) as i:
                    for q in range(ring):
                        pool.wait_ge(s_xn, i * ring + q + 1)
                        pool.wait_ge(s_xgf[q], i * 16)
                        nc.gpsimd.tensor_tensor(xg[:, q, :], xn[:, q, :], rows_dram[1][:], ALU.mult).then_inc(s_xg, 1)

        @block.scalar
        def _(act):
            if x_dram:
                act.wait_ge(s_x, 16 * len(x_dram))
            for t in range(tiles):
                if t >= ring:
                    act.wait_ge(s_sq, t - ring + 1)
                nc.scalar.activation(xn[:, t % ring, :], x[:, t, :], ACT.Square,
                                     accum_out=ss[:, t:t + 1]).then_inc(s_sq, 1)
            act.wait_ge(s_rstd, 1)
            for t in range(tiles):
                q = t % ring
                if t >= ring:
                    act.wait_ge(s_tr, t - ring + 1)
                    if rows_dram:
                        act.wait_ge(s_xg, t - ring + 1)
                nc.scalar.activation(xn[:, q, :], x[:, t, :], ACT.Copy, scale=rstd[:, t:t + 1]).then_inc(s_xn, 1)

        @block.tensor
        def _(pe):
            for t in range(tiles):
                q = t % ring
                pe.wait_ge(s_xn, t + 1)
                if t >= ring:
                    pe.wait_ge(s_free, t - ring + 1)
                for k in range(DK):
                    tr = nc.tensor.transpose(ps[:, 2 * q + k // 4, (k % 4) * P:(k % 4 + 1) * P],
                                             xn[:, q, k * P:(k + 1) * P], g.ident[:])
                tr.then_inc(s_tr, 1)

        @block.vector
        def _(dve):
            for t in range(tiles):
                q = t % ring
                dve.wait_ge(s_tr, t + 1)
                src = ps[:, 2 * q:2 * q + 2, :].rearrange("p b (k t) -> p (b k) t", t=P)
                nc.vector.tensor_tensor(dst[:, :, t * P:(t + 1) * P], src, last(gain, P),
                                        ALU.mult).then_inc(s_free, 1)


def load_weights(sp, ring, src_of, groups, s_loaded, s_done, per_group):
    half = per_group // 2
    for s in range(2):
        for dst, src in src_of(0, s):
            sp.dma_start(dst, src).then_inc(s_loaded[s], 16)
    if groups > 1:
        with sp.Fori(1, groups) as i:
            for s in range(2):
                sp.wait_ge(s_done, (i - 1) * per_group + (s + 1) * half)
                for dst, src in src_of(i, s):
                    sp.dma_start(dst, src).then_inc(s_loaded[s], 16)


def stage_rows(g):
    nc, ps, hT = g.nc, g.psum, g.R2T
    w_in = g.d["w_in"][0].rearrange("(k p) n -> p k n", p=P)
    NZ = DI // BANK
    with ExitStack() as ctx:
        w = g.sb("r_w", [P, 2, DK, BANK], ctx=ctx)
        wdt = g.sb("r_wdt", [P, DK, H], ctx=ctx)
        zs = g.sb("r_z", [P, 3, BANK], ctx=ctx)
        st = g.sb("r_stats", [P, NT, 6], ctx=ctx)
        mv = g.sb("r_mv", [P, NT, 2], ctx=ctx)
        rs = g.sb("r_rstd", [P, NT], ctx=ctx)
        t1 = g.sb("r_t1", [P, NT, H], ctx=ctx)
        t2 = g.sb("r_t2", [P, NT, H], ctx=ctx)
        tot = g.sb("r_tot", [P, NT, H], ctx=ctx)
        s_w = [g.sem(f"r_w_loaded{i}") for i in range(2)]
        s_wdt = g.sem("r_wdt_loaded")
        s_mm = g.sem("r_product")
        s_ev = g.sem("r_evacuated")
        s_zst = [g.sem(f"r_z_stored{i}") for i in range(3)]
        s_dt = g.sem("r_dt")
        s_pad = g.sem("r_padded")
        s_dta = g.sem("r_dt_chain")
        s_cum = g.sem("r_cum")
        s_v = g.sem("r_v_chain")
        s_vm = g.sem("r_v_stats")
        s_vo = g.sem("r_v_out")
        s_vr = g.sem("r_v_rstd")
        s_act = g.sem("r_act")
        block = ctx.enter_context(nc.Block("rows"))

        @block.sync
        def _(sp):
            sp.dma_start(w[:, 0], w_in[:, :, 0:BANK]).then_inc(s_w[0], 16)
            sp.dma_start(w[:, 1], w_in[:, :, BANK:2 * BANK]).then_inc(s_w[1], 16)
            with nc.allow_non_contiguous_dma(reason="24 columns of dt"):
                sp.dma_start(wdt[:], w_in[:, :, COL_DT:COL_DT + H]).then_inc(s_wdt, 16)
            sp.wait_ge(s_mm, NT)
            sp.dma_start(w[:, 0], w_in[:, :, 2 * BANK:3 * BANK]).then_inc(s_w[0], 16)
            sp.wait_ge(s_mm, 2 * NT)
            sp.dma_start(w[:, 1], w_in[:, :, COL_V:COL_V + BANK]).then_inc(s_w[1], 16)
            sp.wait_ge(s_vo, NT)
            sp.dma_start(g.out["gv"], g.v[0:NS, NT - 1, :]).then_inc(g.s_out, g.stored())
            sp.wait_ge(g.s_out, 16 * g.n_out)

        @block.tensor
        def _(pe):
            for j in range(NZ + 1):
                pe.wait_ge(s_w[j % 2], 16 * (j // 2 + 1))
                for c in range(NT):
                    n = j * NT + c
                    if n >= 3:
                        pe.wait_ge(s_ev, n - 2)
                    for k in range(DK):
                        mm = nc.tensor.matmul(ps[:, n % 3, :], hT[:, k, c * P:(c + 1) * P], w[:, j % 2, k, :],
                                              start=(k == 0), stop=(k == DK - 1))
                    mm.then_inc(s_mm, 1)
                if j == 0:
                    pe.wait_ge(s_wdt, 16)
                    for c in range(NT):
                        for k in range(DK):
                            mm = nc.tensor.matmul(ps[:, 3, c * H:(c + 1) * H], hT[:, k, c * P:(c + 1) * P],
                                                  wdt[:, k, :], start=(k == 0), stop=(k == DK - 1))
                    mm.then_inc(s_dt, 1)
                if j == 1:
                    pe.wait_ge(s_dta, 4)
                    a = g.dta[:, 0:NC, :].rearrange("p c h -> p (c h)")
                    nc.tensor.matmul(ps[:, 4, 0:NC * H], g.tri[:], a, start=True, stop=True)
                    nc.tensor.matmul(ps[0:NS, 4, NC * H:NT * H], g.btri[:], g.dta[0:NS, NC, :], start=True, stop=True)
                    nc.tensor.matmul(ps[:, 5, 0:NC * H], g.ones[:], a, start=True, stop=True)
                    nc.tensor.matmul(ps[0:NS, 5, NC * H:NT * H], g.same[:], g.dta[0:NS, NC, :],
                                     start=True, stop=True).then_inc(s_cum, 1)

        @block.scalar
        def _(act):
            def softplus():
                act.wait_ge(s_dta, 1)
                nc.scalar.activation(t1[:], t2[:], ACT.Abs).then_inc(s_act, 1)
                act.wait_ge(s_act, 1)
                nc.scalar.activation(t1[:], t1[:], ACT.Exp, scale=-1.0).then_inc(s_act, 1)
                act.wait_ge(s_act, 2)
                nc.scalar.activation(t1[:], t1[:], ACT.Ln, bias=1.0).then_inc(s_act, 1)

            def decays():
                act.wait_ge(s_dta, 5)
                nc.scalar.activation(g.eacs[:], g.acs[:], ACT.Exp)
                nc.scalar.activation(g.etot[:], tot[:], ACT.Exp)
                act.wait_ge(s_dta, 6)
                nc.scalar.activation(t1[:], t2[:], ACT.Exp).then_inc(s_act, 1)

            for j in range(NZ + 1):
                for c in range(NT):
                    n = j * NT + c
                    act.wait_ge(s_mm, n + 1)
                    if j < NZ:
                        if n >= 3:
                            act.wait_ge(s_zst[n % 3], 16 * (n // 3))
                        nc.scalar.activation(zs[:, n % 3, :], ps[:, n % 3, :], ACT.Silu).then_inc(s_ev, 1)
                        act.wait_ge(s_ev, n + 1)
                        act.dma_start(g.z_scr[c, :, j * BANK:(j + 1) * BANK], zs[:, n % 3, :]).then_inc(s_zst[n % 3], 16)
                    else:
                        nc.scalar.activation(g.v[:, c, :], ps[:, n % 3, :], ACT.Gelu).then_inc(s_ev, 1)
                if j == 0:
                    softplus()
                if j == 1:
                    decays()
            for s in range(3):
                act.wait_ge(s_zst[s], 16 * (NZ * NT // 3))

        @block.vector
        def _(dve):
            nc.vector.memset(g.acs[:, NC, :], 0.0)
            nc.vector.memset(tot[:, NC, :], 0.0).then_inc(s_pad, 1)
            dve.wait_ge(s_pad, 1)
            ch = Chain(dve, s_dta)
            dve.wait_ge(s_dt, 1)
            pdt = ps[:, 3, 0:NT * H].rearrange("p (c h) -> p c h", h=H)
            ch.done(nc.vector.tensor_tensor(t2[:], pdt, mid(g.dtb[:], NT), ALU.add))
            dve.wait_ge(s_act, 3)
            ch.done(nc.vector.tensor_scalar(g.dt[:], t2[:], 0.0, None, ALU.max))
            ch.done(nc.vector.tensor_tensor(g.dt[:], g.dt[:], t1[:], ALU.add))
            ch.done(nc.vector.tensor_tensor(g.dta[:], g.dt[:], mid(g.aneg[:], NT), ALU.mult))
            dve.wait_ge(s_cum, 1)
            for dst, b in ((g.acs, 4), (tot, 5)):
                nc.vector.tensor_copy(dst[:, 0:NC, :], ps[:, b, 0:NC * H].rearrange("p (c h) -> p c h", h=H))
                op = nc.vector.tensor_copy(dst[0:NS, NC, :], ps[0:NS, b, NC * H:NT * H])
            ch.done(op)
            ch.done(nc.vector.tensor_tensor(t2[:], tot[:], g.acs[:], ALU.subtract))
            dve.wait_ge(s_act, 4)
            ch.done(nc.vector.tensor_tensor(g.dte[:], g.dt[:], t1[:], ALU.mult))
            for c in range(NT):
                dve.wait_ge(s_ev, NZ * NT + c + 1)
                nc.vector.bn_stats(st[:, c, :], g.v[:, c, :]).then_inc(s_v, 1)
                dve.wait_ge(s_v, c + 1)
                nc.vector.bn_aggr(mv[:, c, :], st[:, c, :]).then_inc(s_vm, 1)
            dve.wait_ge(s_vr, 1)
            vc = Chain(dve, s_v, NT)
            for c in range(NT):
                vc.done(nc.vector.tensor_scalar(g.v[:, c, :], g.v[:, c, :], mv[:, c, 0:1], rs[:, c:c + 1],
                                                ALU.subtract, ALU.mult))
                vc.done(nc.vector.tensor_tensor(g.v[:, c, :], g.v[:, c, :], g.lng[:], ALU.mult))
                nc.vector.tensor_tensor(g.v[:, c, :], g.v[:, c, :], g.lnb[:], ALU.add).then_inc(s_vo, 1)

        @block.gpsimd
        def _(pool):
            pool.wait_ge(s_vm, NT)
            nc.gpsimd.tensor_scalar(rs[:], mv[:, :, 1], 1.0, EPS, ALU.mult, ALU.add).then_inc(s_vm, 1)
            pool.wait_ge(s_vm, NT + 1)
            nc.gpsimd.tensor_tensor(rs[:], rs[:], g.mhalf[:, 0:NT], ALU.pow).then_inc(s_vr, 1)


def product_T(g, pe, w, s_w, s_done, s_credit, act_T, kt, groups, ps):
    with pe.Fori(0, groups) as i:
        for s in range(2):
            pe.wait_ge(s_w[s], i * 16 + 16)
            for q in range(2):
                pe.wait_ge(s_credit, i * 4 + 2 * s + q + 1)
                for n in range(3):
                    for k in range(kt):
                        mm = g.nc.tensor.matmul(ps[:, 3 * q + n, 0:SLAB], w[:, s, k, q * P:(q + 1) * P],
                                                act_T[:, k, n * SLAB:(n + 1) * SLAB],
                                                start=(k == 0), stop=(k == kt - 1))
                mm.then_inc(s_done, 1)


CB_S = CONV - 1 + SEQ
CB_B = CONV - 1 + LS
CB_W = CB_S + NB * CB_B
CB_OUT = CB_W - (CONV - 1)


def stage_turned(g):
    nc, ps, hT = g.nc, g.psum, g.R2T
    w_in = g.d["w_in"][0].rearrange("(k p) n -> p k n", p=P)
    NG_X, NG_U = CF // 4, GMF // 4
    with ExitStack() as ctx:
        w = g.sb("t_w", [P, 2, DK, 2 * P], ctx=ctx)
        cb = g.sb("t_conv_in", [P, 2, CB_W], ctx=ctx)
        ca = g.sb("t_conv_out", [P, 2, CB_W], ctx=ctx)
        so = g.sb("t_silu", [P, 2, SEQ], ctx=ctx)
        zr = g.sb("t_zero", [P, D], ctx=ctx)
        s_zr, s_zf = g.sem("t_zero_ready"), g.sem("t_blocks_zeroed")
        s_w = [g.sem(f"t_w_loaded{i}") for i in range(2)]
        s_mm = g.sem("t_product")
        s_pf = g.sem("t_psum_free")
        s_z = g.sem("t_zeroed")
        s_in = g.sem("t_conv_in_ready")
        s_st = g.sem("t_state_in")
        s_c = g.sem("t_conv_chain")
        s_co = g.sem("t_conv_done")
        s_so = g.sem("t_silu_done")
        s_sto = [g.sem(f"t_stored{i}") for i in range(2)]
        s_ls = g.sem("t_lasts")
        s_lt = g.sem("t_lasts_turned")
        s_le = g.sem("t_lasts_rows")
        block = ctx.enter_context(nc.Block("turned"))

        def sample_view(ap, lo, n):
            return ap[:, CB_S:CB_S + NB * CB_B].rearrange("p (b j) -> p b j", j=CB_B)[:, :, lo:lo + n]

        first = 2 * T // P

        @block.sync
        def _(sp):
            sp.wait_ge(s_zr, 1)
            sp.dma_start(g.moe_scr[first * P:NSLOT, :].rearrange("(b p) n -> p b n", p=P),
                         mid(zr[:], NBLK - first)).then_inc(s_zf, 16)

            def cols(base):
                return lambda i, s: [(w[:, s], w_in[:, :, bass.ds(i * 4 * P + base + s * 2 * P, 2 * P)])]
            load_weights(sp, w, cols(COL_XBC), NG_X, s_w, s_mm, 4)
            for s in range(2):
                sp.wait_ge(s_mm, 4 * (NG_X - 1) + 2 * s + 2)
                sp.dma_start(w[:, s], w_in[:, :, COL_U + 2 * s * P:COL_U + 2 * (s + 1) * P]).then_inc(s_w[s], 16)
            sp.wait_ge(s_le, 3)
            sp.dma_start(g.out["conv_p"], g.lrow[0:CONV - 1, :]).then_inc(g.s_out, g.stored())
            sp.dma_start(g.out["conv_s"], g.lrow[CONV - 1:27, :]).then_inc(g.s_out, g.stored())
            sp.wait_ge(s_zf, 16)
            sp.wait_ge(g.s_out, 16 * g.n_out)

        @block.tensor
        def _(pe):
            product_T(g, pe, w, s_w, s_mm, s_pf, hT, DK, NG_X, ps)
            for s in range(2):
                pe.wait_ge(s_w[s], 16 * (NG_X + 1))
                for q in range(2):
                    pe.wait_ge(s_pf, 4 * NG_X + 2 * s + q + 1)
                    for n in range(3):
                        for k in range(DK):
                            mm = nc.tensor.matmul(ps[:, 3 * q + n, 0:SLAB], w[:, s, k, q * P:(q + 1) * P],
                                                  hT[:, k, n * SLAB:(n + 1) * SLAB],
                                                  start=(k == 0), stop=(k == DK - 1))
                    mm.then_inc(s_mm, 1)
            pe.wait_ge(s_ls, CF + 2)
            for r in range(3):
                if r:
                    pe.wait_ge(s_le, r)
                for k in range(8 if r < 2 else 4):
                    f = 8 * r + k
                    tr = nc.tensor.transpose(ps[0:27, 6 + k // 4, (k % 4) * P:(k % 4 + 1) * P],
                                             g.lasts[:, f, :], g.ident[:])
                tr.then_inc(s_lt, 1)

        @block.scalar
        def _(act):
            act.sem_inc(s_pf, 2)
            act.wait_ge(s_z, 1)
            with act.Fori(0, CF // 2) as i:
                for q in range(2):
                    act.wait_ge(s_mm, i * 2 + q + 1)
                    act.wait_ge(s_co, i * 2 + q + 1)
                    act.wait_ge(s_ls, i * 2 + q + 1)
                    for n in range(2):
                        nc.scalar.copy(cb[:, q, CONV - 1 + n * SLAB:CONV - 1 + (n + 1) * SLAB], ps[:, 3 * q + n, 0:SLAB])
                    nc.scalar.copy(cb[:, q, CONV - 1 + 2 * SLAB:CB_S], ps[:, 3 * q + 2, 0:SEQ - 2 * SLAB])
                    nc.scalar.copy(sample_view(cb[:, q, :], CONV - 1, LS),
                                   ps[:, 3 * q + 2, SEQ - 2 * SLAB:SLAB].rearrange("p (b j) -> p b j", j=LS)
                                   ).then_inc(s_pf, 1)
                for q in range(2):
                    act.wait_ge(s_co, i * 2 + q + 3)
                    act.wait_ge(s_sto[q], i * 16)
                    nc.scalar.activation(so[:, q, :], ca[:, q, 0:SEQ], ACT.Silu)
                    nc.scalar.activation(g.xbs[:, i * 2 + q, :].rearrange("p (b j) -> p b j", j=LS),
                                         sample_view(ca[:, q, :], 0, LS), ACT.Silu).then_inc(s_so, 1)
                    act.wait_ge(s_so, i * 2 + q + 1)
                    act.dma_start(g.x_scr[:, :, i * 2 + q, :].rearrange("c p t -> p c t"),
                                  so[:, q, :].rearrange("p (c t) -> p c t", t=P)).then_inc(s_sto[q], 16)
            for f in range(GMF):
                act.wait_ge(s_mm, CF + f + 1)
                for n in range(3):
                    a = nc.scalar.activation(g.uT[:, f, n * SLAB:(n + 1) * SLAB], ps[:, 3 * (f % 2) + n, 0:SLAB], ACT.Gelu)
                a.then_inc(s_pf, 1)
            for q in range(2):
                act.wait_ge(s_sto[q], 16 * (CF // 2))

        @block.vector
        def _(dve):
            nc.vector.memset(cb[:, :, 0:CONV - 1], 0.0).then_inc(s_z, 1)
            dve.sem_inc(s_co, 2)
            with dve.Fori(0, CF // 2) as i:
                for q in range(2):
                    f = i * 2 + q
                    o, c = ca[:, q, 0:CB_OUT], cb[:, q, :]
                    dve.wait_ge(s_pf, f + 3)
                    dve.wait_ge(s_st, f + 1)
                    dve.wait_ge(s_so, i * 2)
                    wk = [g.veca[:, bass.ds(f + j * CF, 1)] for j in range(CONV + 1)]
                    ch = Chain(dve, s_c, i * 6 + 3 * q)
                    ch.done(nc.vector.tensor_scalar(o, c[:, 0:CB_OUT], wk[0], wk[CONV], ALU.mult, ALU.add))
                    for j in range(1, CONV):
                        op = nc.vector.scalar_tensor_tensor(o, c[:, j:j + CB_OUT], wk[j], o, ALU.mult, ALU.add)
                        if j < CONV - 1:
                            ch.done(op)
                    op.then_inc(s_co, 1)
            for r in range(3):
                dve.wait_ge(s_lt, r + 1)
                n = 8 if r < 2 else 4
                nc.vector.tensor_copy(g.lrow[:, 8 * r * P:(8 * r + n) * P],
                                      ps[0:27, 6:6 + n // 4, :].rearrange("p b t -> p (b t)")).then_inc(s_le, 1)

        @block.gpsimd
        def _(pool):
            nc.gpsimd.memset(zr[:], 0.0).then_inc(s_zr, 1)
            pool.sem_inc(s_ls, 2)
            with pool.Fori(0, CF // 2) as i:
                for q in range(2):
                    f = i * 2 + q
                    pool.wait_ge(s_co, f + 1)
                    nc.gpsimd.tensor_copy(sample_view(cb[:, q, :], 0, CONV - 1),
                                          g.cst[:, f, :].rearrange("p (b j) -> p b j", j=CONV - 1)).then_inc(s_st, 1)
                    pool.wait_ge(s_pf, f + 3)
                    nc.gpsimd.tensor_copy(g.lasts[:, f, 0:CONV - 1], cb[:, q, SEQ:SEQ + CONV - 1])
                    nc.gpsimd.tensor_copy(g.lasts[:, f, CONV - 1:27].rearrange("p (b j) -> p b j", j=CONV - 1),
                                          sample_view(cb[:, q, :], LS, CONV - 1)).then_inc(s_ls, 1)


def stage_gmlp(g):
    nc, ps, d = g.nc, g.psum, g.d
    with ExitStack() as ctx:
        wr = g.sb("g_w_rows", [P, G, P], ctx=ctx)
        wT = g.sb("g_wT", [P, G, P], ctx=ctx)
        ws = g.sb("g_w_sample", [NS, G, NS], ctx=ctx)
        sg = g.sb("g_s", [P, 2, G, P], ctx=ctx)
        s_w = g.sem("g_w_loaded")
        s_ws = g.sem("g_ws_loaded")
        s_z = g.sem("g_zeroed")
        s_tr = g.sem("g_w_turned")
        s_wT = g.sem("g_w_ready")
        s_mm = g.sem("g_product")
        s_sb = g.sem("g_biased")
        s_u = g.sem("g_gated")
        block = ctx.enter_context(nc.Block("gmlp"))

        @block.sync
        def _(sp):
            sp.dma_start(wr[:], d["gm_ws"][0].rearrange("g t s -> t g s")).then_inc(s_w, 16)
            sp.wait_ge(s_z, 1)
            with nc.allow_non_contiguous_dma(reason="4 x 4 corners"):
                for b in range(NB):
                    for gg in range(G):
                        src = d["gm_ws"][0, gg, 0:LS, 0:LS].rearrange("t s -> s t")
                        sp.dma_start(ws[LS * b:LS * b + LS, gg, LS * b:LS * b + LS], src).then_inc(s_ws, 16)

        @block.gpsimd
        def _(pool):
            nc.gpsimd.memset(ws[:], 0.0).then_inc(s_z, 1)

        @block.tensor
        def _(pe):
            pe.wait_ge(s_w, 16)
            for gg in range(G):
                tr = nc.tensor.transpose(ps[:, 0, gg * P:(gg + 1) * P], wr[:, gg, :], g.ident[:])
            tr.then_inc(s_tr, 1)
            pe.wait_ge(s_wT, 2)
            for c in range(NT):
                b = 1 + c % 2
                if c >= 2:
                    pe.wait_ge(s_sb, c - 1)
                for gg in range(G):
                    if c < NC:
                        mm = nc.tensor.matmul(ps[:, b, gg * P:(gg + 1) * P], g.v[:, c, gg * P:(gg + 1) * P],
                                              wT[:, gg, :], start=True, stop=True)
                    else:
                        mm = nc.tensor.matmul(ps[:, b, gg * NS:(gg + 1) * NS], g.v[0:NS, c, gg * P:(gg + 1) * P],
                                              ws[:, gg, :], start=True, stop=True)
                mm.then_inc(s_mm, 1)

        @block.vector
        def _(dve):
            dve.wait_ge(s_tr, 1)
            nc.vector.tensor_tensor(wT[:], ps[:, 0, :].rearrange("p (g t) -> p g t", t=P), mid(g.tri[:], G),
                                    ALU.mult).then_inc(s_wT, 1)
            dve.wait_ge(s_ws, 16 * NB * G)
            nc.vector.tensor_tensor(ws[:], ws[:], mid(g.btri[:], G), ALU.mult).then_inc(s_wT, 1)
            for c in range(NT):
                b, n = 1 + c % 2, P if c < NC else NS
                dve.wait_ge(s_mm, c + 1)
                s = sg[:, c % 2, :, 0:n]
                src = ps[:, b, 0:G * n].rearrange("p (g t) -> p g t", t=n)
                if c < NC:
                    nc.vector.tensor_tensor(s, src, g.bs[:], ALU.add).then_inc(s_sb, 1)
                else:
                    for gg in range(G):
                        op = nc.vector.tensor_tensor(s[:, gg, :].rearrange("p (b j) -> p b j", j=LS),
                                                     src[:, gg, :].rearrange("p (b j) -> p b j", j=LS),
                                                     mid(g.bs[:, gg, 0:LS], NB), ALU.add)
                    op.then_inc(s_sb, 1)
                dve.wait_ge(s_sb, c + 1)
                u = g.uT[:, :, c * P:c * P + n]
                nc.vector.tensor_tensor(u, u, s, ALU.mult).then_inc(s_u, 1)


def stage_ssd(g):
    nc, ps = g.nc, g.psum
    XW = R * HD
    TX, YO, RB, YD, ST, YT = 0, 1, 3, 5, 6, 7
    gain = VEC["ssm_norm"]
    STEPS = NC * G
    with ExitStack() as ctx:
        xin = g.big1[:, 0:G * 5 * P].rearrange("p (g f t) -> p g f t", g=G, t=P)
        zin = g.big1[:, CD:CD + DI].rearrange("p (g w) -> p g w", g=G)
        ho = g.big1[:, CD + DI:CD + 2 * DI].rearrange("p (f n) -> p f n", n=N)
        dtc = g.sb("s_dta", [P, 2, H], ctx=ctx)
        xrb = g.sb("s_xrow", [P, 2, XW + P], ctx=ctx)
        xdt = g.sb("s_xdt", [P, 2, XW], ctx=ctx)
        xdd = g.sb("s_xdd", [P, 2, XW], ctx=ctx)
        xsk = g.sb("s_xskip", [P, 2, XW], ctx=ctx)
        cbm = g.sb("s_cb", [P, 2, P], ctx=ctx)
        att = g.sb("s_att", [P, 2, R, P], ctx=ctx)
        y = g.sb("s_y", [P, 2, XW], ctx=ctx)
        yz = g.sb("s_yz", [P, 2, XW], ctx=ctx)
        yn = g.sb("s_yn", [P, 2, XW], ctx=ctx)
        junk = g.sb("s_junk", [P, XW], ctx=ctx)
        h = g.sb("s_h", [P, G, XW], ctx=ctx)
        ss = g.sb("s_ss", [P, 2], ctx=ctx)
        rs = g.sb("s_rs", [P, 2], ctx=ctx)
        s_in = [g.sem(f"s_xbc_loaded{i}") for i in range(G)]
        s_zin = [g.sem(f"s_z_loaded{i}") for i in range(G)]
        s_tx, s_yo, s_rb, s_yd, s_st, s_yt = (g.sem("s_" + x) for x in (
            "x_turned", "cb_and_yoff", "running_sums", "ydiag", "new_state", "y_turned"))
        s_xr, s_e, s_ss, s_yn, s_ye = (g.sem("s_" + x) for x in (
            "x_rows", "exp", "squares", "y_normed", "yT_written"))
        s_xdt, s_cbm, s_att, s_y1, s_y2, s_h = (g.sem("s_" + x) for x in (
            "xdt", "cb_masked", "att", "y1", "y2", "h_updated"))
        s_xdd, s_hd, s_y3, s_yz, s_ms, s_rs, s_dtc = (g.sem("s_" + x) for x in (
            "xdd", "h_decayed", "y3", "yz", "mean", "rstd", "dta_chunk"))
        s_rl = g.sem("s_differences")
        s_ht, s_ho = g.sem("s_h_turned"), g.sem("s_h_rows_ready")
        block = ctx.enter_context(nc.Block("ssd"))

        def chunks(eng, body):
            body(0, True, False)
            with eng.Fori(1, NC - 1) as c:
                body(c, False, False)
            body(NC - 1, False, True)

        @block.sync
        def _(sp):
            def load(c, gg):
                x = g.x_scr[c].rearrange("p f t -> p f t")
                sp.dma_start(xin[:, gg, 0:3, :], x[:, 3 * gg:3 * gg + 3, :]).then_inc(s_in[gg], 16)
                sp.dma_start(xin[:, gg, 3:5, :], x[:, XF + gg:CF:G, :]).then_inc(s_in[gg], 16)

            def load_z(c, gg):
                sp.dma_start(zin[:, gg, :], g.z_scr[c][:, gg * XW:(gg + 1) * XW]).then_inc(s_zin[gg], 16)

            for gg in range(G):
                load(0, gg)
                load_z(0, gg)
            with sp.Fori(1, NC) as c:
                for gg in range(G):
                    sp.wait_ge(s_yo, (c - 1) * 4 + gg + 1)
                    load(c, gg)
                    sp.wait_ge(s_yz, (c - 1) * 4 + gg + 1)
                    load_z(c, gg)
            sp.wait_ge(s_ho, 1)
            sp.dma_start(g.out["ssm_p"], ho).then_inc(g.s_out, g.stored())
            sp.wait_ge(g.s_out, 16 * g.n_out)

        @block.tensor
        def _(pe):
            pe.wait_ge(s_dtc, 1)

            def front(c, gg):
                n, q = c * 4 + gg, gg % 2
                xb = xin[:, gg]
                pe.wait_ge(s_in[gg], c * 32 + 32)
                pe.wait_ge(s_xr, n)
                for j in range(4):
                    tr = nc.tensor.transpose(ps[:, TX, j * P:(j + 1) * P], xb[:, j, :], g.ident[:])
                tr.then_inc(s_tx, 1)
                pe.wait_ge(s_y1, n + 1)
                pe.wait_ge(s_h, n + 1)
                nc.tensor.matmul(ps[:, YO + q, XW:XW + P], xb[:, 3, :], xb[:, 4, :], start=True, stop=True)
                nc.tensor.matmul(ps[:, YO + q, 0:XW], xb[:, 4, :], h[:, gg, :], start=True, stop=True).then_inc(s_yo, 1)
                pe.wait_ge(s_e, n)
                pe.wait_ge(s_dtc, c * 2 + gg // 2 + 1)
                for r in range(R):
                    a = dtc[:, gg // 2, gg * R + r:gg * R + r + 1].to_broadcast([P, P])
                    mm = nc.tensor.matmul(ps[:, RB + r // 3, (r % 3) * P:(r % 3 + 1) * P], a, g.tri[:],
                                          start=True, stop=True)
                mm.then_inc(s_rb, 1)

            def turn(c, gg):
                n, q = c * 4 + gg, gg % 2
                pe.wait_ge(s_yn, n + 3)
                pe.wait_ge(s_ye, n)
                for j in range(3):
                    tr = nc.tensor.transpose(ps[:, YT, j * P:(j + 1) * P], yn[:, q, j * P:(j + 1) * P], g.ident[:])
                tr.then_inc(s_yt, 1)

            def back(c, gg):
                n, q = c * 4 + gg, gg % 2
                pe.wait_ge(s_att, n + 1)
                pe.wait_ge(s_y2, n)
                for r in range(R):
                    mm = nc.tensor.matmul(ps[:, YD, r * HD:(r + 1) * HD], att[:, q, r, :],
                                          xdt[:, q, r * HD:(r + 1) * HD], start=True, stop=True)
                mm.then_inc(s_yd, 1)
                pe.wait_ge(s_xdd, n + 1)
                pe.wait_ge(s_h, n + G)
                nc.tensor.matmul(ps[:, ST, 0:XW], xrb[:, q, XW:XW + P], xdd[:, q, :], start=True,
                                 stop=True).then_inc(s_st, 1)

            def body(c, first, last):
                for gg in range(G):
                    if gg < G - 1:
                        front(c, gg + 1)
                    elif not last:
                        front(c + 1, 0)
                    back(c, gg)
                    if gg:
                        turn(c, gg - 1)
                    elif not first:
                        turn(c - 1, G - 1)

            front(0, 0)
            chunks(pe, body)
            turn(NC - 1, G - 1)
            pe.wait_ge(s_h, STEPS + G)
            pe.wait_ge(s_ye, STEPS)
            for j in range(XF):
                tr = nc.tensor.transpose(ps[:, j // 4, (j % 4) * P:(j % 4 + 1) * P],
                                         h[:, j // 3, (j % 3) * P:(j % 3 + 1) * P], g.ident[:])
            tr.then_inc(s_ht, 1)

        @block.scalar
        def _(act):
            act.sem_inc(s_st, 2)
            act.sem_inc(s_yd, 2)
            act.sem_inc(s_yn, 2)

            def rows(c, gg):
                n, q = c * 4 + gg, gg % 2
                act.wait_ge(s_tx, n + 1)
                act.wait_ge(s_st, n + 1)
                nc.scalar.copy(xrb[:, q, :], ps[:, TX, :]).then_inc(s_xr, 1)
                act.wait_ge(s_rb, n + 1)
                act.wait_ge(s_yd, n + 1)
                for r in range(R):
                    e = nc.scalar.activation(att[:, q, r, :], ps[:, RB + r // 3, (r % 3) * P:(r % 3 + 1) * P],
                                             ACT.Relu, bias=g.acs[:, c, gg * R + r:gg * R + r + 1], scale=-1.0)
                e.then_inc(s_rl, 1)
                act.wait_ge(s_rl, n + 1)
                nc.scalar.activation(att[:, q], att[:, q], ACT.Exp, scale=-1.0).then_inc(s_e, 1)

            def norm(c, gg):
                n, q = c * 4 + gg, gg % 2
                act.wait_ge(s_yz, n + 1)
                act.wait_ge(s_rs, n)
                nc.scalar.activation(junk[:], yz[:, q, :], ACT.Square, scale=XW ** -0.5,
                                     accum_out=ss[:, q:q + 1]).then_inc(s_ss, 1)
                act.wait_ge(s_rs, n + 1)
                if not (isinstance(c, int) and c == 0 and gg < 2):
                    act.wait_ge(s_yt, n - 1)
                nc.scalar.activation(yn[:, q, :], yz[:, q, :], ACT.Copy, scale=rs[:, q:q + 1]).then_inc(s_yn, 1)

            def write(c, gg):
                n = c * 4 + gg
                act.wait_ge(s_yt, n + 1)
                for j in range(3):
                    f = 3 * gg + j
                    a = nc.scalar.activation(g.yT[:, f, bass.ds(c * P, P)], ps[:, YT, j * P:(j + 1) * P],
                                             ACT.Copy, scale=g.vecb[:, gain + f:gain + f + 1])
                a.then_inc(s_ye, 1)

            def body(c, first, last):
                for gg in range(G):
                    rows(c, gg)
                    if gg:
                        norm(c, gg - 1)
                    elif not first:
                        norm(c - 1, G - 1)
                    if gg >= 2:
                        write(c, gg - 2)
                    elif not first:
                        write(c - 1, gg + 2)

            chunks(act, body)
            norm(NC - 1, G - 1)
            write(NC - 1, G - 2)
            write(NC - 1, G - 1)
            act.wait_ge(s_ht, 1)
            nc.scalar.copy(ho.rearrange("p f n -> p (f n)"),
                           ps[:, 0:3, :].rearrange("p b t -> p (b t)")).then_inc(s_ho, 1)

        @block.vector
        def _(dve):
            nc.vector.memset(h[:], 0.0).then_inc(s_h, G)
            dve.sem_inc(s_y1, 2)

            def hd(ap):
                return ap.rearrange("p (r d) -> p r d", d=HD)

            def front(c, gg):
                n, q = c * 4 + gg, gg % 2
                dve.wait_ge(s_yo, n + 1)
                nc.vector.tensor_tensor(cbm[:, q, :], ps[:, YO + q, XW:XW + P], g.tri[:], ALU.mult).then_inc(s_cbm, 1)
                if not (isinstance(c, int) and c == 0 and gg < 2):
                    dve.wait_ge(s_yz, n - 1)
                nc.vector.tensor_tensor(hd(y[:, q, :]), hd(ps[:, YO + q, 0:XW]),
                                        last(g.eacs[:, c, gg * R:(gg + 1) * R], HD), ALU.mult).then_inc(s_y1, 1)
                dve.wait_ge(s_xr, n + 1)
                dve.wait_ge(s_yd, n + 1)
                nc.vector.tensor_tensor(hd(xdt[:, q, :]), hd(xrb[:, q, 0:XW]),
                                        last(g.dt[:, c, gg * R:(gg + 1) * R], HD), ALU.mult)
                dve.wait_ge(s_e, n + 1)
                dve.wait_ge(s_cbm, n + 1)
                nc.vector.tensor_tensor(att[:, q], att[:, q], mid(cbm[:, q, :], R), ALU.mult).then_inc(s_att, 1)

            def back(c, gg):
                n, q = c * 4 + gg, gg % 2
                dve.wait_ge(s_yd, n + 3)
                dve.wait_ge(s_y1, n + 3)
                nc.vector.tensor_tensor(y[:, q, :], y[:, q, :], ps[:, YD, 0:XW], ALU.add).then_inc(s_y2, 1)
                dve.wait_ge(s_st, n + 3)
                dve.wait_ge(s_hd, n + 1)
                nc.vector.tensor_tensor(h[:, gg, :], h[:, gg, :], ps[:, ST, 0:XW], ALU.add).then_inc(s_h, 1)

            def body(c, first, last):
                for gg in range(G):
                    front(c, gg)
                    if gg:
                        back(c, gg - 1)
                    elif not first:
                        back(c - 1, G - 1)

            chunks(dve, body)
            back(NC - 1, G - 1)

        @block.gpsimd
        def _(pool):
            def hd(ap):
                return ap.rearrange("p (r d) -> p r d", d=HD)

            def keep_dta(c, half):
                nc.gpsimd.tensor_copy(dtc[:, half, :], g.dta[:, c, :]).then_inc(s_dtc, 1)

            def front(c, gg):
                n, q = c * 4 + gg, gg % 2
                pool.wait_ge(s_xr, n + 1)
                nc.gpsimd.tensor_tensor(hd(xsk[:, q, :]), hd(xrb[:, q, 0:XW]),
                                        last(g.dskip[:, gg * R:(gg + 1) * R], HD), ALU.mult)
                pool.wait_ge(s_st, n + 1)
                nc.gpsimd.tensor_tensor(hd(xdd[:, q, :]), hd(xrb[:, q, 0:XW]),
                                        last(g.dte[:, c, gg * R:(gg + 1) * R], HD), ALU.mult).then_inc(s_xdd, 1)
                pool.wait_ge(s_yo, n + 1)
                pool.wait_ge(s_h, n + 1)
                nc.gpsimd.tensor_tensor(hd(h[:, gg, :]), hd(h[:, gg, :]),
                                        last(g.etot[:, c, gg * R:(gg + 1) * R], HD), ALU.mult).then_inc(s_hd, 1)

            def back(c, gg):
                n, q = c * 4 + gg, gg % 2
                pool.wait_ge(s_y2, n + 1)
                pool.wait_ge(s_xdd, n + 1)
                pool.wait_ge(s_yn, n + 1)
                nc.gpsimd.tensor_tensor(yz[:, q, :], y[:, q, :], xsk[:, q, :], ALU.add).then_inc(s_y3, 1)
                pool.wait_ge(s_y3, n + 1)
                pool.wait_ge(s_zin[gg], c * 16 + 16)
                nc.gpsimd.tensor_tensor(yz[:, q, :], yz[:, q, :], zin[:, gg, :], ALU.mult).then_inc(s_yz, 1)
                pool.wait_ge(s_ss, n + 1)
                nc.gpsimd.tensor_tensor(ss[:, q:q + 1], ss[:, q:q + 1], g.eps[:, 0:1], ALU.add).then_inc(s_ms, 1)
                pool.wait_ge(s_ms, n + 1)
                nc.gpsimd.tensor_tensor(rs[:, q:q + 1], ss[:, q:q + 1], g.mhalf[:, 0:1], ALU.pow).then_inc(s_rs, 1)

            def body(c, first, last):
                for gg in range(G):
                    if gg == 0 and not first:
                        pool.wait_ge(s_rb, c * 4)
                        keep_dta(c, 1)
                    front(c, gg)
                    if gg:
                        back(c, gg - 1)
                    elif not first:
                        back(c - 1, G - 1)
                    if gg == 2 and not last:
                        pool.wait_ge(s_rb, c * 4 + 2)
                        keep_dta(c + 1, 0)

            keep_dta(0, 0)
            keep_dta(0, 1)
            chunks(pool, body)
            back(NC - 1, G - 1)


def stage_ssd_sample(g):
    nc, ps, c = g.nc, g.psum, NC
    XW = R * HD
    gain = VEC["ssm_norm"]
    h_in = g.d["state_ssm"][0].rearrange("b h p n -> b (h p) n")
    with ExitStack() as ctx:
        xr = g.sb("q_rows", [NS, CD - G * N], ctx=ctx)
        xdt = g.sb("q_xdt", [NS, DI], ctx=ctx)
        xdd = g.sb("q_xdd", [NS, DI], ctx=ctx)
        xsk = g.sb("q_xskip", [NS, DI], ctx=ctx)
        zin = xr[:, 0:DI]
        bm = g.big1[0:NS, 0:NB * G * N].rearrange("p (b n) -> p b n", b=NB)
        H0 = NB * G * N
        h0 = g.big1[:, H0:H0 + 2 * DI].rearrange("p (s f n) -> p s f n", s=2, n=N)
        hT = g.big1[:, H0 + 2 * DI:H0 + 3 * DI]
        cm = g.sb("q_c_masked", [P, 2, G, NS], ctx=ctx)
        cbm = g.sb("q_cb", [NS, G, NS], ctx=ctx)
        att = g.sb("q_att", [NS, H, NS], ctx=ctx)
        et = g.sb("q_etot", [P, XF, NB], ctx=ctx)
        y = g.sb("q_y", [NS, DI], ctx=ctx)
        yd = g.sb("q_ydiag", [NS, DI], ctx=ctx)
        ss = g.sb("q_ss", [NS, G], ctx=ctx)
        s_z = g.sem("q_z_loaded")
        s_h0 = [g.sem(f"q_h0_loaded{i}") for i in range(2)]
        s_ho = [g.sem(f"q_h_stored{i}") for i in range(2)]
        s_p = g.sem("q_products")
        s_a = g.sem("q_act")
        s_v = g.sem("q_vector")
        s_g = g.sem("q_pool")
        s_ht = g.sem("q_h_turned")
        s_hc = g.sem("q_hT_ready")
        s_dx = g.sem("q_dta_spread")
        s_cm = g.sem("q_c_masked_ready")
        s_yo = g.sem("q_yoff")
        s_ys = g.sem("q_yoff_added")
        s_hd = g.sem("q_h_decayed_ready")
        s_st = g.sem("q_state_product")
        s_hn = g.sem("q_h_new")
        s_yd, s_yz, s_ms, s_yn, s_tail = (g.sem("q_" + x) for x in (
            "ydiag", "y_gated", "mean", "y_normed", "y_chain"))
        block = ctx.enter_context(nc.Block("ssd_sample"))

        @block.sync
        def _(sp):
            for s in range(2):
                sp.dma_start(h0[:, s], h_in[s].rearrange("(j p) n -> p j n", p=P)).then_inc(s_h0[s], 16)
            sp.wait_ge(s_v, 5)
            sp.wait_ge(s_g, 1)
            sp.dma_start(zin, g.z_scr[c][0:NS, :]).then_inc(s_z, 16)
            def store(n, s):
                sp.wait_ge(s_hn, n + 1)
                sp.dma_start(g.out["ssm_s"][n].rearrange("(j p) n -> p j n", p=P), h0[:, s]).then_inc(s_ho[s], 16)

            with sp.Fori(0, NB // 2 - 1) as i:
                for s in range(2):
                    store(i * 2 + s, s)
                for s in range(2):
                    sp.wait_ge(s_ho[s], i * 16 + 16)
                    sp.dma_start(h0[:, s], h_in[i * 2 + s + 2].rearrange("(j p) n -> p j n", p=P)).then_inc(s_h0[s], 16)
            for s in range(2):
                store(NB - 2 + s, s)
            for s in range(2):
                sp.wait_ge(s_ho[s], 16 * (NB // 2))

        @block.tensor
        def _(pe):
            for f in range(XF + G):
                nc.tensor.transpose(ps[0:NS, f // 4, (f % 4) * P:(f % 4 + 1) * P], g.xbs[:, f, :], g.ident[:])
            for gg in range(G):
                nc.tensor.matmul(ps[0:NS, 4, gg * NS:(gg + 1) * NS], g.xbs[:, XF + gg, :], g.xbs[:, XF + G + gg, :],
                                 start=True, stop=True)
            for h in range(H):
                at = h * NS
                nc.tensor.matmul(ps[0:NS, 5 + at // BANK, at % BANK:at % BANK + NS],
                                 g.dta[0:NS, c, h:h + 1].to_broadcast([NS, NS]), g.btri[:], start=True, stop=True)
            for j in range(XF):
                if j == 0:
                    pe.wait_ge(s_dx, 1)
                mm = nc.tensor.matmul(ps[:, 7, j * NB:(j + 1) * NB], y[:, j * P:(j + 1) * P], g.rowmask[:],
                                      start=True, stop=True)
            mm.then_inc(s_p, 1)
            pe.wait_ge(s_v, 5)
            pe.wait_ge(s_g, 1)
            for h in range(H):
                at = h * HD
                mm = nc.tensor.matmul(ps[0:NS, at // BANK, at % BANK:at % BANK + HD], att[:, h, :],
                                      xdt[:, at:at + HD], start=True, stop=True)
            mm.then_inc(s_p, 1)
            pe.wait_ge(s_yd, 1)
            with pe.Fori(0, NB // 2) as i:
                for s in range(2):
                    n = i * 2 + s
                    pe.wait_ge(s_h0[s], i * 16 + 16)
                    pe.wait_ge(s_hn, n)
                    for j in range(XF):
                        tr = nc.tensor.transpose(ps[:, j // 4, (j % 4) * P:(j % 4 + 1) * P], h0[:, s, j, :], g.ident[:])
                    tr.then_inc(s_ht, 1)
                    pe.wait_ge(s_hc, n + 1)
                    pe.wait_ge(s_cm, n + 1)
                    pe.wait_ge(s_ys, n)
                    for gg in range(G):
                        mm = nc.tensor.matmul(ps[0:NS, 3 + gg, 0:XW], cm[:, s, gg, :], hT[:, gg * XW:(gg + 1) * XW],
                                              start=True, stop=True)
                    mm.then_inc(s_yo, 1)
                    for j in range(XF):
                        mm = nc.tensor.matmul(ps[:, j // 4, (j % 4) * P:(j % 4 + 1) * P], xdd[:, j * P:(j + 1) * P],
                                              bm[:, n, (j // 3) * N:(j // 3 + 1) * N], start=True, stop=True)
                    mm.then_inc(s_st, 1)
            pe.wait_ge(s_yn, 1)
            pe.wait_ge(s_hn, NB)
            for f in range(XF):
                tr = nc.tensor.transpose(ps[:, 0, f * NS:(f + 1) * NS], y[:, f * P:(f + 1) * P], g.ident[0:NS, 0:NS])
            tr.then_inc(s_p, 1)

        @block.scalar
        def _(act):
            act.wait_ge(s_p, 1)
            nc.scalar.copy(xr[:], ps[0:NS, 0:4, :].rearrange("p b t -> p (b t)")).then_inc(s_a, 1)
            nc.scalar.activation(et[:].rearrange("p j b -> p (j b)"), ps[:, 7, 0:XF * NB], ACT.Exp).then_inc(s_a, 1)
            act.wait_ge(s_v, 1)
            nc.scalar.activation(att[:], att[:], ACT.Exp).then_inc(s_a, 1)
            act.wait_ge(s_p, 2)
            nc.scalar.copy(yd[:], ps[0:NS, 0:3, :].rearrange("p b t -> p (b t)")).then_inc(s_yd, 1)
            with act.Fori(0, NB // 2) as i:
                for s in range(2):
                    n = i * 2 + s
                    act.wait_ge(s_ht, n + 1)
                    act.wait_ge(s_yo, n)
                    nc.scalar.copy(hT, ps[:, 0:3, :].rearrange("p b t -> p (b t)")).then_inc(s_hc, 1)
            act.wait_ge(s_yz, 1)
            for gg in range(G):
                a = nc.scalar.activation(xdt[:, gg * XW:(gg + 1) * XW], y[:, gg * XW:(gg + 1) * XW], ACT.Square,
                                         accum_out=ss[:, gg:gg + 1])
            a.then_inc(s_a, 1)
            act.wait_ge(s_p, 3)
            for f in range(XF):
                nc.scalar.activation(g.yT[:, f, SEQ:T], ps[:, 0, f * NS:(f + 1) * NS], ACT.Copy,
                                     scale=g.vecb[:, gain + f:gain + f + 1])

        @block.gpsimd
        def _(pool):
            pool.wait_ge(s_a, 1)
            for b in range(NB):
                nc.gpsimd.tensor_scalar(bm[:, b, :], xr[:, DI:DI + G * N], g.rowmask[:, b:b + 1], None, ALU.mult)
            x3 = xr[:, 0:DI].rearrange("p (h d) -> p h d", d=HD)
            nc.gpsimd.tensor_tensor(xdd[:].rearrange("p (h d) -> p h d", d=HD), x3,
                                    last(g.dte[0:NS, c, :], HD), ALU.mult)
            nc.gpsimd.tensor_tensor(xsk[:].rearrange("p (h d) -> p h d", d=HD), x3,
                                    last(g.dskip[0:NS, :], HD), ALU.mult).then_inc(s_g, 1)
            pool.wait_ge(s_a, 2)
            with pool.Fori(0, NB // 2) as i:
                for s in range(2):
                    n = i * 2 + s
                    pool.wait_ge(s_yo, i * 2)
                    nc.gpsimd.tensor_tensor(cm[:, s], g.xbs[:, XF + G:CF, :], mid(g.colmask[:, n, :], G),
                                            ALU.mult).then_inc(s_cm, 1)
                    pool.wait_ge(s_h0[s], i * 16 + 16)
                    pool.wait_ge(s_ht, n + 1)
                    nc.gpsimd.tensor_tensor(h0[:, s], h0[:, s], last(et[:, :, n], N), ALU.mult).then_inc(s_hd, 1)
            pool.wait_ge(s_ms, 1)
            nc.gpsimd.tensor_tensor(ss[:], ss[:], g.mhalf[0:NS, 0:G], ALU.pow).then_inc(s_g, 1)

        @block.vector
        def _(dve):
            nc.vector.tensor_copy(y[:].rearrange("p (h d) -> p h d", d=HD),
                                  last(g.dta[0:NS, c, :], HD)).then_inc(s_dx, 1)
            dve.wait_ge(s_p, 1)
            for h0_, n_, b_ in ((0, 16, 5), (16, 8, 6)):
                op = nc.vector.tensor_tensor(att[:, h0_:h0_ + n_, :],
                                             ps[0:NS, b_, 0:n_ * NS].rearrange("p (h t) -> p h t", t=NS),
                                             last(g.acs[0:NS, c, h0_:h0_ + n_], NS), ALU.subtract)
            ch = Chain(dve, s_dx, 1)
            ch.done(op)
            ch = Chain(dve, s_v)
            ch.done(nc.vector.tensor_scalar(att[:], att[:], 0.0, None, ALU.min))
            ch.done(nc.vector.tensor_tensor(cbm[:], ps[0:NS, 4, 0:G * NS].rearrange("p (g t) -> p g t", t=NS),
                                            mid(g.btri[:], G), ALU.mult))
            dve.wait_ge(s_a, 3)
            for gg in range(G):
                a = att[:, gg * R:(gg + 1) * R, :]
                op = nc.vector.tensor_tensor(a, a, mid(cbm[:, gg, :], R), ALU.mult)
            ch.done(op)
            ch.done(nc.vector.tensor_tensor(xdt[:].rearrange("p (h d) -> p h d", d=HD),
                                            xr[:, 0:DI].rearrange("p (h d) -> p h d", d=HD),
                                            last(g.dt[0:NS, c, :], HD), ALU.mult))
            ch.done(nc.vector.memset(y[:], 0.0))
            with dve.Fori(0, NB // 2) as i:
                for s in range(2):
                    n = i * 2 + s
                    dve.wait_ge(s_yo, n + 1)
                    dve.wait_ge(s_ys, n)
                    yv = y[:].rearrange("p (g w) -> p g w", w=XW)
                    nc.vector.tensor_tensor(yv, yv, ps[0:NS, 3:7, 0:XW], ALU.add).then_inc(s_ys, 1)
                    dve.wait_ge(s_st, n + 1)
                    dve.wait_ge(s_hd, n + 1)
                    nc.vector.tensor_tensor(h0[:, s].rearrange("p j n -> p (j n)"), h0[:, s].rearrange("p j n -> p (j n)"),
                                            ps[:, 0:3, :].rearrange("p b t -> p (b t)"), ALU.add).then_inc(s_hn, 1)
            dve.wait_ge(s_ys, NB)
            dve.wait_ge(s_yd, 1)
            dve.wait_ge(s_g, 1)
            dve.wait_ge(s_z, 16)
            y3 = y[:].rearrange("p (h d) -> p h d", d=HD)
            tc = Chain(dve, s_tail)
            tc.done(nc.vector.tensor_tensor(y3, y3, last(g.eacs[0:NS, c, :], HD), ALU.mult))
            tc.done(nc.vector.tensor_tensor(y[:], y[:], yd[:], ALU.add))
            tc.done(nc.vector.tensor_tensor(y[:], y[:], xsk[:], ALU.add))
            nc.vector.tensor_tensor(y[:], y[:], zin, ALU.mult).then_inc(s_yz, 1)
            dve.wait_ge(s_a, 4)
            nc.vector.tensor_scalar(ss[:], ss[:], 1.0 / XW, EPS, ALU.mult, ALU.add).then_inc(s_ms, 1)
            dve.wait_ge(s_g, 2)
            nc.vector.tensor_tensor(y[:].rearrange("p (g w) -> p g w", w=XW), y[:].rearrange("p (g w) -> p g w", w=XW),
                                    last(ss[:], XW), ALU.mult).then_inc(s_yn, 1)



def stage_merge(g):
    nc, ps, d, hT, mT = g.nc, g.psum, g.d, g.R2T, g.R1T
    GA, GB, WA, WB = 0, DK, 2 * DK, 2 * DK + XF
    KT = WB + GMF
    wg = d["w_gate"][0].rearrange("(k p) n -> p k n", p=P)
    wa = d["w_a_proj"][0].rearrange("(k p) n -> p k n", p=P)
    wb = d["w_b_proj"][0].rearrange("(k p) n -> p k n", p=P)
    with ExitStack() as ctx:
        w = g.sb("m_w", [P, 2, KT, P], ctx=ctx)
        sg = g.sb("m_gate", [P, 2, T], ctx=ctx)
        tb = g.sb("m_b", [P, T], ctx=ctx)
        s_w = [g.sem(f"m_w_loaded{i}") for i in range(2)]
        s_mm = g.sem("m_product")
        s_ga = g.sem("m_gate_ready")
        s_pr = g.sem("m_projection_read")
        s_tb = g.sem("m_b_added")
        block = ctx.enter_context(nc.Block("merge"))

        @block.sync
        def _(sp):
            def src(i, s):
                f = i * 2 + s
                return [(w[:, s, GA:GA + DK], wg[:, :, bass.ds(f * P, P)]),
                        (w[:, s, GB:GB + DK], wg[:, :, bass.ds(f * P + D, P)]),
                        (w[:, s, WA:WA + XF], wa[:, :, bass.ds(f * P, P)]),
                        (w[:, s, WB:WB + GMF], wb[:, :, bass.ds(f * P, P)])]
            load_weights(sp, w, src, DK // 2, s_w, s_mm, 8)

        @block.tensor
        def _(pe):
            with pe.Fori(0, DK // 2) as i:
                for s in range(2):
                    pe.wait_ge(s_w[s], i * 64 + 64)
                    for q in range(2):
                        m = i * 4 + 2 * s + q
                        for k0, kt, act_T, b in ((GB if q else GA, DK, hT, 0),
                                                 (WB if q else WA, GMF if q else XF, g.uT if q else g.yT, 3)):
                            if b == 0:
                                pe.wait_ge(s_ga, m)
                            else:
                                pe.wait_ge(s_pr, m + 2)
                            for n in range(3):
                                for k in range(kt):
                                    mm = nc.tensor.matmul(ps[:, b + n, 0:SLAB], w[:, s, k0 + k, :],
                                                          act_T[:, k, n * SLAB:(n + 1) * SLAB],
                                                          start=(k == 0), stop=(k == kt - 1))
                            mm.then_inc(s_mm, 1)

        @block.scalar
        def _(act):
            with act.Fori(0, DK // 2) as i:
                for s in range(2):
                    for q in range(2):
                        m = i * 4 + 2 * s + q
                        act.wait_ge(s_mm, i * 8 + 4 * s + 2 * q + 1)
                        act.wait_ge(s_pr, m + 1)
                        bias = g.vecb[:, bass.ds(i * 2 + s + VEC["b_gate"] + q * DK, 1)]
                        a = nc.scalar.activation(sg[:, q, :].rearrange("p (n t) -> p n t", t=SLAB),
                                                 ps[:, 0:3, 0:SLAB], ACT.Sigmoid, bias=bias)
                        a.then_inc(s_ga, 1)

        @block.vector
        def _(dve):
            dve.sem_inc(s_pr, 2)
            with dve.Fori(0, DK // 2) as i:
                for s in range(2):
                    f = i * 2 + s
                    for q in range(2):
                        m = i * 4 + 2 * s + q
                        dve.wait_ge(s_ga, m + 1)
                        dve.wait_ge(s_mm, i * 8 + 4 * s + 2 * q + 2)
                        if q:
                            dve.wait_ge(s_tb, f)
                        dst = tb[:] if q else mT[:, f, 0:T]
                        nc.vector.tensor_tensor(dst.rearrange("p (n t) -> p n t", t=SLAB),
                                                sg[:, q, :].rearrange("p (n t) -> p n t", t=SLAB),
                                                ps[:, 3:6, 0:SLAB], ALU.mult).then_inc(s_pr, 1)

        @block.gpsimd
        def _(pool):
            nc.gpsimd.memset(mT[:, :, T:TP], 0.0)
            with pool.Fori(0, DK) as f:
                pool.wait_ge(s_pr, f * 2 + 4)
                nc.gpsimd.tensor_tensor(mT[:, f, 0:T], mT[:, f, 0:T], tb[:], ALU.add).then_inc(s_tb, 1)


def stage_add_rows(g, tag, act_T, w_dram, x, x_dram=None):
    nc, ps = g.nc, g.psum
    wv = w_dram.rearrange("(k p) n -> p k n", p=P)
    with ExitStack() as ctx:
        w = g.sb("a_w", [P, 2, DK, BANK], ctx=ctx)
        s_w = [g.sem(f"{tag}_w_loaded{i}") for i in range(2)]
        s_x = g.sem(tag + "_x_loaded")
        s_z = g.sem(tag + "_x_padded")
        s_mm = g.sem(tag + "_product")
        s_ad = g.sem(tag + "_added")
        block = ctx.enter_context(nc.Block(tag))

        @block.sync
        def _(sp):
            for j in range(2):
                sp.dma_start(w[:, j], wv[:, :, j * BANK:(j + 1) * BANK]).then_inc(s_w[j], 16)
            for i, (dst, src) in enumerate(x_dram or ()):
                if i:
                    sp.wait_ge(s_z, 1)
                sp.dma_start(dst, src).then_inc(s_x, 16)

        @block.gpsimd
        def _(pool):
            if x_dram:
                nc.gpsimd.memset(x[:, NT - 1, :], 0.0).then_inc(s_z, 1)

        @block.tensor
        def _(pe):
            for j in range(2):
                pe.wait_ge(s_w[j], 16)
                for c in range(NT):
                    n = j * NT + c
                    if n >= 4:
                        pe.wait_ge(s_ad, n - 3)
                    for k in range(DK):
                        mm = nc.tensor.matmul(ps[:, n % 4, :], act_T[:, k, c * P:(c + 1) * P], w[:, j, k, :],
                                              start=(k == 0), stop=(k == DK - 1))
                    mm.then_inc(s_mm, 1)

        @block.vector
        def _(dve):
            if x_dram:
                dve.wait_ge(s_x, 16 * len(x_dram))
            for j in range(2):
                for c in range(NT):
                    n = j * NT + c
                    dve.wait_ge(s_mm, n + 1)
                    o = x[:, c, j * BANK:(j + 1) * BANK]
                    nc.vector.tensor_tensor(o, o, ps[:, n % 4, :], ALU.add).then_inc(s_ad, 1)


def stage_mem_kv(g, mT, kT, vr):
    nc, ps, d = g.nc, g.psum, g.d
    wk = d["w_mem_k"][0].rearrange("(k p) n -> p k n", p=P)
    wv = d["w_mem_v"][0].rearrange("(k p) n -> p k n", p=P)
    with ExitStack() as ctx:
        w = g.sb("k_w", [P, 2, DK, BANK], ctx=ctx)
        kr = g.sb("k_rows", [P, MT, D], ctx=ctx)
        s_w = [g.sem(f"k_w_loaded{i}") for i in range(2)]
        s_mm, s_ev = g.sem("k_product"), g.sem("k_rows_ready")
        s_tr, s_te = g.sem("k_turned"), g.sem("k_turned_read")
        block = ctx.enter_context(nc.Block("mem_kv"))

        @block.sync
        def _(sp):
            for j in range(4):
                if j >= 2:
                    sp.wait_ge(s_mm, MT * (j - 1))
                src = (wk, wv)[j // 2][:, :, (j % 2) * BANK:(j % 2 + 1) * BANK]
                sp.dma_start(w[:, j % 2], src).then_inc(s_w[j % 2], 16)
            sp.wait_ge(s_ev, 8)
            sp.dma_start(g.out["mk"].rearrange("(t p) n -> p t n", p=P), kr[:]).then_inc(g.s_out, g.stored())
            sp.dma_start(g.out["mv"].rearrange("(t p) n -> p t n", p=P), vr[:]).then_inc(g.s_out, g.stored())
            sp.wait_ge(g.s_out, 16 * g.n_out)

        @block.tensor
        def _(pe):
            for j in range(4):
                pe.wait_ge(s_w[j % 2], 16 * (j // 2 + 1))
                for t in range(MT):
                    n = j * MT + t
                    if n >= 4:
                        pe.wait_ge(s_ev, n - 3)
                    for k in range(DK):
                        mm = nc.tensor.matmul(ps[:, n % 4, :], mT[:, k, t * P:(t + 1) * P], w[:, j % 2, k, :],
                                              start=(k == 0), stop=(k == DK - 1))
                    mm.then_inc(s_mm, 1)
            pe.wait_ge(s_ev, 4)
            for k in range(DK):
                for t in range(MT):
                    tr = nc.tensor.transpose(ps[:, 4 + k // 2, (k % 2) * ML + t * P:(k % 2) * ML + (t + 1) * P],
                                             kr[:, t, k * P:(k + 1) * P], g.ident[:])
            tr.then_inc(s_tr, 1)

        @block.scalar
        def _(act):
            for j in range(4):
                for t in range(MT):
                    n = j * MT + t
                    act.wait_ge(s_mm, n + 1)
                    dst = (kr, vr)[j // 2][:, t, (j % 2) * BANK:(j % 2 + 1) * BANK]
                    nc.scalar.copy(dst, ps[:, n % 4, :]).then_inc(s_ev, 1)

        @block.vector
        def _(dve):
            dve.wait_ge(s_tr, 1)
            nc.vector.tensor_copy(kT[:].rearrange("p k m -> p (k m)"),
                                  ps[:, 4:8, :].rearrange("p b t -> p (b t)")).then_inc(s_te, 1)


def stage_query(g, hT, qT):
    nc, ps = g.nc, g.psum
    wq = g.d["w_mem_q"][0].rearrange("(k p) n -> p k n", p=P)
    with ExitStack() as ctx:
        w = g.sb("u_w", [P, 2, DK, 2 * P], ctx=ctx)
        s_w = [g.sem(f"u_w_loaded{i}") for i in range(2)]
        s_mm, s_pf = g.sem("u_product"), g.sem("u_read")
        block = ctx.enter_context(nc.Block("query"))

        @block.sync
        def _(sp):
            load_weights(sp, w, lambda i, s: [(w[:, s], wq[:, :, bass.ds(i * 4 * P + s * 2 * P, 2 * P)])],
                         DK // 4, s_w, s_mm, 4)

        @block.tensor
        def _(pe):
            product_T(g, pe, w, s_w, s_mm, s_pf, hT, DK, DK // 4, ps)

        @block.scalar
        def _(act):
            act.sem_inc(s_pf, 2)
            with act.Fori(0, DK // 2) as i:
                for q in range(2):
                    act.wait_ge(s_mm, i * 2 + q + 1)
                    nc.scalar.copy(qT[:, i * 2 + q, 0:T].rearrange("p (n t) -> p n t", t=SLAB),
                                   ps[:, 3 * q:3 * q + 3, 0:SLAB]).then_inc(s_pf, 1)


def stage_attention(g, qT, kT, vr, oT):
    nc, ps = g.nc, g.psum
    S, PT, O = 0, 2, 4
    with ExitStack() as ctx:
        qs = g.sb("b_q", [P, MH, 2, P], ctx=ctx)
        pr = g.sb("b_p", [P, 2, ML], ctx=ctx)
        pT = g.sb("b_pT", [P, 2, ML], ctx=ctx)
        mx = g.sb("b_max", [P, 2], ctx=ctx)
        nb = g.sb("b_nbias", [P, 2], ctx=ctx)
        sm = g.sb("b_sum", [P, 2], ctx=ctx)
        ri = g.sb("b_rsum", [P, 2], ctx=ctx)
        s_q, s_s, s_mx, s_nb, s_e, s_ri, s_pn, s_pt, s_pc, s_o, s_oc = (g.sem("b_" + x) for x in (
            "q_kept", "scores", "max", "nbias", "exp", "rsum", "p_normed", "p_turned", "pT_ready",
            "values", "o_written"))
        block = ctx.enter_context(nc.Block("attention"))

        def chunks(eng, body):
            body(0, True, False)
            with eng.Fori(1, NC - 1) as c:
                body(c, False, False)
            body(NC - 1, False, True)

        @block.gpsimd
        def _(pool):
            with pool.Fori(0, NC) as c:
                for h in range(MH):
                    pool.wait_ge(s_s, c * 4 + h + 1)
                    nc.gpsimd.tensor_copy(qs[:, h], qT[:, 2 * h:2 * h + 2, bass.ds(c * P, P)]).then_inc(s_q, 1)

        @block.tensor
        def _(pe):
            pe.sem_inc(s_s, MH)

            def scores(c, h):
                n, q = c * 4 + h, h % 2
                pe.wait_ge(s_q, n + 1)
                pe.wait_ge(s_e, n + 1)
                for k in range(2):
                    mm = nc.tensor.matmul(ps[:, S + q, 0:ML], qs[:, h, k, :], kT[:, 2 * h + k, :],
                                          start=(k == 0), stop=(k == 1))
                mm.then_inc(s_s, 1)

            def turn(c, h):
                n, q = c * 4 + h, h % 2
                pe.wait_ge(s_pn, n + 1)
                pe.wait_ge(s_pc, n + 1)
                for t in range(MT):
                    tr = nc.tensor.transpose(ps[:, PT + q, t * P:(t + 1) * P], pr[:, q, t * P:(t + 1) * P], g.ident[:])
                tr.then_inc(s_pt, 1)

            def values(c, h):
                n, q = c * 4 + h, h % 2
                pe.wait_ge(s_pc, n + 3)
                pe.wait_ge(s_oc, n + 1)
                for k in range(2):
                    for t in range(MT):
                        mm = nc.tensor.matmul(ps[:, O + q, k * P:(k + 1) * P],
                                              vr[:, t, (2 * h + k) * P:(2 * h + k + 1) * P],
                                              pT[:, q, t * P:(t + 1) * P], start=(t == 0), stop=(t == MT - 1))
                mm.then_inc(s_o, 1)

            def body(c, first, last_):
                for h in range(MH):
                    if h < MH - 1:
                        scores(c, h + 1)
                    elif not last_:
                        scores(c + 1, 0)
                    turn(c, h)
                    if h:
                        values(c, h - 1)
                    elif not first:
                        values(c - 1, MH - 1)

            scores(0, 0)
            chunks(pe, body)
            values(NC - 1, MH - 1)

        @block.scalar
        def _(act):
            act.sem_inc(s_e, 2)
            act.sem_inc(s_oc, 2)

            def exp(c, h):
                n, q = c * 4 + h, h % 2
                act.wait_ge(s_nb, n + 1)
                act.wait_ge(s_pt, n + 1)
                nc.scalar.activation(pr[:, q, :], ps[:, S + q, 0:ML], ACT.Exp, bias=nb[:, q:q + 1], scale=SCALE,
                                     accum_out=sm[:, q:q + 1]).then_inc(s_e, 1)

            def write(c, h):
                n, q = c * 4 + h, h % 2
                act.wait_ge(s_o, n + 1)
                nc.scalar.copy(oT[:, 2 * h:2 * h + 2, bass.ds(c * P, P)],
                               ps[:, O + q, 0:2 * P].rearrange("p (k t) -> p k t", t=P)).then_inc(s_oc, 1)

            def body(c, first, last_):
                for h in range(MH):
                    exp(c, h)
                    if h >= 2:
                        write(c, h - 2)
                    elif not first:
                        write(c - 1, h + 2)

            chunks(act, body)
            write(NC - 1, MH - 2)
            write(NC - 1, MH - 1)

        @block.vector
        def _(dve):
            dve.sem_inc(s_pt, 2)
            dve.sem_inc(s_pc, 2)

            def front(c, h):
                n, q = c * 4 + h, h % 2
                dve.wait_ge(s_s, n + 1 + MH)
                nc.vector.reduce_max(mx[:, q:q + 1], ps[:, S + q, 0:ML], AX).then_inc(s_mx, 1)
                dve.wait_ge(s_mx, n + 1)
                nc.vector.tensor_scalar(nb[:, q:q + 1], mx[:, q:q + 1], -SCALE, None, ALU.mult).then_inc(s_nb, 1)

            def mid_(c, h):
                n, q = c * 4 + h, h % 2
                dve.wait_ge(s_e, n + 3)
                nc.vector.reciprocal(ri[:, q:q + 1], sm[:, q:q + 1]).then_inc(s_ri, 1)
                dve.wait_ge(s_ri, n + 1)
                nc.vector.tensor_scalar(pr[:, q, :], pr[:, q, :], ri[:, q:q + 1], None, ALU.mult).then_inc(s_pn, 1)

            def back(c, h):
                n, q = c * 4 + h, h % 2
                dve.wait_ge(s_pt, n + 3)
                if not (isinstance(c, int) and c == 0 and h < 2):
                    dve.wait_ge(s_o, n - 1)
                nc.vector.tensor_copy(pT[:, q, :], ps[:, PT + q, 0:ML]).then_inc(s_pc, 1)

            def body(c, first, last_):
                for h in range(MH):
                    if h < MH - 1:
                        front(c, h + 1)
                    elif not last_:
                        front(c + 1, 0)
                    mid_(c, h)
                    back(c, h)

            front(0, 0)
            chunks(dve, body)


def stage_attention_sample(g, qT, oT):
    nc, ps, d = g.nc, g.psum, g.d
    k_in = d["cache_mem_k"][0].rearrange("b m h e -> b m (h e)")
    v_in = d["cache_mem_v"][0].rearrange("b m h e -> b m (h e)")
    KT, S, PT, O = 0, 4, 5, 6
    with ExitStack() as ctx:
        kr = g.sb("d_k", [P, 2, MT, D], ctx=ctx)
        vr = g.sb("d_v", [P, 2, MT, D], ctx=ctx)
        kT = g.sb("d_kT", [P, DK, ML], ctx=ctx)
        pr = g.sb("d_p", [P, ML], ctx=ctx)
        pT = g.sb("d_pT", [P, MT, P], ctx=ctx)
        st = g.sb("d_stats", [P, 4], ctx=ctx)
        s_k = [g.sem(f"d_k_loaded{i}") for i in range(2)]
        s_v = [g.sem(f"d_v_loaded{i}") for i in range(2)]
        s_tr, s_ka, s_kv, s_s, s_mx, s_nb, s_e, s_ri, s_pn, s_pt, s_pc, s_o, s_oc = (g.sem("d_" + x) for x in (
            "k_turned", "kT_lower", "kT_upper", "scores", "max", "nbias", "exp", "rsum", "p_normed",
            "p_turned", "pT_ready", "values", "o_written"))
        block = ctx.enter_context(nc.Block("attention_sample"))

        @block.sync
        def _(sp):
            def load(ring, src, s, sem):
                sp.dma_start(ring[:, s], src.rearrange("(t p) n -> p t n", p=P)).then_inc(sem, 16)
            for s in range(2):
                load(kr, k_in[s], s, s_k[s])
                load(vr, v_in[s], s, s_v[s])
            with sp.Fori(1, NB // 2) as i:
                for s in range(2):
                    sp.wait_ge(s_tr, i * 2 + s - 1)
                    load(kr, k_in[i * 2 + s], s, s_k[s])
                    sp.wait_ge(s_o, i * 2 + s - 1)
                    load(vr, v_in[i * 2 + s], s, s_v[s])

        @block.tensor
        def _(pe):
            with pe.Fori(0, NB // 2) as i:
                for s in range(2):
                    n = i * 2 + s
                    pe.wait_ge(s_k[s], i * 16 + 16)
                    pe.wait_ge(s_ka, n)
                    pe.wait_ge(s_kv, n)
                    for k in range(DK):
                        for t in range(MT):
                            at = (k % 2) * ML + t * P
                            tr = nc.tensor.transpose(ps[:, KT + k // 2, at:at + P], kr[:, s, t, k * P:(k + 1) * P],
                                                     g.ident[:])
                    tr.then_inc(s_tr, 1)
                    pe.wait_ge(s_ka, n + 1)
                    pe.wait_ge(s_kv, n + 1)
                    pe.wait_ge(s_e, n)
                    for h in range(MH):
                        for k in range(2):
                            mm = nc.tensor.matmul(ps[h * NS:(h + 1) * NS, S, 0:ML], qT[:, 2 * h + k, SEQ:T],
                                                  kT[:, 2 * h + k, :], start=(k == 0), stop=(k == 1))
                    mm.then_inc(s_s, 1)
                    pe.wait_ge(s_pn, n + 1)
                    pe.wait_ge(s_pc, n)
                    for t in range(MT):
                        tr = nc.tensor.transpose(ps[:, PT, t * P:(t + 1) * P], pr[:, t * P:(t + 1) * P], g.ident[:])
                    tr.then_inc(s_pt, 1)
                    pe.wait_ge(s_pc, n + 1)
                    pe.wait_ge(s_v[s], i * 16 + 16)
                    pe.wait_ge(s_oc, n)
                    for k in range(DK):
                        for t in range(MT):
                            mm = nc.tensor.matmul(ps[:, O, k * NS:(k + 1) * NS], vr[:, s, t, k * P:(k + 1) * P],
                                                  pT[:, t, (k // 2) * NS:(k // 2 + 1) * NS],
                                                  start=(t == 0), stop=(t == MT - 1))
                    mm.then_inc(s_o, 1)

        @block.scalar
        def _(act):
            with act.Fori(0, NB) as n:
                act.wait_ge(s_tr, n + 1)
                act.wait_ge(s_s, n)
                nc.scalar.copy(kT[:, 0:DK // 2, :].rearrange("p k m -> p (k m)"),
                               ps[:, 0:2, :].rearrange("p b t -> p (b t)")).then_inc(s_ka, 1)
                act.wait_ge(s_nb, n + 1)
                act.wait_ge(s_pt, n)
                nc.scalar.activation(pr[:], ps[:, S, 0:ML], ACT.Exp, bias=st[:, 1:2], scale=SCALE,
                                     accum_out=st[:, 2:3]).then_inc(s_e, 1)

        @block.vector
        def _(dve):
            with dve.Fori(0, NB) as n:
                dve.wait_ge(s_tr, n + 1)
                dve.wait_ge(s_s, n)
                nc.vector.tensor_copy(kT[:, DK // 2:DK, :].rearrange("p k m -> p (k m)"),
                                      ps[:, 2:4, :].rearrange("p b t -> p (b t)")).then_inc(s_kv, 1)
                dve.wait_ge(s_s, n + 1)
                nc.vector.reduce_max(st[:, 0:1], ps[:, S, 0:ML], AX).then_inc(s_mx, 1)
                dve.wait_ge(s_mx, n + 1)
                nc.vector.tensor_scalar(st[:, 1:2], st[:, 0:1], -SCALE, None, ALU.mult).then_inc(s_nb, 1)
                dve.wait_ge(s_e, n + 1)
                nc.vector.reciprocal(st[:, 3:4], st[:, 2:3]).then_inc(s_ri, 1)
                dve.wait_ge(s_ri, n + 1)
                nc.vector.tensor_scalar(pr[:], pr[:], st[:, 3:4], None, ALU.mult).then_inc(s_pn, 1)
                dve.wait_ge(s_pt, n + 1)
                dve.wait_ge(s_o, n)
                nc.vector.tensor_copy(pT[:].rearrange("p t l -> p (t l)"), ps[:, PT, 0:ML]).then_inc(s_pc, 1)
                dve.wait_ge(s_o, n + 1)
                nc.vector.tensor_copy(oT[:, :, bass.ds(n * LS + SEQ, LS)],
                                      ps[:, O, 0:DK * NS].rearrange("p (k t) -> p k t", t=NS)[:, :, bass.ds(n * LS, LS)]
                                      ).then_inc(s_oc, 1)


def stage_router(g, hT, m):
    nc, ps, d = g.nc, g.psum, g.d
    NR = NG + NE
    with ExitStack() as ctx:
        wr = g.sb("o_w", [P, DK, NR], ctx=ctx)
        rb = g.sb("o_bias", [P, NR], ctx=ctx)
        lg = g.sb("o_logits", [P, NT, NR], ctx=ctx)
        t4 = g.sb("o_t4", [P, NT, 4], ctx=ctx)
        oh = g.sb("o_onehot", [P, 3, NT, 4], ctx=ctx)
        le = g.sb("o_chosen", [P, NT, 4], ctx=ctx)
        t16 = g.sb("o_t16", [P, NT, NE], ctx=ctx)
        mx = g.sb("o_max", [P, 3, NT], ctx=ctx)
        sc = g.sb("o_scalars", [P, 4, NT], ctx=ctx)
        M = g.sb("o_picks", [P, 3, NT, NE], ctx=ctx)
        run = g.sb("o_before", [P, NT + 1, NE], ctx=ctx)
        pos = g.sb("o_pos", [P, NT, NE], ctx=ctx)
        cnt = g.sb("o_counts", [P, NE], ctx=ctx)
        nbk = g.sb("o_blocks", [P, NE], ctx=ctx)
        ends = g.sb("o_ends", [P, NE], ctx=ctx)
        base = g.sb("o_base", [P, NE], ctx=ctx)
        thr = g.sb("o_thresholds", [P, NT], ctx=ctx)
        prio = g.sb("o_priority", [P, 4], ctx=ctx)
        low = g.sb("o_lower", [P, NE, NE], ctx=ctx)
        c9 = g.sb("o_c9", [P, NE, NT], ctx=ctx)
        bid = g.sb("o_block_ids", [P, NBLK], ctx=ctx)
        cb = g.sb("o_cb", [P, NBLK, NE], ctx=ctx)
        be = g.sb("o_block_expert", [P, NBLK], ctx=ctx)
        half = g.sb("o_even", [P, NBLK // 2], ctx=ctx)
        valid = g.sb("o_valid", [P, NT], ctx=ctx)
        dst = g.sb("o_dest", [P, 2, NT], ctx=ctx)
        tok = g.sb("o_tokens", [P, NT], U32, ctx=ctx)
        zt = g.sb("o_zero", [P, NSLOT // P + 1], U32, ctx=ctx)
        s_w, s_c, s_c2, s_lg, s_v, s_x, s_p, s_tz, s_sc, s_done = (g.sem("o_" + x) for x in (
            "w_loaded", "constants", "constants2", "logits", "vector", "exp", "prefix", "table_zeroed",
            "scattered", "tables"))
        block = ctx.enter_context(nc.Block("router"))

        @block.sync
        def _(sp):
            with nc.allow_non_contiguous_dma(reason="20 columns of the routers"):
                sp.dma_start(wr[:, :, 0:NG], d["w_router_group"][0].rearrange("(k p) n -> p k n", p=P)).then_inc(s_w, 16)
                sp.dma_start(wr[:, :, NG:NR], d["w_router_expert"][0].rearrange("(k p) n -> p k n", p=P)).then_inc(s_w, 16)
            sp.dma_start(rb[:, 0:NG], g.flat["b_router_group"].partition_broadcast(P)).then_inc(s_w, 16)
            sp.dma_start(rb[:, NG:NR], g.flat["b_router_expert"].partition_broadcast(P)).then_inc(s_w, 16)
            sp.wait_ge(s_c, 1)
            sp.dma_start(g.tok_scr.rearrange("(p b) o -> p (b o)", p=P), zt[:]).then_inc(s_tz, 16)

        @block.gpsimd
        def _(pool):
            nc.gpsimd.memset(zt[:], 0).then_inc(s_c, 1)
            nc.gpsimd.iota(tok[:], [[P, NT]], 0, 1)
            it = dict(allow_small_or_imprecise_dtypes=True)
            nc.gpsimd.iota(thr[:], [[P, NT]], 0, 0, **it)
            nc.gpsimd.iota(prio[:], [[-1, 4]], 4, 0, **it)
            nc.gpsimd.iota(bid[:], [[1, NBLK]], 0, 0, **it)
            nc.gpsimd.iota(half[:], [[2, NBLK // 2]], 0, 0, **it)
            nc.gpsimd.memset(low[:], 1.0)
            nc.gpsimd.memset(valid[:, 0:NC], 1.0)
            nc.gpsimd.memset(valid[:, NC:NT], 0.0)
            nc.gpsimd.memset(run[:, 0, :], 0.0).then_inc(s_c, 1)
            pool.wait_ge(s_c, 2)
            nc.gpsimd.memset(valid[0:NS, NC:NT], 1.0)
            nc.gpsimd.affine_select(low[:], low[:], [[1, NE], [-1, NE]], ALU.is_ge, 0.0, 0, 0).then_inc(s_c2, 1)
            pool.wait_ge(s_done, 1)
            pool.wait_ge(s_tz, 16)
            for c in range(NT):
                n = P if c < NC else NS
                for k in range(2):
                    nc.gpsimd.indirect_dma_start(
                        out=g.tok_scr, out_offset=bass.IndirectOffsetOnAxis(ap=m.slot[0:n, k, c:c + 1], axis=0),
                        in_=tok[0:n, c:c + 1], in_offset=None).then_inc(s_sc, 16)
            pool.wait_ge(s_sc, 16 * 2 * NT)

        @block.tensor
        def _(pe):
            pe.wait_ge(s_w, 64)
            for c in range(NT):
                for k in range(DK):
                    mm = nc.tensor.matmul(ps[:, 0, c * NR:(c + 1) * NR], hT[:, k, c * P:(c + 1) * P], wr[:, k, :],
                                          start=(k == 0), stop=(k == DK - 1))
            mm.then_inc(s_lg, 1)
            pe.wait_ge(s_p, 1)
            nc.tensor.matmul(ps[:, 1, 0:NT * NE], g.stri[:], M[:, 2].rearrange("p c e -> p (c e)"), start=True, stop=False)
            nc.tensor.matmul(ps[:, 1, 0:NT * NE], g.ones[:], run[:, 0:NT].rearrange("p c e -> p (c e)"),
                             start=False, stop=True)
            nc.tensor.matmul(ps[:, 2, 0:NE], g.ones[:], run[:, NT, :], start=True, stop=True).then_inc(s_lg, 1)

        @block.scalar
        def _(act):
            act.wait_ge(s_x, 1)
            nc.scalar.activation(t4[:], t4[:], ACT.Exp).then_inc(s_x, 1)
            act.wait_ge(s_x, 3)
            nc.scalar.activation(sc[:, 0, :], sc[:, 0, :], ACT.Exp).then_inc(s_x, 1)

        @block.vector
        def _(dve):
            ch = Chain(dve, s_v)
            tt, ts = nc.vector.tensor_tensor, nc.vector.tensor_scalar

            def tile4(ap):
                return ap.unsqueeze(2).to_broadcast([P, NT, 4])

            def first_of(o, vals, top):
                ch.done(tt(o, vals, tile4(top), ALU.is_equal))
                ch.done(tt(o, o, mid(prio[:], NT), ALU.mult))
                ch.done(nc.vector.tensor_reduce(sc[:, 3, :], o, AX, ALU.max))
                ch.done(tt(o, o, tile4(sc[:, 3, :]), ALU.is_equal))

            dve.wait_ge(s_lg, 1)
            dve.wait_ge(s_c, 2)
            dve.wait_ge(s_c2, 1)
            ch.done(tt(lg[:], ps[:, 0, 0:NT * NR].rearrange("p (c r) -> p c r", r=NR), mid(rb[:], NT), ALU.add))
            gl = lg[:, :, 0:NG]
            ch.done(nc.vector.tensor_reduce(mx[:, 0, :], gl, AX, ALU.max))
            ch.n += 1
            tt(t4[:], gl, tile4(mx[:, 0, :]), ALU.subtract).then_inc(s_v, 1)
            dve.wait_ge(s_v, ch.n)
            nc.vector.tensor_copy(sc[:, 1, :], mx[:, 0, :]).then_inc(s_x, 1)
            first_of(oh[:, 0], gl, mx[:, 0, :])
            ch.done(tt(t16[:].rearrange("p c (g e) -> p c g e", e=EPG), lg[:, :, NG:NR].rearrange("p c (g e) -> p c g e", e=EPG),
                       oh[:, 0].unsqueeze(3).to_broadcast([P, NT, NG, EPG]), ALU.mult))
            ch.done(nc.vector.tensor_reduce(le[:], t16[:].rearrange("p c (g e) -> p c e g", e=EPG), AX, ALU.add))
            ch.done(nc.vector.tensor_reduce(mx[:, 1, :], le[:], AX, ALU.max))
            first_of(oh[:, 1], le[:], mx[:, 1, :])
            dve.wait_ge(s_x, 2)
            ch.done(nc.vector.tensor_reduce(sc[:, 1, :], t4[:], AX, ALU.add))
            ch.done(ts(t4[:], oh[:, 1], -1.0, 1.0, ALU.mult, ALU.add))
            ch.done(tt(le[:], le[:], t4[:], ALU.mult))
            ch.done(nc.vector.scalar_tensor_tensor(le[:], oh[:, 1], -BIG, le[:], ALU.mult, ALU.add))
            ch.done(nc.vector.tensor_reduce(mx[:, 2, :], le[:], AX, ALU.max))
            first_of(oh[:, 2], le[:], mx[:, 2, :])
            tt(sc[:, 0, :], mx[:, 2, :], mx[:, 1, :], ALU.subtract).then_inc(s_x, 1)
            dve.wait_ge(s_x, 4)
            ch.done(ts(sc[:, 2, :], sc[:, 0, :], 1.0, None, ALU.add))
            ch.done(tt(sc[:, 2, :], sc[:, 2, :], sc[:, 1, :], ALU.mult))
            ch.done(nc.vector.reciprocal(m.wt[:, 0, :], sc[:, 2, :]))
            ch.done(tt(m.wt[:, 1, :], m.wt[:, 0, :], sc[:, 0, :], ALU.mult))
            ch.done(tt(oh[:, 0], oh[:, 0], valid[:].unsqueeze(2).to_broadcast([P, NT, 4]), ALU.mult))
            for k in range(2):
                ch.done(tt(M[:, k].rearrange("p c (g e) -> p c g e", e=EPG),
                           oh[:, 0].unsqueeze(3).to_broadcast([P, NT, NG, EPG]),
                           oh[:, 1 + k].unsqueeze(2).to_broadcast([P, NT, NG, EPG]), ALU.mult))
            ch.done(tt(M[:, 2], M[:, 0], M[:, 1], ALU.add))
            for c in range(NT):
                ch.done(tt(run[:, c + 1, :], run[:, c, :], M[:, 2, c, :], ALU.add))
            nc.vector.tensor_copy(pos[:, 0, 0:1], run[:, NT, 0:1]).then_inc(s_p, 1)
            dve.wait_ge(s_lg, 2)
            ch.done(nc.vector.tensor_copy(cnt[:], ps[:, 2, 0:NE]))
            ch.done(tt(c9[:], last(cnt[:], NT), mid(thr[:], NE), ALU.is_gt))
            ch.done(nc.vector.tensor_reduce(nbk[:], c9[:], AX, ALU.add))
            ch.done(tt(low[:], low[:], mid(nbk[:], NE), ALU.mult))
            ch.done(nc.vector.tensor_reduce(ends[:], low[:], AX, ALU.add))
            ch.done(tt(base[:], ends[:], nbk[:], ALU.subtract))
            ch.done(ts(base[:], base[:], float(P), None, ALU.mult))
            ch.done(tt(pos[:], ps[:, 1, 0:NT * NE].rearrange("p (c e) -> p c e", e=NE), mid(base[:], NT), ALU.add))
            for k in range(2):
                ch.done(tt(t16[:], pos[:], M[:, k], ALU.mult))
                ch.done(nc.vector.tensor_reduce(dst[:, k, :], t16[:], AX, ALU.add))
            ch.done(nc.vector.tensor_copy(m.slot[:], dst[:]))
            ch.done(tt(cb[:], mid(ends[:], NBLK), last(bid[:], NE), ALU.is_le))
            ch.done(nc.vector.tensor_reduce(be[:], cb[:], AX, ALU.add))
            ch.done(ts(be[:], be[:], float(NE - 1), None, ALU.min))
            ch.done(nc.vector.tensor_copy(m.bexp[:], be[:]))
            ch.done(ts(half[:], half[:], ends[:, NE - 1:NE], None, ALU.is_lt))
            ch.done(nc.vector.tensor_reduce(be[:, 0:1], half[:], AX, ALU.add))
            nc.vector.tensor_copy(m.pairs[:], be[:, 0:1]).then_inc(s_done, 1)


def stage_experts(g, m):
    nc, ps, d = g.nc, g.psum, g.d
    X, GA, UP, HT, DN = 0, 2, 3, 4, 5
    weg = d["w_expert_gate"][0].rearrange("e (k p) n -> e p k n", p=P)
    weu = d["w_expert_up"][0].rearrange("e (k p) n -> e p k n", p=P)
    wed = d["w_expert_down"][0].rearrange("e (k p) n -> e p k n", p=P)
    out_v = g.moe_scr.rearrange("(b p) n -> b p n", p=P)
    with ExitStack() as ctx:
        wg = g.sb("e_wg", [P, 2, DK, FF], ctx=ctx)
        wu = g.sb("e_wu", [P, 2, DK, FF], ctx=ctx)
        wd = g.sb("e_wd", [P, 2, FK, D], ctx=ctx)
        tab = g.sb("e_table", [P, NBLK + 1], U32, ctx=ctx)
        idx = g.sb("e_idx", [P, 2, 1], U32, ctx=ctx)
        xb = g.sb("e_x", [P, 2, D], ctx=ctx)
        xT = g.sb("e_xT", [P, 2, DK, P], ctx=ctx)
        sg = g.sb("e_silu", [P, FF], ctx=ctx)
        hh = g.sb("e_h", [P, FF], ctx=ctx)
        hT = g.sb("e_hT", [P, FK, P], ctx=ctx)
        ob = g.sb("e_out", [P, 2, D], ctx=ctx)
        s_t = g.sem("e_table_loaded")
        s_wgu = [g.sem(f"e_gate_up_loaded{i}") for i in range(2)]
        s_wd = [g.sem(f"e_down_loaded{i}") for i in range(2)]
        s_ix = g.sem("e_idx_ready")
        s_go = g.sem("e_waited")
        s_x = [g.sem(f"e_x_gathered{i}") for i in range(2)]
        s_xt, s_xc, s_g, s_u, s_sg, s_h, s_ht, s_hc, s_dn, s_oa, s_ov = (g.sem("e_" + x) for x in (
            "x_turned", "xT_ready", "gate", "up", "silu", "h", "h_turned", "hT_ready", "down",
            "out_lower", "out_upper"))
        s_o = [g.sem(f"e_stored{i}") for i in range(2)]
        block = ctx.enter_context(nc.Block("experts"))

        def pairs(eng):
            return eng.value_load(m.pairs[0:1, 0:1], min_val=1, max_val=NBLK // 2)

        @block.sync
        def _(sp):
            with nc.allow_non_contiguous_dma(reason="one slot's token per element"):
                sp.dma_start(tab[:], g.tok_scr.rearrange("(b p) o -> p (b o)", p=P)).then_inc(s_t, 16)
            np_ = pairs(sp)
            with sp.Fori(0, np_) as i:
                for s in range(2):
                    e = sp.value_load(m.bexp[0:1, bass.ds(i * 2 + s, 1)], min_val=0, max_val=NE - 1)
                    sp.wait_ge(s_u, i * 2 + s + 1)
                    sp.dma_start(wg[:, s], weg[e]).then_inc(s_wgu[s], 16)
                    sp.dma_start(wu[:, s], weu[e]).then_inc(s_wgu[s], 16)
                    sp.wait_ge(s_dn, i * 2 + s + 1)
                    sp.dma_start(wd[:, s], wed[e]).then_inc(s_wd[s], 16)

        @block.gpsimd
        def _(pool):
            pool.wait_ge(s_t, 16)

            def gather(b, s, k):
                pool.wait_ge(s_xt, b + 1)
                nc.gpsimd.tensor_copy(idx[:, s, :], tab[:, bass.ds(b, 1)]).then_inc(s_ix, 1)
                pool.wait_ge(s_ix, b + 1)
                pool.sem_inc(s_go, 1)
                nc.gpsimd.indirect_dma_start(
                    out=xb[:, s, :], out_offset=None, in_=g.h_scr,
                    in_offset=bass.IndirectOffsetOnAxis(ap=idx[:, s, 0:1], axis=0)).then_inc(s_x[s], 16)

            np_ = pairs(pool)
            gather(0, 0, 0)
            with pool.Fori(0, np_) as i:
                gather(i * 2 + 1, 1, i)
                gather(i * 2 + 2, 0, i)

        @block.tensor
        def _(pe):
            pe.sem_inc(s_u, 2)
            pe.sem_inc(s_dn, 2)
            pe.sem_inc(s_xt, 2)

            def turn(b, s, landed):
                pe.wait_ge(s_x[s], landed)
                pe.wait_ge(s_xc, b)
                for k in range(DK):
                    tr = nc.tensor.transpose(ps[:, X + k // 4, (k % 4) * P:(k % 4 + 1) * P],
                                             xb[:, s, k * P:(k + 1) * P], g.ident[:])
                tr.then_inc(s_xt, 1)

            np_ = pairs(pe)
            turn(0, 0, 16)
            with pe.Fori(0, np_) as i:
                for s in range(2):
                    b = i * 2 + s
                    pe.wait_ge(s_xc, b + 1)
                    pe.wait_ge(s_wgu[s], i * 32 + 32)
                    pe.wait_ge(s_sg, b)
                    for k in range(DK):
                        mm = nc.tensor.matmul(ps[:, GA, :], xT[:, s, k, :], wg[:, s, k, :],
                                              start=(k == 0), stop=(k == DK - 1))
                    mm.then_inc(s_g, 1)
                    pe.wait_ge(s_h, b)
                    for k in range(DK):
                        mm = nc.tensor.matmul(ps[:, UP, :], xT[:, s, k, :], wu[:, s, k, :],
                                              start=(k == 0), stop=(k == DK - 1))
                    mm.then_inc(s_u, 1)
                    turn(b + 1, 1 - s, i * 16 + 16 + 16 * s)
                    pe.wait_ge(s_h, b + 1)
                    pe.wait_ge(s_hc, b)
                    for k in range(FK):
                        tr = nc.tensor.transpose(ps[:, HT, k * P:(k + 1) * P], hh[:, k * P:(k + 1) * P], g.ident[:])
                    tr.then_inc(s_ht, 1)
                    pe.wait_ge(s_hc, b + 1)
                    pe.wait_ge(s_wd[s], i * 16 + 16)
                    pe.wait_ge(s_oa, b)
                    pe.wait_ge(s_ov, b)
                    for j in range(2):
                        for k in range(FK):
                            mm = nc.tensor.matmul(ps[:, DN + j, :], hT[:, k, :], wd[:, s, k, j * BANK:(j + 1) * BANK],
                                                  start=(k == 0), stop=(k == FK - 1))
                    mm.then_inc(s_dn, 1)

        @block.scalar
        def _(act):
            def keep(b, s):
                act.wait_ge(s_xt, b + 3)
                act.wait_ge(s_u, b + 1)
                nc.scalar.copy(xT[:, s].rearrange("p k t -> p (k t)"),
                               ps[:, X:X + 2, :].rearrange("p b t -> p (b t)")).then_inc(s_xc, 1)

            np_ = pairs(act)
            keep(0, 0)
            with act.Fori(0, np_) as i:
                for s in range(2):
                    b = i * 2 + s
                    act.wait_ge(s_g, b + 1)
                    act.wait_ge(s_h, b)
                    nc.scalar.activation(sg[:], ps[:, GA, :], ACT.Silu).then_inc(s_sg, 1)
                    keep(b + 1, 1 - s)
                    act.wait_ge(s_dn, b + 3)
                    act.wait_ge(s_o[s], i * 16)
                    nc.scalar.copy(ob[:, s, 0:BANK], ps[:, DN, :]).then_inc(s_oa, 1)
                    act.wait_ge(s_oa, b + 1)
                    act.wait_ge(s_ov, b + 1)
                    act.dma_start(out_v[b], ob[:, s, :]).then_inc(s_o[s], 16)
            for s in range(2):
                act.wait_ge(s_o[s], np_ * 16)
                act.sem_inc(s_go, 1)

        @block.vector
        def _(dve):
            np_ = pairs(dve)
            with dve.Fori(0, np_) as i:
                for s in range(2):
                    b = i * 2 + s
                    dve.wait_ge(s_sg, b + 1)
                    dve.wait_ge(s_u, b + 3)
                    dve.wait_ge(s_ht, b)
                    nc.vector.tensor_tensor(hh[:], sg[:], ps[:, UP, :], ALU.mult).then_inc(s_h, 1)
                    dve.wait_ge(s_ht, b + 1)
                    dve.wait_ge(s_dn, b + 2)
                    nc.vector.tensor_copy(hT[:].rearrange("p k t -> p (k t)"), ps[:, HT, :]).then_inc(s_hc, 1)
                    dve.wait_ge(s_dn, b + 3)
                    dve.wait_ge(s_o[s], i * 16)
                    nc.vector.tensor_copy(ob[:, s, BANK:D], ps[:, DN + 1, :]).then_inc(s_ov, 1)


def stage_final(g, x, m):
    nc = g.nc
    RING = 3
    with ExitStack() as ctx:
        a = g.sb("f_first", [P, RING, D], ctx=ctx)
        b = g.sb("f_second", [P, RING, D], ctx=ctx)
        y = g.sb("f_y", [P, RING, D], ctx=ctx)
        junk = g.sb("f_junk", [P, D], ctx=ctx)
        gf = g.sb("f_gain", [P, D], ctx=ctx)
        ss = g.sb("f_ss", [P, NT], ctx=ctx)
        s_g = g.sem("f_gain_loaded")
        s_l = [g.sem(f"f_gathered{i}") for i in range(RING)]
        s_a, s_x, s_ss, s_ms, s_rs, s_y = (g.sem("f_" + x_) for x_ in (
            "first_added", "x_ready", "squares", "mean", "rstd", "y_ready"))
        s_o = [g.sem(f"f_stored{i}") for i in range(RING)]
        block = ctx.enter_context(nc.Block("final"))

        def rows(c):
            return P if c < NC else NS

        @block.sync
        def _(sp):
            sp.dma_start(gf[:], g.flat["norm_final"].partition_broadcast(P)).then_inc(s_g, 16)
            for c in range(NT):
                sp.wait_ge(s_y, c + 1)
                dst = g.out["y_p"][c * P:(c + 1) * P, :] if c < NC else g.out["y_s"]
                sp.dma_start(dst, y[0:rows(c), c % RING, :]).then_inc(s_o[c % RING], 16)
            for q in range(RING):
                sp.wait_ge(s_o[q], 16 * (NT // RING))

        @block.gpsimd
        def _(pool):
            def gather(c):
                n, q = rows(c), c % RING
                for k, dst in enumerate((a, b)):
                    nc.gpsimd.indirect_dma_start(
                        out=dst[0:n, q, :], out_offset=None, in_=g.moe_scr,
                        in_offset=bass.IndirectOffsetOnAxis(ap=m.slot[0:n, k, c:c + 1], axis=0)).then_inc(s_l[q], 16)

            for c in range(RING):
                gather(c)
            for c in range(NT):
                n = rows(c)
                pool.wait_ge(s_ss, c + 1)
                nc.gpsimd.tensor_scalar(ss[0:n, c:c + 1], ss[0:n, c:c + 1], 1.0 / D, EPS, ALU.mult, ALU.add).then_inc(s_ms, 1)
                pool.wait_ge(s_ms, c + 1)
                nc.gpsimd.tensor_tensor(ss[0:n, c:c + 1], ss[0:n, c:c + 1], g.mhalf[0:n, 0:1], ALU.pow).then_inc(s_rs, 1)
                if c + RING < NT:
                    gather(c + RING)

        @block.scalar
        def _(act):
            for c in range(NT):
                n = rows(c)
                act.wait_ge(s_x, c + 1)
                act.wait_ge(s_ss, c)
                nc.scalar.activation(junk[0:n, :], x[0:n, c, :], ACT.Square, accum_out=ss[0:n, c:c + 1]).then_inc(s_ss, 1)

        @block.vector
        def _(dve):
            def add(c):
                n, q = rows(c), c % RING
                xc = x[0:n, c, :]
                dve.wait_ge(s_l[q], 32 * (c // RING + 1))
                nc.vector.scalar_tensor_tensor(xc, a[0:n, q, :], m.wt[0:n, 0, c:c + 1], xc, ALU.mult, ALU.add).then_inc(s_a, 1)
                dve.wait_ge(s_a, c + 1)
                nc.vector.scalar_tensor_tensor(xc, b[0:n, q, :], m.wt[0:n, 1, c:c + 1], xc, ALU.mult, ALU.add).then_inc(s_x, 1)

            dve.wait_ge(s_g, 16)
            add(0)
            for c in range(NT):
                n, q = rows(c), c % RING
                if c + 1 < NT:
                    add(c + 1)
                dve.wait_ge(s_rs, c + 1)
                if c >= RING:
                    dve.wait_ge(s_o[q], 16 * (c // RING))
                nc.vector.scalar_tensor_tensor(y[0:n, q, :], x[0:n, c, :], ss[0:n, c:c + 1], gf[0:n, :],
                                               ALU.mult, ALU.mult).then_inc(s_y, 1)


class Tables:

    def __init__(self, g, ctx):
        self.wt = g.sb("wt", [P, 2, NT], ctx=ctx)
        self.slot = g.sb("slot", [P, 2, NT], U32, ctx=ctx)
        self.bexp = g.sb("bexp", [P, NBLK], I32, ctx=ctx)
        self.pairs = g.sb("pairs", [P, 1], I32, ctx=ctx)


def build(nc, d, out, stages=99):
    g = Prog(nc, d, out, stages)
    flat = {}
    for n in ("conv_w", "conv_b", "norm_mix", "norm_mem", "norm_memkv", "norm_ffn", "b_gate", "ssm_norm",
              "dt_bias", "d_skip", "gm_ln_g", "gm_ln_b", "gm_bs", "b_router_group", "b_router_expert", "norm_final"):
        a = d[n]
        names = " ".join("abcd"[:len(a.shape)])
        flat[n] = a.rearrange(f"{names} -> ({names})") if len(a.shape) > 1 else a
    g.flat = flat
    g.x_scr = nc.dram_tensor("x_scr", [NC, P, CF, P], F32, kind="Internal").ap()
    g.z_scr = nc.dram_tensor("z_scr", [NT, P, DI], F32, kind="Internal").ap()
    g.h_scr = nc.dram_tensor("h_scr", [TP, D], F32, kind="Internal").ap()
    g.moe_scr = nc.dram_tensor("moe_scr", [NSLOT, D], F32, kind="Internal").ap()
    g.tok_scr = nc.dram_tensor("tok_scr", [NSLOT + P, 1], U32, kind="Internal").ap()
    with g.ctx as top:
        g.psum = top.enter_context(nc.psum_tensor("psum", [P, 8, BANK], F32))
        g.ident = g.sb("ident", [P, P])
        g.ones = g.sb("ones", [P, P])
        g.tri = g.sb("tri", [P, P])
        g.stri = g.sb("stri", [P, P])
        g.same = g.sb("same", [NS, NS])
        g.btri = g.sb("btri", [NS, NS])
        g.colmask = g.sb("colmask", [P, NB, NS])
        g.rowmask = g.sb("rowmask", [NS, NB])
        g.mhalf = g.sb("mhalf", [P, 16])
        g.eps = g.sb("eps", [P, 1])
        g.veca = g.sb("veca", [P, VEC_A])
        g.vecb = g.sb("vecb", [P, VEC_B])
        g.s_out = nc.alloc_semaphore("outputs_stored")
        big1 = g.big1 = g.sb("big1", [P, NT * D])
        big2 = g.sb("big2", [P, NT * D])
        g.R1, g.R2 = (b[:].rearrange("p (t n) -> p t n", n=D) for b in (big1, big2))
        g.R1T, g.R2T = (b[:].rearrange("p (k t) -> p k t", t=TP) for b in (big1, big2))

        def gain(name):
            return g.vecb[:, VEC[name]:VEC[name] + DK]

        def x_load(x):
            return [(x[:, 0:NC, :], d["x_prompt"][0].rearrange("(t p) n -> p t n", p=P)),
                    (x[0:NS, NC, :], d["x_sample"].rearrange("b t n -> (b t) n"))]

        with ExitStack() as mix:
            g.dtb = g.sb("dtb", [P, H], ctx=mix)
            g.dskip = g.sb("dskip", [P, H], ctx=mix)
            g.aneg = g.sb("aneg", [P, H], ctx=mix)
            g.dt = g.sb("dt", [P, NT, H], ctx=mix)
            g.dta = g.sb("dta", [P, NT, H], ctx=mix)
            g.acs = g.sb("acs", [P, NT, H], ctx=mix)
            g.eacs = g.sb("eacs", [P, NT, H], ctx=mix)
            g.etot = g.sb("etot", [P, NT, H], ctx=mix)
            g.dte = g.sb("dte", [P, NT, H], ctx=mix)
            g.xbs = g.sb("xbs", [P, CF, NS], ctx=mix)
            g.uT = g.sb("uT", [P, GMF, T], ctx=mix)
            with ExitStack() as vs:
                g.v = g.sb("v", [P, NT, GM], ctx=vs)
                g.lng = g.sb("lng", [P, GM], ctx=vs)
                g.lnb = g.sb("lnb", [P, GM], ctx=vs)
                g.bs = g.sb("bs", [P, G, P], ctx=vs)
                g.cst = g.sb("cst", [P, CF, 3 * NB], ctx=vs)
                g.lasts = g.sb("lasts", [P, CF, 27], ctx=vs)
                stage_constants(g)
                stage_norm(g, "norm_mix", g.R1, gain("norm_mix"), g.R2T, NT, x_dram=x_load(g.R1))
                if stages < 2:
                    return
                stage_rows(g)
                with ExitStack() as lr:
                    g.lrow = g.sb("lrow", [27, CD], ctx=lr)
                    stage_turned(g)
                if stages < 3:
                    return
                stage_gmlp(g)
            g.renew_semaphores()
            g.yT = g.sb("yT", [P, XF, T], ctx=mix)
            stage_ssd(g)
            stage_ssd_sample(g)
            if stages < 4:
                return
            stage_merge(g)
        stage_add_rows(g, "w_out", g.R1T, d["w_out"][0], g.R2, x_load(g.R2))
        if stages < 5:
            return
        g.renew_semaphores()
        with ExitStack() as at:
            qT = g.sb("qT", [P, DK, T], ctx=at)
            kT = g.sb("kT", [P, DK, ML], ctx=at)
            vr = g.sb("vr", [P, MT, D], ctx=at)
            stage_norm(g, "norm_mem", g.R2, gain("norm_mem"), g.R1T, NT)
            stage_query(g, g.R1T, qT)
            with ExitStack() as me:
                mr = g.sb("mr", [P, MT, D], ctx=me)
                mT = g.sb("mT", [P, DK, ML], ctx=me)
                stage_norm(g, "norm_memkv", mr, gain("norm_memkv"), mT, MT,
                           x_dram=[(mr[:], d["mem_prompt"][0].rearrange("(t p) n -> p t n", p=P))])
                stage_mem_kv(g, mT, kT, vr)
            stage_attention(g, qT, kT, vr, g.R1T)
            stage_attention_sample(g, qT, g.R1T)
        stage_add_rows(g, "w_mem_o", g.R1T, d["w_mem_o"][0], g.R2)
        if stages < 6:
            return
        g.renew_semaphores()
        with ExitStack() as mo:
            m = Tables(g, mo)
            with ExitStack() as gr:
                row = g.sb("ffn_gain_row", [P, D], ctx=gr)
                stage_row_gain(g, row)
                stage_norm(g, "norm_ffn", g.R2, gain("norm_ffn"), g.R1T, NT, rows_dram=(g.h_scr, row))
            stage_router(g, g.R1T, m)
            if stages < 7:
                return
            stage_experts(g, m)
            stage_final(g, g.R2, m)


def stage_row_gain(g, row):
    nc = g.nc
    s = g.sem("ffn_gain_loaded")
    with nc.Block("row_gain") as block:
        @block.sync
        def _(sp):
            sp.dma_start(row[:], g.flat["norm_ffn"].partition_broadcast(P)).then_inc(s, 16)
            sp.wait_ge(s, 16)


_OUTS = [("y_p", (1, SEQ, D)), ("y_s", (NB, LS, D)), ("ssm_p", (1, 1, H, HD, N)), ("conv_p", (1, 1, CONV - 1, CD)),
         ("mk", (1, 1, ML, MH, MD)), ("mv", (1, 1, ML, MH, MD)), ("ssm_s", (1, NB, H, HD, N)),
         ("conv_s", (1, NB, CONV - 1, CD)), ("gv", (1, NB, LS, GM))]
STAGES = 99


def kernel(**inputs):
    import concourse.bacc as bacc
    from concourse.bass_utils import run_bass_kernel_spmd

    nc = bacc.Bacc("TRN2", target_bir_lowering=False, num_devices=1)
    arrays, d = {}, {}
    for name, a in inputs.items():
        a = np.ascontiguousarray(a)
        arrays["in_" + name] = a
        d[name] = nc.dram_tensor("in_" + name, a.shape, mybir.dt.from_np(a.dtype), kind="ExternalInput").ap()
    o = {n: nc.dram_tensor("out_" + n, shape, F32, kind="ExternalOutput").ap() for n, shape in _OUTS}
    out = {
        "y_p": o["y_p"][0], "y_s": o["y_s"].rearrange("b t n -> (b t) n"),
        "ssm_p": o["ssm_p"][0, 0].rearrange("h p n -> (h p) n").rearrange("(j p) n -> p j n", p=P),
        "conv_p": o["conv_p"][0, 0], "mk": o["mk"][0, 0].rearrange("m h e -> m (h e)"),
        "mv": o["mv"][0, 0].rearrange("m h e -> m (h e)"),
        "ssm_s": o["ssm_s"][0].rearrange("b h p n -> b (h p) n"),
        "conv_s": o["conv_s"][0].rearrange("b r c -> (b r) c"), "gv": o["gv"][0].rearrange("b t n -> (b t) n"),
    }
    build(nc, d, out, STAGES)
    r = run_bass_kernel_spmd(nc, [arrays], core_ids=[0])
    return tuple(r.results[0]["out_" + n] for n, _ in _OUTS)
```

```python
from contextlib import ExitStack

import numpy as np

import concourse.bass as bass
import concourse.mybir as mybir
from concourse.alu_op_type import AluOpType as ALU

ACT = mybir.ActivationFunctionType
AX = mybir.AxisListType.X
F32 = mybir.dt.float32
I32 = mybir.dt.int32
U32 = mybir.dt.uint32
F32R = mybir.dt.float32r

P = 128
BANK = 512
D = 1024
SEQ = 1024
NB, LS = 8, 4
NS = NB * LS
T = SEQ + NS
NC = SEQ // P
NT = NC + 1
TP = NT * P
DK = D // P
H, HD, G, R, N = 24, 64, 4, 6, 128
DI = H * HD
GW = R * HD
CONV = 4
CD = DI + 2 * G * N
CF = CD // P
XF = DI // P
GM = 512
GMF = GM // P
ML, MH, MD = 256, 4, 256
MT = ML // P
NG, EPG = 4, 4
NE = NG * EPG
FF = 512
FK = FF // P
EPS = 1e-6
COL_XBC, COL_DT = DI, DI + CD
COL_U = COL_DT + H
COL_V = COL_U + GM
SLAB = T // 3
NBLK = (2 * T + P - 1) // P + NE
NSLOT = NBLK * P
SCALE = MD ** -0.5
BIG = 1.0e30


class Chain:

    def __init__(self, eng, sem, base=0):
        self.eng, self.sem, self.base, self.n = eng, sem, base, 0

    def done(self, ins):
        self.n += 1
        ins.then_inc(self.sem, 1)
        self.eng.wait_ge(self.sem, self.base + self.n)


def mid(ap, n):
    return ap.unsqueeze(1).to_broadcast([ap.shape[0], n, ap.shape[1]])


def last(ap, n):
    return ap.unsqueeze(2).to_broadcast([ap.shape[0], ap.shape[1], n])


class Prog:

    def __init__(self, nc, d, out, stages):
        self.nc, self.d, self.out, self.stages = nc, d, out, stages
        self.ctx = ExitStack()
        self.names, self.sems, self.n_out = [], [], 0

    def sb(self, name, shape, dt=F32, ctx=None):
        if name in self.names:
            name = f"{name}_{len(self.names)}"
        self.names.append(name)
        return (ctx or self.ctx).enter_context(self.nc.sbuf_tensor(name, list(shape), dt))

    def sb_at(self, name, shape, dt=F32, ctx=None):
        t = self.sb(name, shape, dt, ctx)
        return t, self.nc.sbuf_base - int(np.prod(shape[1:])) * 4

    def alias(self, name, shape, at):
        return self.nc.alloc_sbuf_tensor_at(name, list(shape), F32R, offset=at)

    def stored(self):
        self.n_out += 1
        return 16

    def sem(self, name):
        s = self.nc.alloc_semaphore(name)
        self.sems.append(s)
        return s

    def renew_semaphores(self):
        self.nc.clear_and_free_semaphores(self.sems)
        self.nc.all_engine_barrier()
        self.sems = []


VEC_A = CONV * CF + CF
VEC = {"norm_mix": 0, "norm_mem": 8, "norm_memkv": 16, "norm_ffn": 24, "b_gate": 32, "ssm_norm": 48}
VEC_B = 60


def stage_constants(g):
    nc, d = g.nc, g.d
    ps = g.psum
    with ExitStack() as ctx:
        va = g.sb("va", [VEC_A, P], ctx=ctx)
        vb = g.sb("vb", [VEC_B, P], ctx=ctx)
        sc = g.sb("sc_rows", [3 * NB, CD], ctx=ctx)
        alog = g.sb("alog", [P, H], ctx=ctx)
        s_vec = g.sem("c_vec_loaded")
        s_row = g.sem("c_rows_loaded")
        s_alog = g.sem("c_alog_loaded")
        s_one = g.sem("c_ones")
        s_msk = g.sem("c_masks")
        s_tr = g.sem("c_vec_turned")
        s_tr2 = g.sem("c_state_turned")
        s_ev = g.sem("c_evacuated")
        s_exp = g.sem("c_exp")
        block = ctx.enter_context(nc.Block("constants"))

        @block.sync
        def _(sp):
            for i, (name, n) in enumerate((("conv_w", CONV * CF), ("conv_b", CF))):
                sp.dma_start(va[i * CONV * CF:i * CONV * CF + n, :],
                             g.flat[name].rearrange("(a b) -> a b", b=P)).then_inc(s_vec, 16)
            for name, at in VEC.items():
                n = g.flat[name].shape[0] // P
                sp.dma_start(vb[at:at + n, :], g.flat[name].rearrange("(a b) -> a b", b=P)).then_inc(s_vec, 16)
            sp.dma_start(sc[:], d["state_conv"][0].rearrange("b r c -> (b r) c")).then_inc(s_vec, 16)
            sp.dma_start(alog[:], d["a_log"][0].partition_broadcast(P)).then_inc(s_alog, 16)
            for dst, name in ((g.dtb[:], "dt_bias"), (g.dskip[:], "d_skip"), (g.lng[:], "gm_ln_g"),
                              (g.lnb[:], "gm_ln_b"), (g.bs[:].rearrange("p g t -> p (g t)"), "gm_bs")):
                sp.dma_start(dst, g.flat[name].partition_broadcast(P)).then_inc(s_row, 16)
            sp.wait_ge(s_row, 16 * 5)

        @block.gpsimd
        def _(pool):
            nc.gpsimd.memset(g.ones[:], 1.0).then_inc(s_one, 1)
            nc.gpsimd.memset(g.mhalf[:], -0.5)
            nc.gpsimd.memset(g.eps[:], EPS)
            nc.gpsimd.memset(g.colmask[:], 1.0)
            nc.gpsimd.memset(g.rowmask[:], 1.0).then_inc(s_one, 1)
            pool.wait_ge(s_one, 2)
            sel = nc.gpsimd.affine_select
            one, sq = g.ones, [[1, P]]
            sel(g.ident[:], one[:], sq, ALU.is_equal, 0.0, 0, -1)
            sel(g.tri[:], one[:], sq, ALU.is_ge, 0.0, 0, -1)
            sel(g.stri[:], one[:], sq, ALU.is_gt, 0.0, 0, -1)
            quad = [[LS, NB], [0, LS]]
            sel(g.same[:], one[0:NS, 0:NS], [[-LS, NB], [0, LS]], ALU.is_ge, 0.0, 0, 1).then_inc(s_msk, 1)
            sel(g.colmask[:], g.colmask[:], [[-LS, NB], [1, NS]], ALU.is_ge, 0.0, 0, 0).then_inc(s_msk, 1)
            sel(g.rowmask[:], g.rowmask[:], [[-LS, NB]], ALU.is_ge, 0.0, 0, 1).then_inc(s_msk, 1)
            pool.wait_ge(s_msk, 3)
            sel(g.same[:], g.same[:], quad, ALU.is_ge, 0.0, LS - 1, -1).then_inc(s_msk, 1)
            sel(g.colmask[:], g.colmask[:], [[LS, NB], [-1, NS]], ALU.is_ge, 0.0, LS - 1, 0)
            sel(g.rowmask[:], g.rowmask[:], [[LS, NB]], ALU.is_ge, 0.0, LS - 1, -1)
            pool.wait_ge(s_msk, 4)
            sel(g.btri[:], g.same[:], [[1, NS]], ALU.is_ge, 0.0, 0, -1).then_inc(s_msk, 1)

        @block.tensor
        def _(pe):
            pe.wait_ge(s_msk, 5)
            pe.wait_ge(s_vec, 16 * 9)
            nc.tensor.transpose(ps[:, 0, 0:VEC_A], va[:], g.ident[0:VEC_A, 0:VEC_A])
            nc.tensor.transpose(ps[:, 1, 0:VEC_B], vb[:], g.ident[0:VEC_B, 0:VEC_B]).then_inc(s_tr, 1)
            for f in range(CF):
                tr = nc.tensor.transpose(ps[:, 2, f * 3 * NB:(f + 1) * 3 * NB], sc[:, f * P:(f + 1) * P],
                                         g.ident[0:3 * NB, 0:3 * NB])
            tr.then_inc(s_tr2, 1)

        @block.scalar
        def _(act):
            act.wait_ge(s_alog, 16)
            nc.scalar.activation(alog[:], alog[:], ACT.Exp).then_inc(s_exp, 1)

        @block.vector
        def _(dve):
            dve.wait_ge(s_exp, 1)
            nc.vector.tensor_scalar(g.aneg[:], alog[:], -1.0, None, ALU.mult)
            dve.wait_ge(s_tr, 1)
            nc.vector.tensor_copy(g.veca[:], ps[:, 0, 0:VEC_A])
            nc.vector.tensor_copy(g.vecb[:], ps[:, 1, 0:VEC_B])
            dve.wait_ge(s_tr2, 1)
            nc.vector.tensor_copy(g.cst[:].rearrange("p f r -> p (f r)"), ps[:, 2, 0:CF * 3 * NB]).then_inc(s_ev, 1)


def stage_norm(g, tag, x, gain, dst, tiles, x_dram=None, rows_dram=None):
    nc, ps = g.nc, g.psum
    RING = 3
    assert tiles % RING == 0 or tiles < RING
    ring = min(RING, tiles)
    with ExitStack() as ctx:
        xn = g.sb("n_xn", [P, ring, D], ctx=ctx)
        ss = g.sb("n_ss", [P, tiles], ctx=ctx)
        ms = g.sb("n_ms", [P, tiles], ctx=ctx)
        rstd = g.sb("n_rstd", [P, tiles], ctx=ctx)
        xg = g.sb("n_xg", [P, ring, D], ctx=ctx) if rows_dram else None
        s_x = g.sem(tag + "_x_loaded")
        s_zero = g.sem(tag + "_x_padded")
        s_sq = g.sem(tag + "_squares")
        s_ms = g.sem(tag + "_means")
        s_rstd = g.sem(tag + "_rstd")
        s_xn = g.sem(tag + "_xn_ready")
        s_tr = g.sem(tag + "_turned")
        s_free = g.sem(tag + "_psum_free")
        s_xfree = g.sem(tag + "_xn_free")
        s_xg = g.sem(tag + "_xg_ready")
        s_xgf = [g.sem(f"{tag}_xg_stored{i}") for i in range(ring)] if rows_dram else None
        block = ctx.enter_context(nc.Block(tag))

        @block.sync
        def _(sp):
            if x_dram:
                for i, (dst_ap, src) in enumerate(x_dram):
                    if i:
                        sp.wait_ge(s_zero, 1)
                    sp.dma_start(dst_ap, src).then_inc(s_x, 16)
            if rows_dram:
                with sp.Fori(0, tiles // ring) as i:
                    for q in range(ring):
                        sp.wait_ge(s_xg, i * ring + q + 1)
                        sp.dma_start(rows_dram[0].rearrange("(t p) n -> t p n", p=P)[i * ring + q],
                                     xg[:, q, :]).then_inc(s_xgf[q], 16)
                for q in range(ring):
                    sp.wait_ge(s_xgf[q], 16 * (tiles // ring))

        @block.gpsimd
        def _(pool):
            if tiles == NT and x_dram:
                nc.gpsimd.memset(x[:, NT - 1, :], 0.0).then_inc(s_zero, 1)
            pool.wait_ge(s_sq, tiles)
            nc.gpsimd.tensor_scalar(ms[:], ss[:], 1.0 / D, EPS, ALU.mult, ALU.add).then_inc(s_ms, 1)
            pool.wait_ge(s_ms, 1)
            nc.gpsimd.tensor_tensor(rstd[:], ms[:], g.mhalf[:, 0:tiles], ALU.pow).then_inc(s_rstd, 1)
            if rows_dram:
                with pool.Fori(0, tiles // ring) as i:
                    for q in range(ring):
                        pool.wait_ge(s_xn, i * ring + q + 1)
                        pool.wait_ge(s_xgf[q], i * 16)
                        nc.gpsimd.tensor_tensor(xg[:, q, :], xn[:, q, :], rows_dram[1][:], ALU.mult).then_inc(s_xg, 1)

        @block.scalar
        def _(act):
            if x_dram:
                act.wait_ge(s_x, 16 * len(x_dram))
            for t in range(tiles):
                if t >= ring:
                    act.wait_ge(s_sq, t - ring + 1)
                nc.scalar.activation(xn[:, t % ring, :], x[:, t, :], ACT.Square,
                                     accum_out=ss[:, t:t + 1]).then_inc(s_sq, 1)
            act.wait_ge(s_rstd, 1)
            for t in range(tiles):
                q = t % ring
                if t >= ring:
                    act.wait_ge(s_tr, t - ring + 1)
                    if rows_dram:
                        act.wait_ge(s_xg, t - ring + 1)
                nc.scalar.activation(xn[:, q, :], x[:, t, :], ACT.Copy, scale=rstd[:, t:t + 1]).then_inc(s_xn, 1)

        @block.tensor
        def _(pe):
            for t in range(tiles):
                q = t % ring
                pe.wait_ge(s_xn, t + 1)
                if t >= ring:
                    pe.wait_ge(s_free, t - ring + 1)
                for k in range(DK):
                    tr = nc.tensor.transpose(ps[:, 2 * q + k // 4, (k % 4) * P:(k % 4 + 1) * P],
                                             xn[:, q, k * P:(k + 1) * P], g.ident[:])
                tr.then_inc(s_tr, 1)

        @block.vector
        def _(dve):
            for t in range(tiles):
                q = t % ring
                dve.wait_ge(s_tr, t + 1)
                src = ps[:, 2 * q:2 * q + 2, :].rearrange("p b (k t) -> p (b k) t", t=P)
                nc.vector.tensor_tensor(dst[:, :, t * P:(t + 1) * P], src, last(gain, P),
                                        ALU.mult).then_inc(s_free, 1)


def matmul3(nc, out, ah, al, w_h, w_l, start, stop):
    nc.tensor.matmul(out, ah, w_h, start=start, stop=False)
    nc.tensor.matmul(out, ah, w_l, start=False, stop=False)
    return nc.tensor.matmul(out, al, w_h, start=False, stop=stop)


def stage_rows(g):
    nc, ps, hT = g.nc, g.psum, g.R2T
    hh, hl = g.hT_high, g.hT_low
    w_in = g.d["w_in"][0].rearrange("(k p) n -> p k n", p=P)
    NZ = DI // BANK
    with ExitStack() as ctx:
        w = g.sb("r_w", [P, 2, DK, BANK], ctx=ctx)
        wh = g.sb("r_w_high", [P, DK, BANK], F32R, ctx=ctx)
        wl = g.sb("r_w_low", [P, DK, BANK], F32R, ctx=ctx)
        wdt = g.sb("r_wdt", [P, DK, H], ctx=ctx)
        wdth = g.sb("r_wdt_high", [P, DK, H], F32R, ctx=ctx)
        wdtl = g.sb("r_wdt_low", [P, DK, H], F32R, ctx=ctx)
        zs = g.sb("r_z", [P, 3, BANK], ctx=ctx)
        dtT = g.sb("r_dtT", [H, TP], ctx=ctx)
        st = g.sb("r_stats", [P, NT, 6], ctx=ctx)
        mv = g.sb("r_mv", [P, NT, 2], ctx=ctx)
        rs = g.sb("r_rstd", [P, NT], ctx=ctx)
        t1 = g.sb("r_t1", [P, NT, H], ctx=ctx)
        t2 = g.sb("r_t2", [P, NT, H], ctx=ctx)
        tot = g.etot
        s_w = [g.sem(f"r_w_loaded{i}") for i in range(2)]
        s_wdt = g.sem("r_wdt_loaded")
        s_mm = g.sem("r_product")
        s_ev = g.sem("r_evacuated")
        s_zst = [g.sem(f"r_z_stored{i}") for i in range(3)]
        s_dtT, s_dte = g.sem("r_dtT"), g.sem("r_dtT_read")
        s_dt = g.sem("r_dt")
        s_pad = g.sem("r_padded")
        s_dta = g.sem("r_dt_chain")
        s_cum = g.sem("r_cum")
        s_v = g.sem("r_v_chain")
        s_vm = g.sem("r_v_stats")
        s_vo = g.sem("r_v_out")
        s_vr = g.sem("r_v_rstd")
        s_act = g.sem("r_act")
        s_hh, s_hl = g.sem("r_act_high"), g.sem("r_act_low")
        s_wh, s_wl, s_wf = g.sem("r_w_high_ready"), g.sem("r_w_low_ready"), g.sem("r_w_parts_used")
        s_dh, s_dl = g.sem("r_wdt_high_ready"), g.sem("r_wdt_low_ready")
        PW = 4

        def piece(t, p):
            return t[:, 2 * p:2 * p + 2, :].rearrange("p k n -> p (k n)")

        def raw(j, p):
            return w[:, j % 2, 2 * p:2 * p + 2, :].rearrange("p k n -> p (k n)")

        def tile(t, c):
            return t[:, :, c * P:(c + 1) * P]

        first_col = [COL_V] + [j * BANK for j in range(NZ)]
        block = ctx.enter_context(nc.Block("rows"))

        @block.sync
        def _(sp):
            for j in range(2):
                sp.dma_start(w[:, j], w_in[:, :, first_col[j]:first_col[j] + BANK]).then_inc(s_w[j], 16)
            with nc.allow_non_contiguous_dma(reason="24 columns of dt"):
                sp.dma_start(wdt[:], w_in[:, :, COL_DT:COL_DT + H]).then_inc(s_wdt, 16)
            for j in range(2, NZ + 1):
                sp.wait_ge(s_wl, PW * (j - 1))
                sp.dma_start(w[:, j % 2], w_in[:, :, first_col[j]:first_col[j] + BANK]).then_inc(s_w[j % 2], 16)
            sp.wait_ge(s_vo, NT)
            sp.dma_start(g.out["gv"], g.v[0:NS, NT - 1, :]).then_inc(g.s_out, g.stored())
            sp.wait_ge(g.s_out, 16 * g.n_out)

        @block.tensor
        def _(pe):
            for j in range(NZ + 1):
                for c in range(NT):
                    n = j * NT + c
                    if j == 0:
                        pe.wait_ge(s_hl, c + 1)
                    if n >= 3:
                        pe.wait_ge(s_ev, n - 2)
                    for k in range(DK):
                        if c == 0 and k % 2 == 0:
                            pe.wait_ge(s_wl, PW * j + k // 2 + 1)
                        mm = matmul3(nc, ps[:, n % 3, :], tile(hh, c)[:, k, :], tile(hl, c)[:, k, :], wh[:, k, :],
                                     wl[:, k, :], k == 0, k == DK - 1)
                        if c == NT - 1 and k % 2 and k < DK - 1:
                            mm.then_inc(s_wf, 1)
                    mm.then_inc(s_mm, 1)
                    if n == NT:
                        pe.wait_ge(s_dte, 2)
                        for t in range(NT):
                            tr = nc.tensor.transpose(ps[:, 6, t * H:(t + 1) * H], dtT[:, t * P:(t + 1) * P],
                                                     g.ident[0:H, 0:H])
                        tr.then_inc(s_dt, 1)
                if j == 0:
                    pe.wait_ge(s_dl, 1)
                    for n in range(3):
                        for k in range(DK):
                            x = slice(n * SLAB, (n + 1) * SLAB)
                            mm = matmul3(nc, ps[0:H, 3 + n, 0:SLAB], wdth[:, k, :], wdtl[:, k, :],
                                         hh[:, k, x], hl[:, k, x], k == 0, k == DK - 1)
                    mm.then_inc(s_dtT, 1)
                if j == 1:
                    pe.wait_ge(s_dta, 4)
                    a = g.dta[:, 0:NC, :].rearrange("p c h -> p (c h)")
                    nc.tensor.matmul(ps[:, 4, 0:NC * H], g.tri[:], a, start=True, stop=True)
                    nc.tensor.matmul(ps[0:NS, 4, NC * H:NT * H], g.btri[:], g.dta[0:NS, NC, :], start=True, stop=True)
                    nc.tensor.matmul(ps[:, 5, 0:NC * H], g.ones[:], a, start=True, stop=True)
                    nc.tensor.matmul(ps[0:NS, 5, NC * H:NT * H], g.same[:], g.dta[0:NS, NC, :],
                                     start=True, stop=True).then_inc(s_cum, 1)

        @block.scalar
        def _(act):
            def softplus():
                act.wait_ge(s_dta, 1)
                nc.scalar.activation(t1[:], t2[:], ACT.Abs).then_inc(s_act, 1)
                act.wait_ge(s_act, 1)
                nc.scalar.activation(t1[:], t1[:], ACT.Exp, scale=-1.0).then_inc(s_act, 1)
                act.wait_ge(s_act, 2)
                nc.scalar.activation(t1[:], t1[:], ACT.Ln, bias=1.0).then_inc(s_act, 1)

            def decays():
                act.wait_ge(s_dta, 5)
                nc.scalar.activation(g.eacs[:], g.acs[:], ACT.Exp)
                act.wait_ge(s_dta, 6)
                nc.scalar.activation(g.etot[:], tot[:], ACT.Exp)
                nc.scalar.activation(t1[:], t2[:], ACT.Exp).then_inc(s_act, 1)

            def w_high(j):
                act.wait_ge(s_w[j % 2], 16 * (j // 2 + 1))
                for p in range(PW):
                    if j and p < PW - 1:
                        act.wait_ge(s_wf, (j - 1) * (PW - 1) + p + 1)
                    elif j:
                        act.wait_ge(s_mm, j * NT)
                    nc.scalar.activation(piece(wh, p), raw(j, p), ACT.Copy).then_inc(s_wh, 1)

            def high(c):
                nc.scalar.activation(tile(hh, c), tile(hT, c), ACT.Copy).then_inc(s_hh, 1)

            high(0)
            w_high(0)
            high(1)
            act.wait_ge(s_wdt, 16)
            nc.scalar.activation(wdth[:], wdt[:], ACT.Copy).then_inc(s_dh, 1)
            for j in range(NZ + 1):
                for c in range(NT):
                    n = j * NT + c
                    if j == 0 and c + 2 < NT:
                        high(c + 2)
                    if c == NT - 1 and j < NZ:
                        w_high(j + 1)
                    act.wait_ge(s_mm, n + 1)
                    if j:
                        m = n - NT
                        if m >= 3:
                            act.wait_ge(s_zst[m % 3], 16 * (m // 3))
                        nc.scalar.activation(zs[:, m % 3, :], ps[:, n % 3, :], ACT.Silu).then_inc(s_ev, 1)
                        act.wait_ge(s_ev, n + 1)
                        act.dma_start(g.z_scr[c, :, (j - 1) * BANK:j * BANK], zs[:, m % 3, :]).then_inc(s_zst[m % 3], 16)
                    else:
                        nc.scalar.activation(g.v[:, c, :], ps[:, n % 3, :], ACT.Gelu).then_inc(s_ev, 1)
                    if n == NT + 1:
                        softplus()
                if j == 1:
                    decays()
            for s in range(3):
                act.wait_ge(s_zst[s], 16 * (NZ * NT // 3))

        @block.vector
        def _(dve):
            nc.vector.memset(g.acs[:, NC, :], 0.0)
            nc.vector.memset(dtT[:, T:TP], 0.0).then_inc(s_dte, 1)
            nc.vector.memset(tot[:, NC, :], 0.0).then_inc(s_pad, 1)
            dve.wait_ge(s_pad, 1)

            def low(c):
                dve.wait_ge(s_hh, c + 1)
                nc.vector.tensor_tensor(tile(hl, c), tile(hT, c), tile(hh, c).bitcast(F32), ALU.subtract).then_inc(s_hl, 1)

            def w_low(j):
                for p in range(PW):
                    dve.wait_ge(s_wh, j * PW + p + 1)
                    nc.vector.tensor_tensor(piece(wl, p), raw(j, p), piece(wh, p).bitcast(F32),
                                            ALU.subtract).then_inc(s_wl, 1)

            low(0)
            w_low(0)
            low(1)
            dve.wait_ge(s_dh, 1)
            nc.vector.tensor_tensor(wdtl[:], wdt[:], wdth[:].bitcast(F32), ALU.subtract).then_inc(s_dl, 1)
            for c in range(2, NT):
                low(c)
            w_low(1)
            dve.wait_ge(s_dtT, 1)
            nc.vector.tensor_copy(dtT[:, 0:T].rearrange("p (n t) -> p n t", t=SLAB),
                                  ps[0:H, 3:6, 0:SLAB]).then_inc(s_dte, 1)
            ch = Chain(dve, s_dta)
            dve.wait_ge(s_dt, 1)
            pdt = ps[:, 6, 0:NT * H].rearrange("p (c h) -> p c h", h=H)
            ch.done(nc.vector.tensor_tensor(t2[:], pdt, mid(g.dtb[:], NT), ALU.add))
            dve.wait_ge(s_act, 3)
            ch.done(nc.vector.tensor_scalar(g.dt[:], t2[:], 0.0, None, ALU.max))
            ch.done(nc.vector.tensor_tensor(g.dt[:], g.dt[:], t1[:], ALU.add))
            ch.done(nc.vector.tensor_tensor(g.dta[:], g.dt[:], mid(g.aneg[:], NT), ALU.mult))
            w_low(2)
            dve.wait_ge(s_cum, 1)
            for dst, b in ((g.acs, 4), (tot, 5)):
                nc.vector.tensor_copy(dst[:, 0:NC, :], ps[:, b, 0:NC * H].rearrange("p (c h) -> p c h", h=H))
                op = nc.vector.tensor_copy(dst[0:NS, NC, :], ps[0:NS, b, NC * H:NT * H])
            ch.done(op)
            ch.done(nc.vector.tensor_tensor(t2[:], tot[:], g.acs[:], ALU.subtract))
            dve.wait_ge(s_act, 4)
            ch.done(nc.vector.tensor_tensor(g.dte[:], g.dt[:], t1[:], ALU.mult))
            w_low(3)
            dve.wait_ge(s_ev, NT)
            for c in range(NT):
                nc.vector.bn_stats(st[:, c, :], g.v[:, c, :]).then_inc(s_v, 1)
                dve.wait_ge(s_v, c + 1)
                nc.vector.bn_aggr(mv[:, c, :], st[:, c, :]).then_inc(s_vm, 1)
            dve.wait_ge(s_vr, 1)
            vc = Chain(dve, s_v, NT)
            for c in range(NT):
                vc.done(nc.vector.tensor_scalar(g.v[:, c, :], g.v[:, c, :], mv[:, c, 0:1], rs[:, c:c + 1],
                                                ALU.subtract, ALU.mult))
                vc.done(nc.vector.tensor_tensor(g.v[:, c, :], g.v[:, c, :], g.lng[:], ALU.mult))
                nc.vector.tensor_tensor(g.v[:, c, :], g.v[:, c, :], g.lnb[:], ALU.add).then_inc(s_vo, 1)

        @block.gpsimd
        def _(pool):
            pool.wait_ge(s_vm, NT)
            nc.gpsimd.tensor_scalar(rs[:], mv[:, :, 1], 1.0, EPS, ALU.mult, ALU.add).then_inc(s_vm, 1)
            pool.wait_ge(s_vm, NT + 1)
            nc.gpsimd.tensor_tensor(rs[:], rs[:], g.mhalf[:, 0:NT], ALU.pow).then_inc(s_vr, 1)


CB_S = CONV - 1 + SEQ
CB_B = CONV - 1 + LS
CB_W = CB_S + NB * CB_B
CB_OUT = CB_W - (CONV - 1)


def stage_turned(g):
    nc, ps = g.nc, g.psum
    hh, hl = g.hT_high, g.hT_low
    w_in = g.d["w_in"][0].rearrange("(k p) n -> p k n", p=P)
    w_gate = g.d["w_gate"][0].rearrange("(k p) n -> p k n", p=P)
    GF = 2 * DK
    ALL = CF + GMF + GF
    with ExitStack() as ctx:
        w = g.sb("t_w", [P, 2, DK, P], ctx=ctx)
        wh = g.sb("t_w_high", [P, 2, DK, P], F32R, ctx=ctx)
        wl = g.sb("t_w_low", [P, 2, DK, P], F32R, ctx=ctx)
        cb = g.sb("t_conv_in", [P, 2, CB_W], ctx=ctx)
        ca = g.sb("t_conv_out", [P, 2, CB_W], ctx=ctx)
        s_w = [g.sem(f"t_w_loaded{i}") for i in range(2)]
        s_mm = g.sem("t_product")
        s_wh, s_wl = g.sem("t_w_high_ready"), g.sem("t_w_low_ready")
        s_pf = g.sem("t_psum_free")
        s_gt = g.sem("t_gate_ready")
        s_gst = [g.sem(f"t_gate_stored{i}") for i in range(2)]
        s_z = g.sem("t_zeroed")
        s_in = g.sem("t_conv_in_ready")
        s_st = g.sem("t_state_in")
        s_c = g.sem("t_conv_chain")
        s_co = g.sem("t_conv_done")
        s_so = g.sem("t_silu_done")
        s_sto = [g.sem(f"t_stored{i}") for i in range(2)]
        s_ls = g.sem("t_lasts")
        s_lt = g.sem("t_lasts_turned")
        s_le = g.sem("t_lasts_rows")
        block = ctx.enter_context(nc.Block("turned"))

        def sample_view(ap, lo, n):
            return ap[:, CB_S:CB_S + NB * CB_B].rearrange("p (b j) -> p b j", j=CB_B)[:, :, lo:lo + n]

        @block.sync
        def _(sp):
            def load(f, q, src):
                sp.wait_ge(s_wl, f + 1)
                sp.dma_start(w[:, q], src).then_inc(s_w[q], 16)

            with sp.Fori(0, CF // 2) as i:
                for q in range(2):
                    load(i * 2 + q, q, w_in[:, :, bass.ds(i * 2 * P + COL_XBC + q * P, P)])
            for j in range(GMF):
                load(CF + j, j % 2, w_in[:, :, COL_U + j * P:COL_U + (j + 1) * P])
            with sp.Fori(0, GF // 2) as i:
                for q in range(2):
                    load(i * 2 + (CF + GMF + q), q, w_gate[:, :, bass.ds(i * 2 * P + q * P, P)])
            sp.wait_ge(s_le, 3)
            sp.dma_start(g.out["conv_p"], g.lrow[0:CONV - 1, :]).then_inc(g.s_out, g.stored())
            sp.dma_start(g.out["conv_s"], g.lrow[CONV - 1:27, :]).then_inc(g.s_out, g.stored())
            sp.wait_ge(g.s_out, 16 * g.n_out)

        @block.tensor
        def _(pe):
            with pe.Fori(0, ALL // 2) as i:
                for q in range(2):
                    pe.wait_ge(s_wl, i * 2 + q + 3)
                    pe.wait_ge(s_pf, i * 2 + q + 1)
                    for n in range(3):
                        x = slice(n * SLAB, (n + 1) * SLAB)
                        for k in range(DK):
                            mm = matmul3(nc, ps[:, 3 * q + n, 0:SLAB], wh[:, q, k, :], wl[:, q, k, :],
                                         hh[:, k, x], hl[:, k, x], k == 0, k == DK - 1)
                    mm.then_inc(s_mm, 1)
            pe.wait_ge(s_ls, CF + 2)
            for r in range(3):
                if r:
                    pe.wait_ge(s_le, r)
                for k in range(8 if r < 2 else 4):
                    f = 8 * r + k
                    tr = nc.tensor.transpose(ps[0:27, 6 + k // 4, (k % 4) * P:(k % 4 + 1) * P],
                                             g.lasts[:, f, :], g.ident[:])
                tr.then_inc(s_lt, 1)

        @block.scalar
        def _(act):
            act.sem_inc(s_pf, 2)

            def high(f, n, q):
                act.wait_ge(s_w[q], n * 16)
                nc.scalar.activation(wh[:, q], w[:, q], ACT.Copy).then_inc(s_wh, 1)

            high(0, 1, 0)
            high(1, 1, 1)
            act.wait_ge(s_z, 1)
            with act.Fori(0, CF // 2) as i:
                for q in range(2):
                    act.wait_ge(s_mm, i * 2 + q + 1)
                    act.wait_ge(s_co, i * 2 + q + 1)
                    act.wait_ge(s_ls, i * 2 + q + 1)
                    for n in range(2):
                        nc.scalar.copy(cb[:, q, CONV - 1 + n * SLAB:CONV - 1 + (n + 1) * SLAB], ps[:, 3 * q + n, 0:SLAB])
                    nc.scalar.copy(cb[:, q, CONV - 1 + 2 * SLAB:CB_S], ps[:, 3 * q + 2, 0:SEQ - 2 * SLAB])
                    nc.scalar.copy(sample_view(cb[:, q, :], CONV - 1, LS),
                                   ps[:, 3 * q + 2, SEQ - 2 * SLAB:SLAB].rearrange("p (b j) -> p b j", j=LS)
                                   ).then_inc(s_pf, 1)
                    high(i * 2 + q + 2, i + 2, q)
                for q in range(2):
                    act.wait_ge(s_co, i * 2 + q + 3)
                    nc.scalar.activation(ca[:, q, 0:SEQ], ca[:, q, 0:SEQ], ACT.Silu)
                    nc.scalar.activation(g.xbs[:, i * 2 + q, :].rearrange("p (b j) -> p b j", j=LS),
                                         sample_view(ca[:, q, :], 0, LS), ACT.Silu).then_inc(s_so, 1)
                    act.wait_ge(s_so, i * 2 + q + 1)
                    act.dma_start(g.x_scr[:, :, i * 2 + q, :].rearrange("c p t -> p c t"),
                                  ca[:, q, 0:SEQ].rearrange("p (c t) -> p c t", t=P)).then_inc(s_sto[q], 16)
            for f in range(GMF):
                act.wait_ge(s_mm, CF + f + 1)
                for n in range(3):
                    a = nc.scalar.activation(g.uT[:, f, n * SLAB:(n + 1) * SLAB], ps[:, 3 * (f % 2) + n, 0:SLAB], ACT.Gelu)
                a.then_inc(s_pf, 1)
                high(CF + f + 2, (CF + f + 2) // 2 + 1, f % 2)

            def gate(i, q, more):
                m = i * 2 + (CF + GMF + q)
                act.wait_ge(s_mm, m + 1)
                if more is not None:
                    act.wait_ge(s_gst[q], i * 16)
                bias = g.vecb[:, bass.ds(i * 2 + (VEC["b_gate"] + q), 1)]
                nc.scalar.activation(cb[:, q, 0:T].rearrange("p (n t) -> p n t", t=SLAB),
                                     ps[:, 3 * q:3 * q + 3, 0:SLAB], ACT.Sigmoid, bias=bias).then_inc(s_pf, 1)
                if more:
                    high(m + 2, i + ((CF + GMF) // 2 + 2), q)
                act.wait_ge(s_pf, m + 3)
                act.dma_start(g.gate_scr[i * 2 + q], cb[:, q, 0:T]).then_inc(s_gst[q], 16)

            act.wait_ge(s_co, CF + 2)
            act.wait_ge(s_ls, CF + 2)
            with act.Fori(0, GF // 2 - 1) as i:
                for q in range(2):
                    gate(i, q, True)
            for q in range(2):
                gate(GF // 2 - 1, q, False)
            for q in range(2):
                act.wait_ge(s_sto[q], 16 * (CF // 2))
                act.wait_ge(s_gst[q], 16 * (GF // 2))

        @block.vector
        def _(dve):
            nc.vector.memset(cb[:, :, 0:CONV - 1], 0.0).then_inc(s_z, 1)
            dve.sem_inc(s_co, 2)
            dve.sem_inc(s_wl, 2)

            def low(f, q):
                dve.wait_ge(s_wh, f + 1)
                nc.vector.tensor_tensor(wl[:, q], w[:, q], wh[:, q].bitcast(F32), ALU.subtract).then_inc(s_wl, 1)

            low(0, 0)
            low(1, 1)
            with dve.Fori(0, CF // 2) as i:
                for q in range(2):
                    f = i * 2 + q
                    o, c = ca[:, q, 0:CB_OUT], cb[:, q, :]
                    dve.wait_ge(s_pf, f + 3)
                    dve.wait_ge(s_st, f + 1)
                    dve.wait_ge(s_so, i * 2)
                    dve.wait_ge(s_sto[q], i * 16)
                    wk = [g.veca[:, bass.ds(f + j * CF, 1)] for j in range(CONV + 1)]
                    ch = Chain(dve, s_c, i * 6 + 3 * q)
                    ch.done(nc.vector.tensor_scalar(o, c[:, 0:CB_OUT], wk[0], wk[CONV], ALU.mult, ALU.add))
                    for j in range(1, CONV):
                        op = nc.vector.scalar_tensor_tensor(o, c[:, j:j + CB_OUT], wk[j], o, ALU.mult, ALU.add)
                        if j < CONV - 1:
                            ch.done(op)
                    op.then_inc(s_co, 1)
                    low(f + 2, q)
            with dve.Fori(0, (GMF + GF) // 2 - 1) as i:
                for q in range(2):
                    low(i * 2 + (CF + 2 + q), q)
            for r in range(3):
                dve.wait_ge(s_lt, r + 1)
                n = 8 if r < 2 else 4
                nc.vector.tensor_copy(g.lrow[:, 8 * r * P:(8 * r + n) * P],
                                      ps[0:27, 6:6 + n // 4, :].rearrange("p b t -> p (b t)")).then_inc(s_le, 1)

        @block.gpsimd
        def _(pool):
            pool.sem_inc(s_ls, 2)
            with pool.Fori(0, CF // 2) as i:
                for q in range(2):
                    f = i * 2 + q
                    pool.wait_ge(s_co, f + 1)
                    nc.gpsimd.tensor_copy(sample_view(cb[:, q, :], 0, CONV - 1),
                                          g.cst[:, f, :].rearrange("p (b j) -> p b j", j=CONV - 1)).then_inc(s_st, 1)
                    pool.wait_ge(s_pf, f + 3)
                    nc.gpsimd.tensor_copy(g.lasts[:, f, 0:CONV - 1], cb[:, q, SEQ:SEQ + CONV - 1])
                    nc.gpsimd.tensor_copy(g.lasts[:, f, CONV - 1:27].rearrange("p (b j) -> p b j", j=CONV - 1),
                                          sample_view(cb[:, q, :], LS, CONV - 1)).then_inc(s_ls, 1)


def stage_gmlp(g):
    nc, ps, d = g.nc, g.psum, g.d
    with ExitStack() as ctx:
        wr = g.sb("g_w_rows", [P, G, P], ctx=ctx)
        wT = g.sb("g_wT", [P, G, P], ctx=ctx)
        ws = g.sb("g_w_sample", [NS, G, NS], ctx=ctx)
        sg = g.sb("g_s", [P, 2, G, P], ctx=ctx)
        s_w = g.sem("g_w_loaded")
        s_ws = g.sem("g_ws_loaded")
        s_z = g.sem("g_zeroed")
        s_tr = g.sem("g_w_turned")
        s_wT = g.sem("g_w_ready")
        s_mm = g.sem("g_product")
        s_sb = g.sem("g_biased")
        s_u = g.sem("g_gated")
        block = ctx.enter_context(nc.Block("gmlp"))

        @block.sync
        def _(sp):
            sp.dma_start(wr[:], d["gm_ws"][0].rearrange("g t s -> t g s")).then_inc(s_w, 16)
            sp.wait_ge(s_z, 1)
            with nc.allow_non_contiguous_dma(reason="4 x 4 corners"):
                for b in range(NB):
                    for gg in range(G):
                        src = d["gm_ws"][0, gg, 0:LS, 0:LS].rearrange("t s -> s t")
                        sp.dma_start(ws[LS * b:LS * b + LS, gg, LS * b:LS * b + LS], src).then_inc(s_ws, 16)

        @block.gpsimd
        def _(pool):
            nc.gpsimd.memset(ws[:], 0.0).then_inc(s_z, 1)

        @block.tensor
        def _(pe):
            pe.wait_ge(s_w, 16)
            for gg in range(G):
                tr = nc.tensor.transpose(ps[:, 0, gg * P:(gg + 1) * P], wr[:, gg, :], g.ident[:])
            tr.then_inc(s_tr, 1)
            pe.wait_ge(s_wT, 2)
            for c in range(NT):
                b = 1 + c % 2
                if c >= 2:
                    pe.wait_ge(s_sb, c - 1)
                for gg in range(G):
                    if c < NC:
                        mm = nc.tensor.matmul(ps[:, b, gg * P:(gg + 1) * P], g.v[:, c, gg * P:(gg + 1) * P],
                                              wT[:, gg, :], start=True, stop=True)
                    else:
                        mm = nc.tensor.matmul(ps[:, b, gg * NS:(gg + 1) * NS], g.v[0:NS, c, gg * P:(gg + 1) * P],
                                              ws[:, gg, :], start=True, stop=True)
                mm.then_inc(s_mm, 1)

        @block.vector
        def _(dve):
            dve.wait_ge(s_tr, 1)
            nc.vector.tensor_tensor(wT[:], ps[:, 0, :].rearrange("p (g t) -> p g t", t=P), mid(g.tri[:], G),
                                    ALU.mult).then_inc(s_wT, 1)
            dve.wait_ge(s_ws, 16 * NB * G)
            nc.vector.tensor_tensor(ws[:], ws[:], mid(g.btri[:], G), ALU.mult).then_inc(s_wT, 1)
            for c in range(NT):
                b, n = 1 + c % 2, P if c < NC else NS
                dve.wait_ge(s_mm, c + 1)
                s = sg[:, c % 2, :, 0:n]
                src = ps[:, b, 0:G * n].rearrange("p (g t) -> p g t", t=n)
                if c < NC:
                    nc.vector.tensor_tensor(s, src, g.bs[:], ALU.add).then_inc(s_sb, 1)
                else:
                    for gg in range(G):
                        op = nc.vector.tensor_tensor(s[:, gg, :].rearrange("p (b j) -> p b j", j=LS),
                                                     src[:, gg, :].rearrange("p (b j) -> p b j", j=LS),
                                                     mid(g.bs[:, gg, 0:LS], NB), ALU.add)
                    op.then_inc(s_sb, 1)
                dve.wait_ge(s_sb, c + 1)
                u = g.uT[:, :, c * P:c * P + n]
                nc.vector.tensor_tensor(u, u, s, ALU.mult).then_inc(s_u, 1)


def stage_ssd(g):
    nc, ps = g.nc, g.psum
    XW = R * HD
    TX, YO, RB, YD, ST, YT = 0, 1, 3, 5, 6, 7
    gain = VEC["ssm_norm"]
    STEPS = NC * G
    with ExitStack() as ctx:
        xin = g.big[:, 0:G * 5 * P].rearrange("p (g f t) -> p g f t", g=G, t=P)
        zin = g.big[:, CD:CD + DI].rearrange("p (g w) -> p g w", g=G)
        ho = g.big[:, CD + DI:CD + 2 * DI].rearrange("p (f n) -> p f n", n=N)
        dtc = g.sb("s_dta", [P, 2, H], ctx=ctx)
        xrb = g.sb("s_xrow", [P, 2, XW + P], ctx=ctx)
        xdt = g.sb("s_xdt", [P, 2, XW], ctx=ctx)
        xdd = g.sb("s_xdd", [P, 2, XW], ctx=ctx)
        xsk = g.sb("s_xskip", [P, 2, XW], ctx=ctx)
        cbm = g.sb("s_cb", [P, 2, P], ctx=ctx)
        att = g.sb("s_att", [P, 2, R, P], ctx=ctx)
        y = g.sb("s_y", [P, 2, XW], ctx=ctx)
        yz = g.sb("s_yz", [P, G, XW], ctx=ctx)
        yn = g.sb("s_yn", [P, 2, XW], ctx=ctx)
        junk = g.sb("s_junk", [P, XW], ctx=ctx)
        h = g.sb("s_h", [P, G, XW], ctx=ctx)
        ss = g.sb("s_ss", [P, G], ctx=ctx)
        rs = g.sb("s_rs", [P, G], ctx=ctx)
        s_in = [g.sem(f"s_xbc_loaded{i}") for i in range(G)]
        s_zin = [g.sem(f"s_z_loaded{i}") for i in range(G)]
        s_tx, s_yo, s_rb, s_yd, s_st, s_yt = (g.sem("s_" + x) for x in (
            "x_turned", "cb_and_yoff", "running_sums", "ydiag", "new_state", "y_turned"))
        s_xr, s_e, s_ss, s_yn, s_ye = (g.sem("s_" + x) for x in (
            "x_rows", "exp", "squares", "y_normed", "yT_written"))
        s_xdt, s_cbm, s_att, s_y1, s_y2, s_h = (g.sem("s_" + x) for x in (
            "xdt", "cb_masked", "att", "y1", "y2", "h_updated"))
        s_xdd, s_hd, s_y3, s_yz, s_ms, s_rs, s_dtc = (g.sem("s_" + x) for x in (
            "xdd", "h_decayed", "y3", "yz", "mean", "rstd", "dta_chunk"))
        s_rl = g.sem("s_differences")
        s_ht, s_ho = g.sem("s_h_turned"), g.sem("s_h_rows_ready")
        block = ctx.enter_context(nc.Block("ssd"))

        def before(c, gg, k, first, do):
            if gg >= k:
                do(c, gg - k)
            elif not first:
                do(c - 1, gg - k + G)

        def after(k, m, do):
            n = STEPS + m - k
            if n < STEPS:
                do(n // G, n % G)

        def chunks(eng, body):
            body(0, True, False)
            with eng.Fori(1, NC - 1) as c:
                body(c, False, False)
            body(NC - 1, False, True)

        @block.sync
        def _(sp):
            def load(c, gg):
                x = g.x_scr[c].rearrange("p f t -> p f t")
                sp.dma_start(xin[:, gg, 0:3, :], x[:, 3 * gg:3 * gg + 3, :]).then_inc(s_in[gg], 16)
                sp.dma_start(xin[:, gg, 3:5, :], x[:, XF + gg:CF:G, :]).then_inc(s_in[gg], 16)

            def load_z(c, gg):
                sp.dma_start(zin[:, gg, :], g.z_scr[c][:, gg * XW:(gg + 1) * XW]).then_inc(s_zin[gg], 16)

            for gg in range(G):
                load(0, gg)
                load_z(0, gg)
            with sp.Fori(1, NC) as c:
                for gg in range(G):
                    sp.wait_ge(s_yo, (c - 1) * 4 + gg + 1)
                    load(c, gg)
                    sp.wait_ge(s_yz, (c - 1) * 4 + gg + 1)
                    load_z(c, gg)
            sp.wait_ge(s_ho, 1)
            sp.dma_start(g.out["ssm_p"], ho).then_inc(g.s_out, g.stored())
            sp.wait_ge(g.s_out, 16 * g.n_out)

        @block.tensor
        def _(pe):
            pe.wait_ge(s_dtc, 1)

            def front(c, gg):
                n, q = c * 4 + gg, gg % 2
                xb = xin[:, gg]
                pe.wait_ge(s_in[gg], c * 32 + 32)
                pe.wait_ge(s_xr, n)
                for j in range(4):
                    tr = nc.tensor.transpose(ps[:, TX, j * P:(j + 1) * P], xb[:, j, :], g.ident[:])
                tr.then_inc(s_tx, 1)
                pe.wait_ge(s_y1, n + 1)
                pe.wait_ge(s_h, n + 1)
                nc.tensor.matmul(ps[:, YO + q, XW:XW + P], xb[:, 3, :], xb[:, 4, :], start=True, stop=True)
                nc.tensor.matmul(ps[:, YO + q, 0:XW], xb[:, 4, :], h[:, gg, :], start=True, stop=True).then_inc(s_yo, 1)
                pe.wait_ge(s_rl, n)
                pe.wait_ge(s_dtc, c * 2 + gg // 2 + 1)
                for r in range(R):
                    a = dtc[:, gg // 2, gg * R + r:gg * R + r + 1].to_broadcast([P, P])
                    mm = nc.tensor.matmul(ps[:, RB + r // 3, (r % 3) * P:(r % 3 + 1) * P], a, g.tri[:],
                                          start=True, stop=True)
                mm.then_inc(s_rb, 1)

            def turn(c, gg):
                n, q = c * 4 + gg, gg % 2
                pe.wait_ge(s_yn, n + G + 1)
                pe.wait_ge(s_ye, n)
                for j in range(3):
                    tr = nc.tensor.transpose(ps[:, YT, j * P:(j + 1) * P], yn[:, q, j * P:(j + 1) * P], g.ident[:])
                tr.then_inc(s_yt, 1)

            def back(c, gg):
                n, q = c * 4 + gg, gg % 2
                pe.wait_ge(s_att, n + 1)
                pe.wait_ge(s_y2, n)
                for r in range(R):
                    mm = nc.tensor.matmul(ps[:, YD, r * HD:(r + 1) * HD], att[:, q, r, :],
                                          xdt[:, q, r * HD:(r + 1) * HD], start=True, stop=True)
                mm.then_inc(s_yd, 1)
                pe.wait_ge(s_xdd, n + 1)
                pe.wait_ge(s_h, n + G)
                nc.tensor.matmul(ps[:, ST, 0:XW], xrb[:, q, XW:XW + P], xdd[:, q, :], start=True,
                                 stop=True).then_inc(s_st, 1)

            def body(c, first, last):
                for gg in range(G):
                    before(c, gg, 4, first, turn)
                    if gg < G - 1:
                        front(c, gg + 1)
                    elif not last:
                        front(c + 1, 0)
                    back(c, gg)

            front(0, 0)
            chunks(pe, body)
            for m in range(4):
                after(4, m, turn)
            pe.wait_ge(s_h, STEPS + G)
            pe.wait_ge(s_ye, STEPS)
            for j in range(XF):
                tr = nc.tensor.transpose(ps[:, j // 4, (j % 4) * P:(j % 4 + 1) * P],
                                         h[:, j // 3, (j % 3) * P:(j % 3 + 1) * P], g.ident[:])
            tr.then_inc(s_ht, 1)

        @block.scalar
        def _(act):
            act.sem_inc(s_st, 2)
            act.sem_inc(s_yd, 2)
            act.sem_inc(s_yn, G)

            def rows(c, gg):
                n, q = c * 4 + gg, gg % 2
                act.wait_ge(s_tx, n + 1)
                act.wait_ge(s_st, n + 1)
                nc.scalar.copy(xrb[:, q, :], ps[:, TX, :]).then_inc(s_xr, 1)
                act.wait_ge(s_rb, n + 1)
                act.wait_ge(s_yd, n + 1)
                for r in range(R):
                    e = nc.scalar.activation(att[:, q, r, :], ps[:, RB + r // 3, (r % 3) * P:(r % 3 + 1) * P],
                                             ACT.Relu, bias=g.acs[:, c, gg * R + r:gg * R + r + 1], scale=-1.0)
                e.then_inc(s_rl, 1)
                act.wait_ge(s_rl, n + 1)
                nc.scalar.activation(att[:, q], att[:, q], ACT.Exp, scale=-1.0).then_inc(s_e, 1)

            def squares(c, gg):
                n = c * 4 + gg
                act.wait_ge(s_yz, n + 1)
                if not (isinstance(c, int) and n == 0):
                    act.wait_ge(s_ss, n)
                nc.scalar.activation(junk[:], yz[:, gg, :], ACT.Square, scale=XW ** -0.5,
                                     accum_out=ss[:, gg:gg + 1]).then_inc(s_ss, 1)

            def scale(c, gg):
                n, q = c * 4 + gg, gg % 2
                act.wait_ge(s_rs, n + 1)
                if not (isinstance(c, int) and c == 0 and gg < 2):
                    act.wait_ge(s_yt, n - 1)
                nc.scalar.activation(yn[:, q, :], yz[:, gg, :], ACT.Copy, scale=rs[:, gg:gg + 1]).then_inc(s_yn, 1)

            def write(c, gg):
                n = c * 4 + gg
                act.wait_ge(s_yt, n + 1)
                for j in range(3):
                    f = 3 * gg + j
                    a = nc.scalar.activation(g.yT[:, f, bass.ds(c * P, P)], ps[:, YT, j * P:(j + 1) * P],
                                             ACT.Copy, scale=g.vecb[:, gain + f:gain + f + 1])
                a.then_inc(s_ye, 1)

            def body(c, first, last):
                for gg in range(G):
                    rows(c, gg)
                    before(c, gg, 3, first, scale)
                    before(c, gg, 2, first, squares)
                    before(c, gg, 4, first, write)

            chunks(act, body)
            for m in range(4):
                after(3, m, scale)
                after(2, m, squares)
                after(4, m, write)
            act.wait_ge(s_ht, 1)
            nc.scalar.copy(ho.rearrange("p f n -> p (f n)"),
                           ps[:, 0:3, :].rearrange("p b t -> p (b t)")).then_inc(s_ho, 1)

        @block.vector
        def _(dve):
            nc.vector.memset(h[:], 0.0).then_inc(s_h, G)
            dve.sem_inc(s_y1, 2)

            def hd(ap):
                return ap.rearrange("p (r d) -> p r d", d=HD)

            def front(c, gg):
                n, q = c * 4 + gg, gg % 2
                dve.wait_ge(s_yo, n + 1)
                nc.vector.tensor_tensor(cbm[:, q, :], ps[:, YO + q, XW:XW + P], g.tri[:], ALU.mult).then_inc(s_cbm, 1)
                if not (isinstance(c, int) and c == 0 and gg < 2):
                    dve.wait_ge(s_yz, n - 1)
                nc.vector.tensor_tensor(hd(y[:, q, :]), hd(ps[:, YO + q, 0:XW]),
                                        last(g.eacs[:, c, gg * R:(gg + 1) * R], HD), ALU.mult).then_inc(s_y1, 1)
                dve.wait_ge(s_xr, n + 1)
                dve.wait_ge(s_yd, n + 1)
                nc.vector.tensor_tensor(hd(xdt[:, q, :]), hd(xrb[:, q, 0:XW]),
                                        last(g.dt[:, c, gg * R:(gg + 1) * R], HD), ALU.mult)
                nc.vector.tensor_tensor(hd(xsk[:, q, :]), hd(xrb[:, q, 0:XW]),
                                        last(g.dskip[:, gg * R:(gg + 1) * R], HD), ALU.mult)
                dve.wait_ge(s_e, n + 1)
                dve.wait_ge(s_cbm, n + 1)
                nc.vector.tensor_tensor(att[:, q], att[:, q], mid(cbm[:, q, :], R), ALU.mult).then_inc(s_att, 1)

            def back(c, gg):
                n, q = c * 4 + gg, gg % 2
                dve.wait_ge(s_yd, n + 3)
                dve.wait_ge(s_y1, n + 3)
                nc.vector.tensor_tensor(y[:, q, :], y[:, q, :], ps[:, YD, 0:XW], ALU.add).then_inc(s_y2, 1)
                dve.wait_ge(s_st, n + 3)
                dve.wait_ge(s_hd, n + 1)
                nc.vector.tensor_tensor(h[:, gg, :], h[:, gg, :], ps[:, ST, 0:XW], ALU.add).then_inc(s_h, 1)

            def body(c, first, last):
                for gg in range(G):
                    front(c, gg)
                    if gg:
                        back(c, gg - 1)
                    elif not first:
                        back(c - 1, G - 1)

            chunks(dve, body)
            back(NC - 1, G - 1)

        @block.gpsimd
        def _(pool):
            def hd(ap):
                return ap.rearrange("p (r d) -> p r d", d=HD)

            def keep_dta(c, half):
                nc.gpsimd.tensor_copy(dtc[:, half, :], g.dta[:, c, :]).then_inc(s_dtc, 1)

            def front(c, gg):
                n, q = c * 4 + gg, gg % 2
                pool.wait_ge(s_xr, n + 1)
                pool.wait_ge(s_st, n + 1)
                nc.gpsimd.tensor_tensor(hd(xdd[:, q, :]), hd(xrb[:, q, 0:XW]),
                                        last(g.dte[:, c, gg * R:(gg + 1) * R], HD), ALU.mult).then_inc(s_xdd, 1)
                pool.wait_ge(s_yo, n + 1)
                pool.wait_ge(s_h, n + 1)
                nc.gpsimd.tensor_tensor(hd(h[:, gg, :]), hd(h[:, gg, :]),
                                        last(g.etot[:, c, gg * R:(gg + 1) * R], HD), ALU.mult).then_inc(s_hd, 1)

            def gated(c, gg):
                n, q = c * 4 + gg, gg % 2
                pool.wait_ge(s_y2, n + 1)
                pool.wait_ge(s_yn, n + 1)
                nc.gpsimd.tensor_tensor(yz[:, gg, :], y[:, q, :], xsk[:, q, :], ALU.add).then_inc(s_y3, 1)
                pool.wait_ge(s_y3, n + 1)
                pool.wait_ge(s_zin[gg], c * 16 + 16)
                nc.gpsimd.tensor_tensor(yz[:, gg, :], yz[:, gg, :], zin[:, gg, :], ALU.mult).then_inc(s_yz, 1)

            def rstd(c, gg):
                n = c * 4 + gg
                pool.wait_ge(s_ss, n + 1)
                nc.gpsimd.tensor_tensor(ss[:, gg:gg + 1], ss[:, gg:gg + 1], g.eps[:, 0:1], ALU.add).then_inc(s_ms, 1)
                pool.wait_ge(s_ms, n + 1)
                nc.gpsimd.tensor_tensor(rs[:, gg:gg + 1], ss[:, gg:gg + 1], g.mhalf[:, 0:1], ALU.pow).then_inc(s_rs, 1)

            def body(c, first, last):
                for gg in range(G):
                    if gg == 0 and not first:
                        pool.wait_ge(s_rb, c * 4)
                        keep_dta(c, 1)
                    front(c, gg)
                    before(c, gg, 3, first, rstd)
                    before(c, gg, 1, first, gated)
                    if gg == 2 and not last:
                        pool.wait_ge(s_rb, c * 4 + 2)
                        keep_dta(c + 1, 0)

            keep_dta(0, 0)
            keep_dta(0, 1)
            chunks(pool, body)
            for m in range(3):
                after(3, m, rstd)
                after(1, m, gated)


def stage_ssd_sample(g):
    nc, ps, c = g.nc, g.psum, NC
    XW = R * HD
    gain = VEC["ssm_norm"]
    h_in = g.d["state_ssm"][0].rearrange("b h p n -> b (h p) n")
    with ExitStack() as ctx:
        xr = g.sb("q_rows", [NS, CD - G * N], ctx=ctx)
        xdt = g.sb("q_xdt", [NS, DI], ctx=ctx)
        xdd = g.sb("q_xdd", [NS, DI], ctx=ctx)
        xsk = g.sb("q_xskip", [NS, DI], ctx=ctx)
        zin = xr[:, 0:DI]
        bm = g.big[0:NS, 0:NB * G * N].rearrange("p (b n) -> p b n", b=NB)
        H0 = NB * G * N
        RING = 4
        h0 = g.big[:, H0:H0 + RING * DI].rearrange("p (s f n) -> p s f n", s=RING, n=N)
        hnew = g.big[:, H0 + RING * DI:H0 + (RING + 2) * DI].rearrange("p (s f n) -> p s f n", s=2, n=N)
        hT = g.big[:, H0 + (RING + 2) * DI:H0 + (RING + 3) * DI].rearrange("p (f w) -> p f w", f=2)
        HF, HG = XF // 2, G // 2
        TB, YO, ST = (0, 2), 4, 6
        cm = g.sb("q_c_masked", [P, 2, G, NS], ctx=ctx)
        cbm = g.sb("q_cb", [NS, G, NS], ctx=ctx)
        att = g.sb("q_att", [NS, H, NS], ctx=ctx)
        et = g.sb("q_etot", [P, XF, NB], ctx=ctx)
        y = g.sb("q_y", [NS, DI], ctx=ctx)
        yd = g.sb("q_ydiag", [NS, DI], ctx=ctx)
        ss = g.sb("q_ss", [NS, G], ctx=ctx)
        s_z = g.sem("q_z_loaded")
        s_bm = g.sem("q_b_masked")
        s_h0 = [g.sem(f"q_h0_loaded{i}") for i in range(RING)]
        s_ho = [g.sem(f"q_h_stored{i}") for i in range(2)]
        s_p = g.sem("q_products")
        s_a = g.sem("q_act")
        s_v = g.sem("q_vector")
        s_g = g.sem("q_pool")
        s_ht = g.sem("q_h_turned")
        s_hc = g.sem("q_hT_ready")
        s_dx = g.sem("q_dta_spread")
        s_cm = g.sem("q_c_masked_ready")
        s_yo = g.sem("q_yoff")
        s_ys = g.sem("q_yoff_added")
        s_hd = g.sem("q_h_decayed_ready")
        s_st = g.sem("q_state_product")
        s_hn = g.sem("q_h_new")
        s_yd, s_yz, s_ms, s_yn, s_tail = (g.sem("q_" + x) for x in (
            "ydiag", "y_gated", "mean", "y_normed", "y_chain"))
        block = ctx.enter_context(nc.Block("ssd_sample"))

        @block.sync
        def _(sp):
            for n in range(RING):
                sp.dma_start(h0[:, n], h_in[n].rearrange("(j p) n -> p j n", p=P)).then_inc(s_h0[n], 16)
            sp.wait_ge(s_v, 5)
            sp.wait_ge(s_g, 1)
            sp.dma_start(zin, g.z_scr[c][0:NS, :]).then_inc(s_z, 16)

            for n in range(NB):
                sp.wait_ge(s_hn, n * 2 + 2)
                sp.dma_start(g.out["ssm_s"][n].rearrange("(j p) n -> p j n", p=P), hnew[:, n % 2]).then_inc(s_ho[n % 2], 16)
                if n + RING < NB:
                    sp.dma_start(h0[:, n % RING], h_in[n + RING].rearrange("(j p) n -> p j n", p=P)
                                 ).then_inc(s_h0[n % RING], 16)
            for s in range(2):
                sp.wait_ge(s_ho[s], 16 * (NB // 2))

        @block.tensor
        def _(pe):
            for f in range(XF + G):
                nc.tensor.transpose(ps[0:NS, f // 4, (f % 4) * P:(f % 4 + 1) * P], g.xbs[:, f, :], g.ident[:])
            for gg in range(G):
                nc.tensor.matmul(ps[0:NS, 4, gg * NS:(gg + 1) * NS], g.xbs[:, XF + gg, :], g.xbs[:, XF + G + gg, :],
                                 start=True, stop=True)
            for h in range(H):
                at = h * NS
                nc.tensor.matmul(ps[0:NS, 5 + at // BANK, at % BANK:at % BANK + NS],
                                 g.dta[0:NS, c, h:h + 1].to_broadcast([NS, NS]), g.btri[:], start=True, stop=True)
            for j in range(XF):
                if j == 0:
                    pe.wait_ge(s_dx, 1)
                mm = nc.tensor.matmul(ps[:, 7, j * NB:(j + 1) * NB], y[:, j * P:(j + 1) * P], g.rowmask[:],
                                      start=True, stop=True)
            mm.then_inc(s_p, 1)
            pe.wait_ge(s_v, 5)
            pe.wait_ge(s_g, 1)
            for h in range(H):
                at = h * HD
                mm = nc.tensor.matmul(ps[0:NS, at // BANK, at % BANK:at % BANK + HD], att[:, h, :],
                                      xdt[:, at:at + HD], start=True, stop=True)
            mm.then_inc(s_p, 1)
            pe.wait_ge(s_yd, 1)

            def turn(n, f):
                if f == 0:
                    pe.wait_ge(s_h0[n % RING], 16 * (n // RING + 1))
                pe.wait_ge(s_hc, 2 * n + f + 1)
                for j in range(HF):
                    tr = nc.tensor.transpose(ps[:, TB[f] + j // 4, (j % 4) * P:(j % 4 + 1) * P],
                                             h0[:, n % RING, f * HF + j, :], g.ident[:])
                tr.then_inc(s_ht, 1)

            def products(n, f):
                m = 2 * n + f
                pe.wait_ge(s_hc, m + 3)
                if f == 0:
                    pe.wait_ge(s_cm, n + 1)
                pe.wait_ge(s_ys, m)
                for k in range(HG):
                    mm = nc.tensor.matmul(ps[0:NS, YO + k, 0:XW], cm[:, n % 2, f * HG + k, :],
                                          hT[:, f, k * XW:(k + 1) * XW], start=True, stop=True)
                mm.then_inc(s_yo, 1)
                pe.wait_ge(s_hn, m)
                for j in range(HF):
                    t = f * HF + j
                    mm = nc.tensor.matmul(ps[:, ST + j // 4, (j % 4) * P:(j % 4 + 1) * P], xdd[:, t * P:(t + 1) * P],
                                          bm[:, n, (t // 3) * N:(t // 3 + 1) * N], start=True, stop=True)
                mm.then_inc(s_st, 1)

            pe.wait_ge(s_bm, 1)
            turn(0, 0)
            for m in range(2 * NB):
                if m + 1 < 2 * NB:
                    turn((m + 1) // 2, (m + 1) % 2)
                products(m // 2, m % 2)
            pe.wait_ge(s_yn, 1)
            pe.wait_ge(s_hn, 2 * NB)
            for f in range(XF):
                tr = nc.tensor.transpose(ps[:, 0, f * NS:(f + 1) * NS], y[:, f * P:(f + 1) * P], g.ident[0:NS, 0:NS])
            tr.then_inc(s_p, 1)

        @block.scalar
        def _(act):
            act.wait_ge(s_p, 1)
            nc.scalar.copy(xr[:], ps[0:NS, 0:4, :].rearrange("p b t -> p (b t)")).then_inc(s_a, 1)
            nc.scalar.activation(et[:].rearrange("p j b -> p (j b)"), ps[:, 7, 0:XF * NB], ACT.Exp).then_inc(s_a, 1)
            act.wait_ge(s_v, 1)
            nc.scalar.activation(att[:], att[:], ACT.Exp).then_inc(s_a, 1)
            act.wait_ge(s_a, 1)
            for b in range(NB):
                a = nc.scalar.activation(bm[:, b, :], xr[:, DI:DI + G * N], ACT.Copy, scale=g.rowmask[:, b:b + 1])
            a.then_inc(s_bm, 1)
            act.wait_ge(s_p, 2)
            nc.scalar.copy(yd[:], ps[0:NS, 0:3, :].rearrange("p b t -> p (b t)")).then_inc(s_yd, 1)
            act.sem_inc(s_hc, 2)
            act.sem_inc(s_yo, 2)
            with act.Fori(0, NB) as n:
                for f in range(2):
                    m = n * 2 + f
                    act.wait_ge(s_ht, m + 1)
                    act.wait_ge(s_yo, m + 1)
                    nc.scalar.copy(hT[:, f, :], ps[:, TB[f]:TB[f] + 2, :].rearrange("p b t -> p (b t)")[:, 0:HF * P]
                                   ).then_inc(s_hc, 1)
            act.wait_ge(s_yz, 1)
            for gg in range(G):
                a = nc.scalar.activation(xdt[:, gg * XW:(gg + 1) * XW], y[:, gg * XW:(gg + 1) * XW], ACT.Square,
                                         accum_out=ss[:, gg:gg + 1])
            a.then_inc(s_a, 1)
            act.wait_ge(s_p, 3)
            for f in range(XF):
                nc.scalar.activation(g.yT[:, f, SEQ:T], ps[:, 0, f * NS:(f + 1) * NS], ACT.Copy,
                                     scale=g.vecb[:, gain + f:gain + f + 1])

        @block.gpsimd
        def _(pool):
            pool.wait_ge(s_a, 1)
            x3 = xr[:, 0:DI].rearrange("p (h d) -> p h d", d=HD)
            nc.gpsimd.tensor_tensor(xdd[:].rearrange("p (h d) -> p h d", d=HD), x3,
                                    last(g.dte[0:NS, c, :], HD), ALU.mult)
            nc.gpsimd.tensor_tensor(xsk[:].rearrange("p (h d) -> p h d", d=HD), x3,
                                    last(g.dskip[0:NS, :], HD), ALU.mult).then_inc(s_g, 1)
            pool.wait_ge(s_a, 2)
            for n in range(NB):
                pool.wait_ge(s_yo, n * 2)
                nc.gpsimd.tensor_tensor(cm[:, n % 2], g.xbs[:, XF + G:CF, :], mid(g.colmask[:, n, :], G),
                                        ALU.mult).then_inc(s_cm, 1)
                pool.wait_ge(s_h0[n % RING], 16 * (n // RING + 1))
                for f in range(2):
                    pool.wait_ge(s_ht, n * 2 + f + 1)
                    o = h0[:, n % RING, f * HF:(f + 1) * HF]
                    nc.gpsimd.tensor_tensor(o, o, last(et[:, f * HF:(f + 1) * HF, n], N), ALU.mult).then_inc(s_hd, 1)
            pool.wait_ge(s_ms, 1)
            nc.gpsimd.tensor_tensor(ss[:], ss[:], g.mhalf[0:NS, 0:G], ALU.pow).then_inc(s_g, 1)

        @block.vector
        def _(dve):
            nc.vector.tensor_copy(y[:].rearrange("p (h d) -> p h d", d=HD),
                                  last(g.dta[0:NS, c, :], HD)).then_inc(s_dx, 1)
            dve.wait_ge(s_p, 1)
            for h0_, n_, b_ in ((0, 16, 5), (16, 8, 6)):
                op = nc.vector.tensor_tensor(att[:, h0_:h0_ + n_, :],
                                             ps[0:NS, b_, 0:n_ * NS].rearrange("p (h t) -> p h t", t=NS),
                                             last(g.acs[0:NS, c, h0_:h0_ + n_], NS), ALU.subtract)
            ch = Chain(dve, s_dx, 1)
            ch.done(op)
            ch = Chain(dve, s_v)
            ch.done(nc.vector.tensor_scalar(att[:], att[:], 0.0, None, ALU.min))
            ch.done(nc.vector.tensor_tensor(cbm[:], ps[0:NS, 4, 0:G * NS].rearrange("p (g t) -> p g t", t=NS),
                                            mid(g.btri[:], G), ALU.mult))
            dve.wait_ge(s_a, 3)
            for gg in range(G):
                a = att[:, gg * R:(gg + 1) * R, :]
                op = nc.vector.tensor_tensor(a, a, mid(cbm[:, gg, :], R), ALU.mult)
            ch.done(op)
            ch.done(nc.vector.tensor_tensor(xdt[:].rearrange("p (h d) -> p h d", d=HD),
                                            xr[:, 0:DI].rearrange("p (h d) -> p h d", d=HD),
                                            last(g.dt[0:NS, c, :], HD), ALU.mult))
            ch.done(nc.vector.memset(y[:], 0.0))
            for n in range(NB):
                for f in range(2):
                    m = n * 2 + f
                    dve.wait_ge(s_yo, m + 3)
                    dve.wait_ge(s_ys, m)
                    yv = y[:, f * HG * XW:(f + 1) * HG * XW].rearrange("p (g w) -> p g w", w=XW)
                    nc.vector.tensor_tensor(yv, yv, ps[0:NS, YO:YO + HG, 0:XW], ALU.add).then_inc(s_ys, 1)
                    dve.wait_ge(s_st, m + 1)
                    dve.wait_ge(s_hd, m + 1)
                    if f == 0 and n >= 2:
                        dve.wait_ge(s_ho[n % 2], 16 * (n // 2))
                    nc.vector.tensor_tensor(hnew[:, n % 2, f * HF:(f + 1) * HF].rearrange("p j n -> p (j n)"),
                                            h0[:, n % RING, f * HF:(f + 1) * HF].rearrange("p j n -> p (j n)"),
                                            ps[:, ST:ST + 2, :].rearrange("p b t -> p (b t)")[:, 0:HF * P],
                                            ALU.add).then_inc(s_hn, 1)
            dve.wait_ge(s_ys, 2 * NB)
            dve.wait_ge(s_yd, 1)
            dve.wait_ge(s_g, 1)
            dve.wait_ge(s_z, 16)
            y3 = y[:].rearrange("p (h d) -> p h d", d=HD)
            tc = Chain(dve, s_tail)
            tc.done(nc.vector.tensor_tensor(y3, y3, last(g.eacs[0:NS, c, :], HD), ALU.mult))
            tc.done(nc.vector.tensor_tensor(y[:], y[:], yd[:], ALU.add))
            tc.done(nc.vector.tensor_tensor(y[:], y[:], xsk[:], ALU.add))
            nc.vector.tensor_tensor(y[:], y[:], zin, ALU.mult).then_inc(s_yz, 1)
            dve.wait_ge(s_a, 4)
            nc.vector.tensor_scalar(ss[:], ss[:], 1.0 / XW, EPS, ALU.mult, ALU.add).then_inc(s_ms, 1)
            dve.wait_ge(s_g, 2)
            nc.vector.tensor_tensor(y[:].rearrange("p (g w) -> p g w", w=XW), y[:].rearrange("p (g w) -> p g w", w=XW),
                                    last(ss[:], XW), ALU.mult).then_inc(s_yn, 1)



def stage_merge(g):
    nc, ps, d = g.nc, g.psum, g.d
    yh, yl = g.y_parts
    uh, ul = g.u_parts
    KT = XF + GMF
    wa = d["w_a_proj"][0].rearrange("(k p) n -> p k n", p=P)
    wb = d["w_b_proj"][0].rearrange("(k p) n -> p k n", p=P)
    KS = (slice(0, XF), slice(XF, KT))
    with ExitStack() as ctx:
        w = g.sb("m_w", [P, KT, P], ctx=ctx)
        wh = g.sb("m_w_high", [P, KT, P], F32R, ctx=ctx)
        wl = g.sb("m_w_low", [P, KT, P], F32R, ctx=ctx)
        gt = g.sb("m_gates", [P, 2, T], ctx=ctx)
        mo = g.sb("m_out", [P, 2, T], ctx=ctx)
        s_w = [g.sem(f"m_w_loaded{i}") for i in range(2)]
        s_gt = g.sem("m_gates_loaded")
        s_sh, s_sl = g.sem("m_act_high"), g.sem("m_act_low")
        s_wh, s_wl = g.sem("m_w_high_ready"), g.sem("m_w_low_ready")
        s_mm = g.sem("m_product")
        s_pr = g.sem("m_gated")
        s_ad = g.sem("m_added")
        s_st = [g.sem(f"m_stored{i}") for i in range(2)]
        block = ctx.enter_context(nc.Block("merge"))

        def slabs(ap):
            return ap.rearrange("p (n t) -> p n t", t=SLAB)

        @block.sync
        def _(sp):
            def weights(f, q):
                sp.wait_ge(s_wl, f * 2 + q + 1)
                sp.dma_start(w[:, KS[q]], (wa, wb)[q][:, :, bass.ds(f * P, P)]).then_inc(s_w[q], 16)

            with sp.Fori(0, DK // 2) as i:
                for s in range(2):
                    f = i * 2 + s
                    for q in range(2):
                        weights(f, q)
                    sp.wait_ge(s_ad, f)
                    for q in range(2):
                        sp.dma_start(gt[:, q, :], g.gate_scr[f + q * DK]).then_inc(s_gt, 16)
            for s in range(2):
                sp.wait_ge(s_st[s], 16 * (DK // 2))

        @block.tensor
        def _(pe):
            def product(m, q, acts):
                ah, al = ((yh, yl), (uh, ul))[q]
                pe.wait_ge(s_wl, m + 3)
                pe.wait_ge(s_pr, m + 1)
                kt = GMF if q else XF
                for n in range(3):
                    x = slice(n * SLAB, (n + 1) * SLAB)
                    for k in range(kt):
                        if n == 0:
                            acts(k)
                        j = (XF if q else 0) + k
                        mm = matmul3(nc, ps[:, 3 * q + n, 0:SLAB], wh[:, j, :], wl[:, j, :], ah[:, k, x], al[:, k, x],
                                     k == 0, k == kt - 1)
                mm.then_inc(s_mm, 1)

            product(0, 0, lambda k: pe.wait_ge(s_sl, k + 1))
            product(1, 1, lambda k: pe.wait_ge(s_sl, XF + k + 1))
            with pe.Fori(1, DK) as f:
                product(f * 2, 0, lambda k: None)
                product(f * 2 + 1, 1, lambda k: None)

        @block.scalar
        def _(act):
            def w_high(f, q):
                act.wait_ge(s_w[q], f * 16 + 16)
                act.wait_ge(s_mm, f * 2 + q + 1)
                nc.scalar.activation(wh[:, KS[q]], w[:, KS[q]], ACT.Copy).then_inc(s_wh, 1)

            act.sem_inc(s_mm, 2)
            for q in range(2):
                w_high(0, q)
            for t in range(KT):
                src, dst = (g.yT[:, t], yh[:, t]) if t < XF else (g.uT[:, t - XF], uh[:, t - XF])
                nc.scalar.activation(dst, src, ACT.Copy).then_inc(s_sh, 1)

            def tile(i, s, more):
                f = i * 2 + s
                if more:
                    for q in range(2):
                        w_high(f + 1, q)
                act.wait_ge(s_ad, f + 1)
                act.dma_start(g.merged_scr[f], mo[:, s, :]).then_inc(s_st[s], 16)

            with act.Fori(0, DK // 2 - 1) as i:
                for s in range(2):
                    tile(i, s, True)
            tile(DK // 2 - 1, 0, True)
            tile(DK // 2 - 1, 1, False)

        @block.vector
        def _(dve):
            def w_low(f, q):
                dve.wait_ge(s_wh, f * 2 + q + 1)
                nc.vector.tensor_tensor(wl[:, KS[q]], w[:, KS[q]], wh[:, KS[q]].bitcast(F32),
                                        ALU.subtract).then_inc(s_wl, 1)

            def gated(f, q):
                dve.wait_ge(s_mm, f * 2 + q + 3)
                dve.wait_ge(s_gt, f * 32 + 32)
                nc.vector.tensor_tensor(slabs(gt[:, q, :]), slabs(gt[:, q, :]), ps[:, 3 * q:3 * q + 3, 0:SLAB],
                                        ALU.mult).then_inc(s_pr, 1)

            dve.sem_inc(s_wl, 2)
            dve.sem_inc(s_pr, 2)
            for q in range(2):
                w_low(0, q)
            for t in range(KT):
                dve.wait_ge(s_sh, t + 1)
                if t < XF:
                    src, high, low = g.yT[:, t], yh[:, t], yl[:, t]
                else:
                    src, high, low = g.uT[:, t - XF], uh[:, t - XF], ul[:, t - XF]
                nc.vector.tensor_tensor(low, src, high.bitcast(F32), ALU.subtract).then_inc(s_sl, 1)
            with dve.Fori(0, DK - 1) as f:
                for q in range(2):
                    gated(f, q)
                    w_low(f + 1, q)
            for q in range(2):
                gated(DK - 1, q)

        @block.gpsimd
        def _(pool):
            with pool.Fori(0, DK // 2) as i:
                for s in range(2):
                    f = i * 2 + s
                    pool.wait_ge(s_pr, f * 2 + 4)
                    pool.wait_ge(s_st[s], i * 16)
                    nc.gpsimd.tensor_tensor(mo[:, s, :], gt[:, 0, :], gt[:, 1, :], ALU.add).then_inc(s_ad, 1)


def stage_add_rows(g, tag, act_T, w_dram, x, x_dram=None, act_dram=None):
    nc, ps = g.nc, g.psum
    wv = w_dram.rearrange("(k p) n -> p k n", p=P)
    PW = 4
    AP_ = 3
    TPP = NT // AP_
    with ExitStack() as ctx:
        w = g.sb("a_w", [P, 2, DK, BANK], ctx=ctx)
        wh = g.sb("a_w_high", [P, DK, BANK], F32R, ctx=ctx)
        wl = g.sb("a_w_low", [P, DK, BANK], F32R, ctx=ctx)
        ah = g.sb("a_act_high", [P, DK, TP], F32R, ctx=ctx)
        al = g.R1_low
        s_w = [g.sem(f"{tag}_w_loaded{i}") for i in range(2)]
        s_x = g.sem(tag + "_x_loaded")
        s_a = [g.sem(f"{tag}_act_loaded{i}") for i in range(AP_)]
        s_z, s_az = g.sem(tag + "_x_padded"), g.sem(tag + "_act_padded")
        s_mm = g.sem(tag + "_product")
        s_ad = g.sem(tag + "_added")
        s_ah, s_al = g.sem(tag + "_act_high"), g.sem(tag + "_act_low")
        s_wh, s_wl, s_wf = (g.sem(tag + n) for n in ("_w_high", "_w_low", "_w_parts_used"))
        block = ctx.enter_context(nc.Block(tag))

        def tile(t, c):
            return t[:, :, c * P:(c + 1) * P]

        def piece(t, p):
            return t[:, 2 * p:2 * p + 2, :].rearrange("p k n -> p (k n)")

        @block.sync
        def _(sp):
            sp.dma_start(w[:, 0], wv[:, :, 0:BANK]).then_inc(s_w[0], 16)
            if act_dram is not None:
                for i in range(AP_):
                    lo, hi = i * TPP * P, min((i + 1) * TPP * P, T)
                    sp.dma_start(act_T[:, :, lo:hi], act_dram[:, :, lo:hi].rearrange("k p t -> p k t")).then_inc(s_a[i], 16)
            sp.dma_start(w[:, 1], wv[:, :, BANK:2 * BANK]).then_inc(s_w[1], 16)
            for i, (dst, src) in enumerate(x_dram or ()):
                if i:
                    sp.wait_ge(s_z, 1)
                sp.dma_start(dst, src).then_inc(s_x, 16)

        @block.gpsimd
        def _(pool):
            if x_dram:
                nc.gpsimd.memset(x[:, NT - 1, :], 0.0).then_inc(s_z, 1)
            if act_dram is not None:
                nc.gpsimd.memset(act_T[:, :, T:TP], 0.0).then_inc(s_az, 1)

        @block.tensor
        def _(pe):
            for j in range(2):
                for c in range(NT):
                    n = j * NT + c
                    if j == 0:
                        pe.wait_ge(s_al, c + 1)
                    if n >= 4:
                        pe.wait_ge(s_ad, n - 3)
                    for k in range(DK):
                        if c == 0 and k % 2 == 0:
                            pe.wait_ge(s_wl, PW * j + k // 2 + 1)
                        mm = matmul3(nc, ps[:, n % 4, :], tile(ah, c)[:, k, :], tile(al, c)[:, k, :], wh[:, k, :],
                                     wl[:, k, :], k == 0, k == DK - 1)
                        if j == 0 and c == NT - 1 and k % 2 and k < DK - 1:
                            mm.then_inc(s_wf, 1)
                    mm.then_inc(s_mm, 1)

        @block.scalar
        def _(act):
            def w_high(j):
                act.wait_ge(s_w[j], 16)
                for p in range(PW):
                    if j and p < PW - 1:
                        act.wait_ge(s_wf, p + 1)
                    elif j:
                        act.wait_ge(s_mm, NT)
                    nc.scalar.activation(piece(wh, p), piece(w[:, j], p), ACT.Copy).then_inc(s_wh, 1)

            def high(c):
                if act_dram is not None and c % TPP == 0:
                    act.wait_ge(s_a[c // TPP], 16)
                if act_dram is not None and c == NT - 1:
                    act.wait_ge(s_az, 1)
                nc.scalar.activation(tile(ah, c), tile(act_T, c), ACT.Copy).then_inc(s_ah, 1)

            w_high(0)
            for c in range(NT):
                high(c)
            w_high(1)

        @block.vector
        def _(dve):
            def w_low(j):
                for p in range(PW):
                    dve.wait_ge(s_wh, j * PW + p + 1)
                    nc.vector.tensor_tensor(piece(wl, p), piece(w[:, j], p), piece(wh, p).bitcast(F32),
                                            ALU.subtract).then_inc(s_wl, 1)

            def low(c):
                dve.wait_ge(s_ah, c + 1)
                nc.vector.tensor_tensor(tile(al, c), tile(act_T, c), tile(ah, c).bitcast(F32), ALU.subtract).then_inc(s_al, 1)

            w_low(0)
            for c in range(NT):
                low(c)
            if x_dram:
                dve.wait_ge(s_x, 16 * len(x_dram))
            for j in range(2):
                for c in range(NT):
                    n = j * NT + c
                    if n == NT - 1:
                        w_low(1)
                    dve.wait_ge(s_mm, n + 1)
                    o = x[:, c, j * BANK:(j + 1) * BANK]
                    nc.vector.tensor_tensor(o, o, ps[:, n % 4, :], ALU.add).then_inc(s_ad, 1)


def stage_mem_kv(g, mT, kT, vr):
    nc, ps, d = g.nc, g.psum, g.d
    wk = d["w_mem_k"][0].rearrange("(k p) n -> p k n", p=P)
    wv = d["w_mem_v"][0].rearrange("(k p) n -> p k n", p=P)
    with ExitStack() as ctx:
        w = g.sb("k_w", [P, 2, DK, BANK], ctx=ctx)
        kr = g.sb("k_rows", [P, MT, D], ctx=ctx)
        s_w = [g.sem(f"k_w_loaded{i}") for i in range(2)]
        s_mm, s_ev = g.sem("k_product"), g.sem("k_rows_ready")
        s_tr, s_te = g.sem("k_turned"), g.sem("k_turned_read")
        block = ctx.enter_context(nc.Block("mem_kv"))

        @block.sync
        def _(sp):
            for j in range(4):
                if j >= 2:
                    sp.wait_ge(s_mm, MT * (j - 1))
                src = (wk, wv)[j // 2][:, :, (j % 2) * BANK:(j % 2 + 1) * BANK]
                sp.dma_start(w[:, j % 2], src).then_inc(s_w[j % 2], 16)
            sp.wait_ge(s_ev, 8)
            sp.dma_start(g.out["mk"].rearrange("(t p) n -> p t n", p=P), kr[:]).then_inc(g.s_out, g.stored())
            sp.dma_start(g.out["mv"].rearrange("(t p) n -> p t n", p=P), vr[:]).then_inc(g.s_out, g.stored())
            sp.wait_ge(g.s_out, 16 * g.n_out)

        @block.tensor
        def _(pe):
            for j in range(4):
                pe.wait_ge(s_w[j % 2], 16 * (j // 2 + 1))
                for t in range(MT):
                    n = j * MT + t
                    if n >= 4:
                        pe.wait_ge(s_ev, n - 3)
                    for k in range(DK):
                        mm = nc.tensor.matmul(ps[:, n % 4, :], mT[:, k, t * P:(t + 1) * P], w[:, j % 2, k, :],
                                              start=(k == 0), stop=(k == DK - 1))
                    mm.then_inc(s_mm, 1)
            pe.wait_ge(s_ev, 4)
            for k in range(DK):
                for t in range(MT):
                    tr = nc.tensor.transpose(ps[:, 4 + k // 2, (k % 2) * ML + t * P:(k % 2) * ML + (t + 1) * P],
                                             kr[:, t, k * P:(k + 1) * P], g.ident[:])
            tr.then_inc(s_tr, 1)

        @block.scalar
        def _(act):
            for j in range(4):
                for t in range(MT):
                    n = j * MT + t
                    act.wait_ge(s_mm, n + 1)
                    dst = (kr, vr)[j // 2][:, t, (j % 2) * BANK:(j % 2 + 1) * BANK]
                    nc.scalar.copy(dst, ps[:, n % 4, :]).then_inc(s_ev, 1)

        @block.vector
        def _(dve):
            dve.wait_ge(s_tr, 1)
            nc.vector.tensor_copy(kT[:].rearrange("p k m -> p (k m)"),
                                  ps[:, 4:8, :].rearrange("p b t -> p (b t)")).then_inc(s_te, 1)


def stage_query(g, hT, qT):
    nc, ps = g.nc, g.psum
    wq = g.d["w_mem_q"][0].rearrange("(k p) n -> p k n", p=P)
    with ExitStack() as ctx:
        w = g.sb("u_w", [P, 2, DK, P], ctx=ctx)
        wh = g.sb("u_w_high", [P, 2, DK, P], F32R, ctx=ctx)
        wl = g.sb("u_w_low", [P, 2, DK, P], F32R, ctx=ctx)
        hh = g.sb("u_act_high", [P, DK, T], F32R, ctx=ctx)
        hl = g.R1_low
        s_w = [g.sem(f"u_w_loaded{i}") for i in range(2)]
        s_hh, s_hl, s_wh, s_wl = (g.sem("u_" + n) for n in ("act_high", "act_low", "w_high", "w_low"))
        s_mm, s_pf = g.sem("u_product"), g.sem("u_read")
        block = ctx.enter_context(nc.Block("query"))

        def slab(n):
            return slice(n * SLAB, (n + 1) * SLAB)

        @block.sync
        def _(sp):
            with sp.Fori(0, DK // 2) as i:
                for q in range(2):
                    sp.wait_ge(s_wl, i * 2 + q + 1)
                    sp.dma_start(w[:, q], wq[:, :, bass.ds(i * 2 * P + q * P, P)]).then_inc(s_w[q], 16)

        @block.tensor
        def _(pe):
            def tile(f, q, first):
                pe.wait_ge(s_wl, f + 3)
                pe.wait_ge(s_pf, f + 1)
                for n in range(3):
                    for k in range(DK):
                        if first and k % 4 == 0:
                            pe.wait_ge(s_hl, 2 * n + k // 4 + 1)
                        mm = matmul3(nc, ps[:, 3 * q + n, 0:SLAB], wh[:, q, k, :], wl[:, q, k, :],
                                     hh[:, k, slab(n)], hl[:, k, slab(n)], k == 0, k == DK - 1)
                mm.then_inc(s_mm, 1)

            tile(0, 0, True)
            tile(1, 1, False)
            with pe.Fori(1, DK // 2) as i:
                for q in range(2):
                    tile(i * 2 + q, q, False)

        @block.scalar
        def _(act):
            act.sem_inc(s_pf, 2)

            def w_high(i, q):
                act.wait_ge(s_w[q], i * 16 + 16)
                nc.scalar.activation(wh[:, q], w[:, q], ACT.Copy).then_inc(s_wh, 1)

            def write(i, q):
                act.wait_ge(s_mm, i * 2 + q + 1)
                nc.scalar.activation(qT[:, i * 2 + q, 0:T].rearrange("p (n t) -> p n t", t=SLAB),
                                     ps[:, 3 * q:3 * q + 3, 0:SLAB], ACT.Copy).then_inc(s_pf, 1)

            for n in range(3):
                for k in (0, 4):
                    if n == 0 and k == 4:
                        w_high(0, 0)
                    nc.scalar.activation(hh[:, k:k + 4, slab(n)], hT[:, k:k + 4, slab(n)], ACT.Copy).then_inc(s_hh, 1)
            w_high(0, 1)
            with act.Fori(0, DK // 2 - 1) as i:
                for q in range(2):
                    write(i, q)
                    w_high(i + 1, q)
            for q in range(2):
                write(DK // 2 - 1, q)

        @block.vector
        def _(dve):
            dve.sem_inc(s_wl, 2)

            def w_low(f, q):
                dve.wait_ge(s_wh, f + 1)
                nc.vector.tensor_tensor(wl[:, q], w[:, q], wh[:, q].bitcast(F32), ALU.subtract).then_inc(s_wl, 1)

            for n in range(3):
                for k in (0, 4):
                    if n == 0 and k == 4:
                        w_low(0, 0)
                    dve.wait_ge(s_hh, 2 * n + k // 4 + 1)
                    nc.vector.tensor_tensor(hl[:, k:k + 4, slab(n)], hT[:, k:k + 4, slab(n)],
                                            hh[:, k:k + 4, slab(n)].bitcast(F32), ALU.subtract).then_inc(s_hl, 1)
            w_low(1, 1)
            with dve.Fori(1, DK // 2) as i:
                for q in range(2):
                    w_low(i * 2 + q, q)


def stage_attention(g, qT, kT, vr, oT):
    nc, ps = g.nc, g.psum
    S, PT, O = 0, 2, 4
    with ExitStack() as ctx:
        qs = g.sb("b_q", [P, MH, 2, P], ctx=ctx)
        pr = g.sb("b_p", [P, 2, ML], ctx=ctx)
        pT = g.sb("b_pT", [P, 2, ML], ctx=ctx)
        mx = g.sb("b_max", [P, 2], ctx=ctx)
        nb = g.sb("b_nbias", [P, 2], ctx=ctx)
        sm = g.sb("b_sum", [P, 2], ctx=ctx)
        ri = g.sb("b_rsum", [P, 2], ctx=ctx)
        s_q, s_s, s_mx, s_nb, s_e, s_ri, s_pn, s_pt, s_pc, s_o, s_oc = (g.sem("b_" + x) for x in (
            "q_kept", "scores", "max", "nbias", "exp", "rsum", "p_normed", "p_turned", "pT_ready",
            "values", "o_written"))
        zr = g.sb("b_zero", [P, D], ctx=ctx)
        s_zr, s_zf = g.sem("b_zero_ready"), g.sem("b_blocks_zeroed")
        block = ctx.enter_context(nc.Block("attention"))
        first = 2 * T // P

        @block.sync
        def _(sp):
            sp.wait_ge(s_zr, 1)
            sp.dma_start(g.moe_scr[first * P:NSLOT, :].rearrange("(b p) n -> p b n", p=P),
                         mid(zr[:], NBLK - first)).then_inc(s_zf, 16)
            sp.wait_ge(s_zf, 16)

        def chunks(eng, body):
            body(0, True, False)
            with eng.Fori(1, NC - 1) as c:
                body(c, False, False)
            body(NC - 1, False, True)

        @block.gpsimd
        def _(pool):
            nc.gpsimd.memset(zr[:], 0.0).then_inc(s_zr, 1)
            with pool.Fori(0, NC) as c:
                for h in range(MH):
                    pool.wait_ge(s_s, c * 4 + h + 1)
                    nc.gpsimd.tensor_copy(qs[:, h], qT[:, 2 * h:2 * h + 2, bass.ds(c * P, P)]).then_inc(s_q, 1)

        @block.tensor
        def _(pe):
            pe.sem_inc(s_s, MH)

            def scores(c, h):
                n, q = c * 4 + h, h % 2
                pe.wait_ge(s_q, n + 1)
                pe.wait_ge(s_e, n + 1)
                for k in range(2):
                    mm = nc.tensor.matmul(ps[:, S + q, 0:ML], qs[:, h, k, :], kT[:, 2 * h + k, :],
                                          start=(k == 0), stop=(k == 1))
                mm.then_inc(s_s, 1)

            def turn(c, h):
                n, q = c * 4 + h, h % 2
                pe.wait_ge(s_pn, n + 1)
                pe.wait_ge(s_pc, n + 1)
                for t in range(MT):
                    tr = nc.tensor.transpose(ps[:, PT + q, t * P:(t + 1) * P], pr[:, q, t * P:(t + 1) * P], g.ident[:])
                tr.then_inc(s_pt, 1)

            def values(c, h):
                n, q = c * 4 + h, h % 2
                pe.wait_ge(s_pc, n + 3)
                pe.wait_ge(s_oc, n + 1)
                for k in range(2):
                    for t in range(MT):
                        mm = nc.tensor.matmul(ps[:, O + q, k * P:(k + 1) * P],
                                              vr[:, t, (2 * h + k) * P:(2 * h + k + 1) * P],
                                              pT[:, q, t * P:(t + 1) * P], start=(t == 0), stop=(t == MT - 1))
                mm.then_inc(s_o, 1)

            def body(c, first, last_):
                for h in range(MH):
                    if h < MH - 1:
                        scores(c, h + 1)
                    elif not last_:
                        scores(c + 1, 0)
                    turn(c, h)
                    if h:
                        values(c, h - 1)
                    elif not first:
                        values(c - 1, MH - 1)

            scores(0, 0)
            chunks(pe, body)
            values(NC - 1, MH - 1)

        @block.scalar
        def _(act):
            act.sem_inc(s_e, 2)
            act.sem_inc(s_oc, 2)

            def exp(c, h):
                n, q = c * 4 + h, h % 2
                act.wait_ge(s_nb, n + 1)
                act.wait_ge(s_pt, n + 1)
                nc.scalar.activation(pr[:, q, :], ps[:, S + q, 0:ML], ACT.Exp, bias=nb[:, q:q + 1], scale=SCALE,
                                     accum_out=sm[:, q:q + 1]).then_inc(s_e, 1)

            def write(c, h):
                n, q = c * 4 + h, h % 2
                act.wait_ge(s_o, n + 1)
                nc.scalar.copy(oT[:, 2 * h:2 * h + 2, bass.ds(c * P, P)],
                               ps[:, O + q, 0:2 * P].rearrange("p (k t) -> p k t", t=P)).then_inc(s_oc, 1)

            def body(c, first, last_):
                for h in range(MH):
                    exp(c, h)
                    if h >= 2:
                        write(c, h - 2)
                    elif not first:
                        write(c - 1, h + 2)

            chunks(act, body)
            write(NC - 1, MH - 2)
            write(NC - 1, MH - 1)

        @block.vector
        def _(dve):
            dve.sem_inc(s_pt, 2)
            dve.sem_inc(s_pc, 2)

            def front(c, h):
                n, q = c * 4 + h, h % 2
                dve.wait_ge(s_s, n + 1 + MH)
                nc.vector.reduce_max(mx[:, q:q + 1], ps[:, S + q, 0:ML], AX).then_inc(s_mx, 1)
                dve.wait_ge(s_mx, n + 1)
                nc.vector.tensor_scalar(nb[:, q:q + 1], mx[:, q:q + 1], -SCALE, None, ALU.mult).then_inc(s_nb, 1)

            def mid_(c, h):
                n, q = c * 4 + h, h % 2
                dve.wait_ge(s_e, n + 3)
                nc.vector.reciprocal(ri[:, q:q + 1], sm[:, q:q + 1]).then_inc(s_ri, 1)
                dve.wait_ge(s_ri, n + 1)
                nc.vector.tensor_scalar(pr[:, q, :], pr[:, q, :], ri[:, q:q + 1], None, ALU.mult).then_inc(s_pn, 1)

            def back(c, h):
                n, q = c * 4 + h, h % 2
                dve.wait_ge(s_pt, n + 3)
                if not (isinstance(c, int) and c == 0 and h < 2):
                    dve.wait_ge(s_o, n - 1)
                nc.vector.tensor_copy(pT[:, q, :], ps[:, PT + q, 0:ML]).then_inc(s_pc, 1)

            def body(c, first, last_):
                for h in range(MH):
                    if h < MH - 1:
                        front(c, h + 1)
                    elif not last_:
                        front(c + 1, 0)
                    mid_(c, h)
                    back(c, h)

            front(0, 0)
            chunks(dve, body)


def stage_attention_sample(g, qT, oT):
    nc, ps, d = g.nc, g.psum, g.d
    k_in = d["cache_mem_k"][0].rearrange("b m h e -> b m (h e)")
    v_in = d["cache_mem_v"][0].rearrange("b m h e -> b m (h e)")
    KT, S, PT, O = 0, 4, 5, 6
    with ExitStack() as ctx:
        kr = g.sb("d_k", [P, 2, MT, D], ctx=ctx)
        vr = g.sb("d_v", [P, 2, MT, D], ctx=ctx)
        kT = g.sb("d_kT", [P, DK, ML], ctx=ctx)
        pr = g.sb("d_p", [P, ML], ctx=ctx)
        pT = g.sb("d_pT", [P, MT, P], ctx=ctx)
        st = g.sb("d_stats", [P, 4], ctx=ctx)
        s_k = [g.sem(f"d_k_loaded{i}") for i in range(2)]
        s_v = [g.sem(f"d_v_loaded{i}") for i in range(2)]
        s_tr, s_ka, s_kv, s_s, s_mx, s_nb, s_e, s_ri, s_pn, s_pt, s_pc, s_o, s_oc = (g.sem("d_" + x) for x in (
            "k_turned", "kT_lower", "kT_upper", "scores", "max", "nbias", "exp", "rsum", "p_normed",
            "p_turned", "pT_ready", "values", "o_written"))
        block = ctx.enter_context(nc.Block("attention_sample"))

        @block.sync
        def _(sp):
            def load(ring, src, s, sem):
                sp.dma_start(ring[:, s], src.rearrange("(t p) n -> p t n", p=P)).then_inc(sem, 16)
            for s in range(2):
                load(kr, k_in[s], s, s_k[s])
                load(vr, v_in[s], s, s_v[s])
            with sp.Fori(1, NB // 2) as i:
                for s in range(2):
                    sp.wait_ge(s_tr, i * 2 + s - 1)
                    load(kr, k_in[i * 2 + s], s, s_k[s])
                    sp.wait_ge(s_o, i * 2 + s - 1)
                    load(vr, v_in[i * 2 + s], s, s_v[s])

        def pairs(eng, step):
            with eng.Fori(0, NB // 2 - 1) as i:
                for s in range(2):
                    step(i, s, False)
            for s in range(2):
                step(NB // 2 - 1, s, s == 1)

        @block.tensor
        def _(pe):
            def turn_keys(i, s):
                n = i * 2 + s
                pe.wait_ge(s_k[s], i * 16 + 16)
                pe.wait_ge(s_ka, n)
                pe.wait_ge(s_kv, n)
                for k in range(DK):
                    for t in range(MT):
                        at = (k % 2) * ML + t * P
                        tr = nc.tensor.transpose(ps[:, KT + k // 2, at:at + P], kr[:, s, t, k * P:(k + 1) * P],
                                                 g.ident[:])
                tr.then_inc(s_tr, 1)

            def step(i, s, last_):
                n = i * 2 + s
                pe.wait_ge(s_ka, n + 1)
                pe.wait_ge(s_kv, n + 1)
                pe.wait_ge(s_e, n)
                for h in range(MH):
                    for k in range(2):
                        mm = nc.tensor.matmul(ps[h * NS:(h + 1) * NS, S, 0:ML], qT[:, 2 * h + k, SEQ:T],
                                              kT[:, 2 * h + k, :], start=(k == 0), stop=(k == 1))
                mm.then_inc(s_s, 1)
                if not last_:
                    turn_keys(*((i + 1, 0) if s else (i, 1)))
                pe.wait_ge(s_pn, n + 1)
                pe.wait_ge(s_pc, n)
                for t in range(MT):
                    tr = nc.tensor.transpose(ps[:, PT, t * P:(t + 1) * P], pr[:, t * P:(t + 1) * P], g.ident[:])
                tr.then_inc(s_pt, 1)
                pe.wait_ge(s_pc, n + 1)
                pe.wait_ge(s_v[s], i * 16 + 16)
                pe.wait_ge(s_oc, n)
                for k in range(DK):
                    for t in range(MT):
                        mm = nc.tensor.matmul(ps[:, O, k * NS:(k + 1) * NS], vr[:, s, t, k * P:(k + 1) * P],
                                              pT[:, t, (k // 2) * NS:(k // 2 + 1) * NS],
                                              start=(t == 0), stop=(t == MT - 1))
                mm.then_inc(s_o, 1)

            turn_keys(0, 0)
            pairs(pe, step)

        @block.scalar
        def _(act):
            def keys(n):
                act.wait_ge(s_tr, n + 1)
                act.wait_ge(s_s, n)
                nc.scalar.copy(kT[:, 0:DK // 2, :].rearrange("p k m -> p (k m)"),
                               ps[:, 0:2, :].rearrange("p b t -> p (b t)")).then_inc(s_ka, 1)

            def step(i, s, last_):
                n = i * 2 + s
                act.wait_ge(s_nb, n + 1)
                act.wait_ge(s_pt, n)
                nc.scalar.activation(pr[:], ps[:, S, 0:ML], ACT.Exp, bias=st[:, 1:2], scale=SCALE,
                                     accum_out=st[:, 2:3]).then_inc(s_e, 1)
                if not last_:
                    keys(n + 1)

            keys(0)
            pairs(act, step)

        @block.vector
        def _(dve):
            def keys(n):
                dve.wait_ge(s_tr, n + 1)
                dve.wait_ge(s_s, n)
                nc.vector.tensor_copy(kT[:, DK // 2:DK, :].rearrange("p k m -> p (k m)"),
                                      ps[:, 2:4, :].rearrange("p b t -> p (b t)")).then_inc(s_kv, 1)

            def step(i, s, last_):
                n = i * 2 + s
                dve.wait_ge(s_s, n + 1)
                nc.vector.reduce_max(st[:, 0:1], ps[:, S, 0:ML], AX).then_inc(s_mx, 1)
                dve.wait_ge(s_mx, n + 1)
                nc.vector.tensor_scalar(st[:, 1:2], st[:, 0:1], -SCALE, None, ALU.mult).then_inc(s_nb, 1)
                dve.wait_ge(s_e, n + 1)
                nc.vector.reciprocal(st[:, 3:4], st[:, 2:3]).then_inc(s_ri, 1)
                dve.wait_ge(s_ri, n + 1)
                nc.vector.tensor_scalar(pr[:], pr[:], st[:, 3:4], None, ALU.mult).then_inc(s_pn, 1)
                dve.wait_ge(s_pt, n + 1)
                dve.wait_ge(s_o, n)
                nc.vector.tensor_copy(pT[:].rearrange("p t l -> p (t l)"), ps[:, PT, 0:ML]).then_inc(s_pc, 1)
                if not last_:
                    keys(n + 1)
                dve.wait_ge(s_o, n + 1)
                nc.vector.tensor_copy(oT[:, :, bass.ds(n * LS + SEQ, LS)],
                                      ps[:, O, 0:DK * NS].rearrange("p (k t) -> p k t", t=NS)[:, :, bass.ds(n * LS, LS)]
                                      ).then_inc(s_oc, 1)

            keys(0)
            pairs(dve, step)


def stage_router(g, hT, m):
    nc, ps, d = g.nc, g.psum, g.d
    NR = NG + NE
    with ExitStack() as ctx:
        wr = g.sb("o_w", [P, DK, NR], ctx=ctx)
        rb = g.sb("o_bias", [P, NR], ctx=ctx)
        lg = g.sb("o_logits", [P, NT, NR], ctx=ctx)
        t4 = g.sb("o_t4", [P, NT, 4], ctx=ctx)
        oh = g.sb("o_onehot", [P, 3, NT, 4], ctx=ctx)
        le = g.sb("o_chosen", [P, NT, 4], ctx=ctx)
        t16 = g.sb("o_t16", [P, NT, NE], ctx=ctx)
        mx = g.sb("o_max", [P, 3, NT], ctx=ctx)
        sc = g.sb("o_scalars", [P, 4, NT], ctx=ctx)
        M = g.sb("o_picks", [P, 3, NT, NE], ctx=ctx)
        run = g.sb("o_before", [P, NT + 1, NE], ctx=ctx)
        pos = g.sb("o_pos", [P, NT, NE], ctx=ctx)
        cnt = g.sb("o_counts", [P, NE], ctx=ctx)
        nbk = g.sb("o_blocks", [P, NE], ctx=ctx)
        ends = g.sb("o_ends", [P, NE], ctx=ctx)
        base = g.sb("o_base", [P, NE], ctx=ctx)
        thr = g.sb("o_thresholds", [P, NT], ctx=ctx)
        prio = g.sb("o_priority", [P, 4], ctx=ctx)
        low = g.sb("o_lower", [P, NE, NE], ctx=ctx)
        c9 = g.sb("o_c9", [P, NE, NT], ctx=ctx)
        valid = g.sb("o_valid", [P, NT], ctx=ctx)
        dst = g.sb("o_dest", [P, 2, NT], ctx=ctx)
        tok = g.sb("o_tokens", [P, NT], U32, ctx=ctx)
        zt = g.sb("o_zero", [P, NSLOT // P + 1], U32, ctx=ctx)
        s_res, s_w, s_c, s_c2, s_lg, s_v, s_x, s_p, s_tz, s_sc, s_done = (g.sem("o_" + x) for x in (
            "residual_stored", "w_loaded", "constants", "constants2", "logits", "vector", "exp", "prefix", "table_zeroed",
            "scattered", "tables"))
        block = ctx.enter_context(nc.Block("router"))

        @block.sync
        def _(sp):
            with nc.allow_non_contiguous_dma(reason="20 columns of the routers"):
                sp.dma_start(wr[:, :, 0:NG], d["w_router_group"][0].rearrange("(k p) n -> p k n", p=P)).then_inc(s_w, 16)
                sp.dma_start(wr[:, :, NG:NR], d["w_router_expert"][0].rearrange("(k p) n -> p k n", p=P)).then_inc(s_w, 16)
            sp.dma_start(rb[:, 0:NG], g.flat["b_router_group"].partition_broadcast(P)).then_inc(s_w, 16)
            sp.dma_start(rb[:, NG:NR], g.flat["b_router_expert"].partition_broadcast(P)).then_inc(s_w, 16)
            for ap, dst in g.residual(g.R2):
                sp.dma_start(dst, ap).then_inc(s_res, 16)
            sp.wait_ge(s_c, 1)
            sp.dma_start(g.tok_scr.rearrange("(p b) o -> p (b o)", p=P), zt[:]).then_inc(s_tz, 16)
            sp.wait_ge(s_lg, 1)
            for p in range(GU):
                g.load_piece(sp, 0, p)
            sp.wait_ge(s_res, 32)
            for p in range(GU, PIECES):
                g.load_piece(sp, 0, p)

        @block.gpsimd
        def _(pool):
            nc.gpsimd.memset(zt[:], 0).then_inc(s_c, 1)
            nc.gpsimd.iota(tok[:], [[P, NT]], 0, 1)
            it = dict(allow_small_or_imprecise_dtypes=True)
            nc.gpsimd.iota(thr[:], [[P, NT]], 0, 0, **it)
            nc.gpsimd.iota(prio[:], [[-1, 4]], 4, 0, **it)
            nc.gpsimd.memset(low[:], 1.0)
            nc.gpsimd.memset(valid[:, 0:NC], 1.0)
            nc.gpsimd.memset(valid[:, NC:NT], 0.0)
            nc.gpsimd.memset(run[:, 0, :], 0.0).then_inc(s_c, 1)
            pool.wait_ge(s_c, 2)
            nc.gpsimd.memset(valid[0:NS, NC:NT], 1.0)
            nc.gpsimd.affine_select(low[:], low[:], [[1, NE], [-1, NE]], ALU.is_ge, 0.0, 0, 0).then_inc(s_c2, 1)
            pool.wait_ge(s_done, 1)
            pool.wait_ge(s_tz, 16)
            for c in range(NT):
                n = P if c < NC else NS
                for k in range(2):
                    nc.gpsimd.indirect_dma_start(
                        out=g.tok_scr, out_offset=bass.IndirectOffsetOnAxis(ap=m.slot[0:n, k, c:c + 1], axis=0),
                        in_=tok[0:n, c:c + 1], in_offset=None).then_inc(s_sc, 16)
            pool.wait_ge(s_sc, 16 * 2 * NT)

        @block.tensor
        def _(pe):
            pe.wait_ge(s_w, 64)
            for c in range(NT):
                for k in range(DK):
                    mm = nc.tensor.matmul(ps[:, 0, c * NR:(c + 1) * NR], hT[:, k, c * P:(c + 1) * P], wr[:, k, :],
                                          start=(k == 0), stop=(k == DK - 1))
            mm.then_inc(s_lg, 1)
            pe.wait_ge(s_p, 1)
            nc.tensor.matmul(ps[:, 1, 0:NT * NE], g.stri[:], M[:, 2].rearrange("p c e -> p (c e)"), start=True, stop=False)
            nc.tensor.matmul(ps[:, 1, 0:NT * NE], g.ones[:], run[:, 0:NT].rearrange("p c e -> p (c e)"),
                             start=False, stop=True)
            nc.tensor.matmul(ps[:, 2, 0:NE], g.ones[:], run[:, NT, :], start=True, stop=True).then_inc(s_lg, 1)

        @block.scalar
        def _(act):
            act.wait_ge(s_x, 1)
            nc.scalar.activation(t4[:], t4[:], ACT.Exp).then_inc(s_x, 1)
            act.wait_ge(s_x, 3)
            nc.scalar.activation(sc[:, 0, :], sc[:, 0, :], ACT.Exp).then_inc(s_x, 1)

        @block.vector
        def _(dve):
            ch = Chain(dve, s_v)
            tt, ts = nc.vector.tensor_tensor, nc.vector.tensor_scalar

            def tile4(ap):
                return ap.unsqueeze(2).to_broadcast([P, NT, 4])

            def first_of(o, vals, top):
                ch.done(tt(o, vals, tile4(top), ALU.is_equal))
                ch.done(tt(o, o, mid(prio[:], NT), ALU.mult))
                ch.done(nc.vector.tensor_reduce(sc[:, 3, :], o, AX, ALU.max))
                ch.done(tt(o, o, tile4(sc[:, 3, :]), ALU.is_equal))

            dve.wait_ge(s_lg, 1)
            dve.wait_ge(s_c, 2)
            dve.wait_ge(s_c2, 1)
            ch.done(tt(lg[:], ps[:, 0, 0:NT * NR].rearrange("p (c r) -> p c r", r=NR), mid(rb[:], NT), ALU.add))
            gl = lg[:, :, 0:NG]
            ch.done(nc.vector.tensor_reduce(mx[:, 0, :], gl, AX, ALU.max))
            ch.n += 1
            tt(t4[:], gl, tile4(mx[:, 0, :]), ALU.subtract).then_inc(s_v, 1)
            dve.wait_ge(s_v, ch.n)
            nc.vector.tensor_copy(sc[:, 1, :], mx[:, 0, :]).then_inc(s_x, 1)
            first_of(oh[:, 0], gl, mx[:, 0, :])
            ch.done(tt(t16[:].rearrange("p c (g e) -> p c g e", e=EPG), lg[:, :, NG:NR].rearrange("p c (g e) -> p c g e", e=EPG),
                       oh[:, 0].unsqueeze(3).to_broadcast([P, NT, NG, EPG]), ALU.mult))
            ch.done(nc.vector.tensor_reduce(le[:], t16[:].rearrange("p c (g e) -> p c e g", e=EPG), AX, ALU.add))
            ch.done(nc.vector.tensor_reduce(mx[:, 1, :], le[:], AX, ALU.max))
            first_of(oh[:, 1], le[:], mx[:, 1, :])
            dve.wait_ge(s_x, 2)
            ch.done(nc.vector.tensor_reduce(sc[:, 1, :], t4[:], AX, ALU.add))
            ch.done(ts(t4[:], oh[:, 1], -1.0, 1.0, ALU.mult, ALU.add))
            ch.done(tt(le[:], le[:], t4[:], ALU.mult))
            ch.done(nc.vector.scalar_tensor_tensor(le[:], oh[:, 1], -BIG, le[:], ALU.mult, ALU.add))
            ch.done(nc.vector.tensor_reduce(mx[:, 2, :], le[:], AX, ALU.max))
            first_of(oh[:, 2], le[:], mx[:, 2, :])
            tt(sc[:, 0, :], mx[:, 2, :], mx[:, 1, :], ALU.subtract).then_inc(s_x, 1)
            dve.wait_ge(s_x, 4)
            ch.done(ts(sc[:, 2, :], sc[:, 0, :], 1.0, None, ALU.add))
            ch.done(tt(sc[:, 2, :], sc[:, 2, :], sc[:, 1, :], ALU.mult))
            ch.done(nc.vector.reciprocal(m.wt[:, 0, :], sc[:, 2, :]))
            ch.done(tt(m.wt[:, 1, :], m.wt[:, 0, :], sc[:, 0, :], ALU.mult))
            ch.done(tt(oh[:, 0], oh[:, 0], valid[:].unsqueeze(2).to_broadcast([P, NT, 4]), ALU.mult))
            for k in range(2):
                ch.done(tt(M[:, k].rearrange("p c (g e) -> p c g e", e=EPG),
                           oh[:, 0].unsqueeze(3).to_broadcast([P, NT, NG, EPG]),
                           oh[:, 1 + k].unsqueeze(2).to_broadcast([P, NT, NG, EPG]), ALU.mult))
            ch.done(tt(M[:, 2], M[:, 0], M[:, 1], ALU.add))
            for c in range(NT):
                ch.done(tt(run[:, c + 1, :], run[:, c, :], M[:, 2, c, :], ALU.add))
            nc.vector.tensor_copy(pos[:, 0, 0:1], run[:, NT, 0:1]).then_inc(s_p, 1)
            dve.wait_ge(s_lg, 2)
            ch.done(nc.vector.tensor_copy(cnt[:], ps[:, 2, 0:NE]))
            ch.done(tt(c9[:], last(cnt[:], NT), mid(thr[:], NE), ALU.is_gt))
            ch.done(nc.vector.tensor_reduce(nbk[:], c9[:], AX, ALU.add))
            ch.done(ts(nbk[:], nbk[:], 1.0, None, ALU.max))
            ch.done(tt(low[:], low[:], mid(nbk[:], NE), ALU.mult))
            ch.done(nc.vector.tensor_reduce(ends[:], low[:], AX, ALU.add))
            ch.done(tt(base[:], ends[:], nbk[:], ALU.subtract))
            ch.done(ts(base[:], base[:], float(P), None, ALU.mult))
            ch.done(tt(pos[:], ps[:, 1, 0:NT * NE].rearrange("p (c e) -> p c e", e=NE), mid(base[:], NT), ALU.add))
            for k in range(2):
                ch.done(tt(t16[:], pos[:], M[:, k], ALU.mult))
                ch.done(nc.vector.tensor_reduce(dst[:, k, :], t16[:], AX, ALU.add))
            ch.done(nc.vector.tensor_copy(m.slot[:], dst[:]))
            ch.done(ts(base[:], base[:], 1.0 / P, None, ALU.mult))
            ch.done(nc.vector.tensor_copy(m.start[:], base[:]))
            ch.done(ts(nbk[:], nbk[:], -1.0, None, ALU.add))
            nc.vector.tensor_copy(m.more[:], nbk[:]).then_inc(s_done, 1)


PC = DK * FF // 2
PIECES = 6
GU = 4
DW = PIECES - GU


def place_pieces(g):
    d = g.d
    weights = [d[n][0].rearrange("e (k p) n -> e p k n", p=P)
               for n in ("w_expert_gate", "w_expert_up", "w_expert_down")]
    g.pieces = g.big[:, 0:PIECES * PC].rearrange("p (q n) -> p q n", n=PC)
    g.s_piece = [g.sem(f"e_piece_loaded{i}") for i in range(PIECES)]

    def load_piece(sp, e, p):
        half, kt = p % 2, (DK, DK, FK)[p // 2] // 2
        src = weights[p // 2][e][:, half * kt:(half + 1) * kt, :]
        sp.dma_start(g.pieces[:, p, :].rearrange("p (k n) -> p k n", k=kt), src).then_inc(g.s_piece[p], 16)
    g.load_piece = load_piece


def stage_experts(g, m):
    nc, ps, d = g.nc, g.psum, g.d
    X, GA, UP, HT, DN = 0, 2, 3, 4, 5
    out_v = g.moe_scr.rearrange("(b p) n -> b p n", p=P)
    with ExitStack() as ctx:
        raw, s_w = g.pieces, g.s_piece
        wh = g.sb("e_w_high", [P, PIECES, PC], F32R, ctx=ctx)
        wl = g.sb("e_w_low", [P, PIECES, PC], F32R, ctx=ctx)
        tab = g.sb("e_table", [P, NBLK + 1], U32, ctx=ctx)
        idx = g.sb("e_idx", [P, 1], U32, ctx=ctx)
        xb = g.sb("e_x", [P, D], ctx=ctx)
        xh = g.sb("e_xT_high", [P, DK, P], F32R, ctx=ctx)
        xl = g.sb("e_xT_low", [P, DK, P], F32R, ctx=ctx)
        sg = g.sb("e_silu", [P, FF], ctx=ctx)
        hh = g.sb("e_h", [P, FF], ctx=ctx)
        hth = g.sb("e_hT_high", [P, FK, P], F32R, ctx=ctx)
        htl = g.sb("e_hT_low", [P, FK, P], F32R, ctx=ctx)
        ob = g.sb("e_out", [P, D], ctx=ctx)
        s_t = g.sem("e_table_loaded")
        s_ix = g.sem("e_idx_ready")
        s_go = g.sem("e_waited")
        s_x = g.sem("e_x_gathered")
        s_wh, s_wl, s_dh, s_dl, s_res, s_xt, s_xh, s_xl, s_g, s_u, s_sg, s_h, s_ht, s_hh, s_hl, s_dn, s_oc, s_o, s_of = (
            g.sem("e_" + x) for x in (
                "w_high", "w_low", "down_high", "down_low", "residual_loaded", "x_turned", "x_high", "x_low", "gate", "up", "silu",
                "h", "h_turned", "h_high", "h_low", "down", "out_copied", "out_stored", "out_free"))
        block = ctx.enter_context(nc.Block("experts"))

        def start(eng, e):
            return eng.value_load(m.start[0:1, bass.ds(e, 1)], min_val=0, max_val=NBLK)

        def more(eng, e):
            return eng.value_load(m.more[0:1, bass.ds(e, 1)], min_val=0, max_val=NBLK)

        def within(b):
            return nc.s_assert_within(b, 0, NBLK - 2, skip_runtime_bounds_check_because=(
                "an expert's blocks are at most its slots over 128 and one more, NBLK - 1 in all"))

        def each_block(eng, plain, last_of):
            def expert(e, final):
                first, n = start(eng, e), more(eng, e)
                with eng.If(n > 0):
                    with eng.Fori(0, n) as i:
                        plain(e, i, within(first + i))
                last_of(e, n, within(first + n), final)

            with eng.Fori(0, NE - 1) as e:
                expert(e, False)
            expert(NE - 1, True)

        def flat(ap):
            return ap.rearrange("p b t -> p (b t)")

        @block.sync
        def _(sp):
            with nc.allow_non_contiguous_dma(reason="one slot's token per element"):
                sp.dma_start(tab[:], g.tok_scr.rearrange("(b p) o -> p (b o)", p=P)).then_inc(s_t, 16)

            def load(e, pieces):
                for p in pieces:
                    if p < GU:
                        sp.wait_ge(s_wl, (e - 1) * GU + p + 1)
                    else:
                        sp.wait_ge(s_dl, (e - 1) * DW + p - GU + 1)
                    g.load_piece(sp, e, p)

            load(1, range(GU))
            with sp.Fori(0, NE - 2) as e:
                load(e + 2, range(GU))
                load(e + 1, range(GU, PIECES))
            load(NE - 1, range(GU, PIECES))
            sp.wait_ge(s_wl, NE * GU)
            sp.wait_ge(s_dl, NE * DW)
            for ap, src in g.residual(g.R2):
                sp.dma_start(ap, src).then_inc(s_res, 16)
            sp.wait_ge(s_res, 32)

        @block.gpsimd
        def _(pool):
            pool.wait_ge(s_t, 16)

            def gather(b):
                pool.wait_ge(s_xt, b + 1)
                pool.sem_inc(s_go, 1)
                nc.gpsimd.tensor_copy(idx[:], tab[:, bass.ds(b, 1)]).then_inc(s_ix, 1)
                pool.wait_ge(s_ix, b + 1)
                pool.sem_inc(s_go, 1)
                nc.gpsimd.indirect_dma_start(
                    out=xb[:], out_offset=None, in_=g.h_scr,
                    in_offset=bass.IndirectOffsetOnAxis(ap=idx[:, 0:1], axis=0)).then_inc(s_x, 16)

            def finish(b):
                pool.wait_ge(s_oc, b + 1)
                pool.sem_inc(s_go, 1)
                nc.gpsimd.dma_start(out_v[b], ob[:]).then_inc(s_o, 16)
                pool.wait_ge(s_o, b * 16 + 16)
                pool.sem_inc(s_of, 1)

            for b in range(3):
                gather(b)
            nb = within(start(pool, NE - 1) + more(pool, NE - 1))
            with pool.Fori(0, nb) as b:
                gather(b + 3)
                finish(b)
            finish(nb)
            pool.wait_ge(s_x, nb * 16 + 48)
            pool.sem_inc(s_go, 1)

        @block.tensor
        def _(pe):
            pe.sem_inc(s_xt, 1)

            def turn(b):
                pe.wait_ge(s_x, b * 16 + 16)
                pe.wait_ge(s_xl, b)
                for k in range(DK):
                    tr = nc.tensor.transpose(ps[:, X + k // 4, (k % 4) * P:(k % 4 + 1) * P],
                                             xb[:, k * P:(k + 1) * P], g.ident[:])
                tr.then_inc(s_xt, 1)

            def product(bank, ah, al, p, kt, n, col, split):
                for k in range(kt):
                    half = k // (kt // 2)
                    if k % (kt // 2) == 0:
                        split(half)
                    q, at = p + half, (k % (kt // 2)) * n + col
                    w_h, w_l = wh[:, q, at:at + BANK], wl[:, q, at:at + BANK]
                    nc.tensor.matmul(ps[:, bank, :], ah[:, k, :], w_h, start=(k == 0), stop=False)
                    nc.tensor.matmul(ps[:, bank, :], ah[:, k, :], w_l, start=False, stop=False)
                    mm = nc.tensor.matmul(ps[:, bank, :], al[:, k, :], w_h, start=False, stop=(k == kt - 1))
                return mm

            def hidden(e, b):
                pe.wait_ge(s_xl, b + 1)
                pe.wait_ge(s_sg, b)
                product(GA, xh, xl, 0, DK, FF, 0, lambda i: pe.wait_ge(s_wl, e * GU + 1 + i)).then_inc(s_g, 1)
                pe.wait_ge(s_h, b)
                product(UP, xh, xl, 2, DK, FF, 0, lambda i: pe.wait_ge(s_wl, e * GU + 3 + i)).then_inc(s_u, 1)
                turn(b + 1)

            def down(e, b):
                pe.wait_ge(s_hl, b + 1)
                pe.wait_ge(s_oc, b)
                for j in range(2):
                    mm = product(DN + j, hth, htl, 4, FK, D, j * BANK,
                                 lambda i: pe.wait_ge(s_dl, e * DW + 1 + i))
                mm.then_inc(s_dn, 1)

            def turn_h(b):
                pe.wait_ge(s_h, b + 1)
                pe.wait_ge(s_hl, b)
                for k in range(FK):
                    tr = nc.tensor.transpose(ps[:, HT, k * P:(k + 1) * P], hh[:, k * P:(k + 1) * P], g.ident[:])
                tr.then_inc(s_ht, 1)

            def others(e, first):
                n = more(pe, e)
                with pe.If(n > 0):
                    with pe.Fori(0, n) as i:
                        b = within(first + i)
                        hidden(e, b + 1)
                        down(e, b)
                        turn_h(b + 1)

            turn(0)
            hidden(0, 0)
            turn_h(0)
            others(0, 0)
            with pe.Fori(0, NE - 1) as e:
                b = within(start(pe, e) + more(pe, e))
                hidden(e + 1, b + 1)
                down(e, b)
                turn_h(b + 1)
                others(e + 1, b + 1)
            down(NE - 1, within(start(pe, NE - 1) + more(pe, NE - 1)))

        @block.scalar
        def _(act):
            def copy_(dst, src):
                return nc.scalar.activation(dst, src, ACT.Copy)

            def turned(b):
                act.wait_ge(s_xt, b + 2)
                act.wait_ge(s_u, b)
                copy_(xh[:].rearrange("p k t -> p (k t)"), flat(ps[:, X:X + 2, :])).then_inc(s_xh, 1)

            def high(e, p):
                act.wait_ge(s_w[p], e * 16 + 16)
                copy_(wh[:, p, :], raw[:, p, :]).then_inc(s_wh, 1)

            def high_down(e, p):
                act.wait_ge(s_w[p], e * 16 + 16)
                copy_(wh[:, p, :], raw[:, p, :]).then_inc(s_dh, 1)

            def silu(b):
                act.wait_ge(s_g, b + 1)
                act.wait_ge(s_h, b)
                nc.scalar.activation(sg[:], ps[:, GA, :], ACT.Silu).then_inc(s_sg, 1)

            def h_high(b):
                act.wait_ge(s_ht, b + 1)
                act.wait_ge(s_dn, b)
                copy_(hth[:].rearrange("p k t -> p (k t)"), ps[:, HT, :]).then_inc(s_hh, 1)

            def down_parts(e):
                act.wait_ge(s_dn, start(act, e))
                high_down(e, 4)
                high_down(e, 5)

            def out(n):
                act.wait_ge(s_dn, n)
                act.wait_ge(s_of, n)
                copy_(ob[:], flat(ps[:, DN:DN + 2, :])).then_inc(s_oc, 1)

            def plain(e, i, b):
                silu(b)
                turned(b + 1)
                with act.If(b > 0):
                    out(b)
                with act.If(i < 1):
                    down_parts(e)
                h_high(b)

            def last_of(e, n, b, final):
                silu(b)
                if not final:
                    high(e + 1, 0)
                    high(e + 1, 1)
                turned(b + 1)
                if not final:
                    high(e + 1, 2)
                    high(e + 1, 3)
                with act.If(b > 0):
                    out(b)
                with act.If(n < 1):
                    down_parts(e)
                h_high(b)
                if final:
                    out(b + 1)

            act.sem_inc(s_of, 1)
            turned(0)
            for p in range(GU):
                high(0, p)
            each_block(act, plain, last_of)

        @block.vector
        def _(dve):

            def turned(b):
                dve.wait_ge(s_xh, b + 1)
                nc.vector.tensor_tensor(xl[:].rearrange("p k t -> p (k t)"), flat(ps[:, X:X + 2, :]),
                                        xh[:].bitcast(F32).rearrange("p k t -> p (k t)"), ALU.subtract).then_inc(s_xl, 1)

            def low(e, p):
                dve.wait_ge(s_wh, e * GU + p + 1)
                nc.vector.tensor_tensor(wl[:, p, :], raw[:, p, :], wh[:, p, :].bitcast(F32),
                                        ALU.subtract).then_inc(s_wl, 1)

            def gated(b):
                dve.wait_ge(s_sg, b + 1)
                dve.wait_ge(s_u, b + 1)
                dve.wait_ge(s_ht, b)
                nc.vector.tensor_tensor(hh[:], sg[:], ps[:, UP, :], ALU.mult).then_inc(s_h, 1)

            def h_low(b):
                dve.wait_ge(s_hh, b + 1)
                nc.vector.tensor_tensor(htl[:].rearrange("p k t -> p (k t)"), ps[:, HT, :],
                                        hth[:].bitcast(F32).rearrange("p k t -> p (k t)"), ALU.subtract).then_inc(s_hl, 1)

            def down_parts(e):
                for p in range(GU, PIECES):
                    dve.wait_ge(s_dh, e * DW + p - GU + 1)
                    nc.vector.tensor_tensor(wl[:, p, :], raw[:, p, :], wh[:, p, :].bitcast(F32),
                                            ALU.subtract).then_inc(s_dl, 1)

            def plain(e, i, b):
                gated(b)
                turned(b + 1)
                with dve.If(i < 1):
                    down_parts(e)
                h_low(b)

            def last_of(e, n, b, final):
                if not final:
                    low(e + 1, 0)
                    low(e + 1, 1)
                gated(b)
                turned(b + 1)
                if not final:
                    low(e + 1, 2)
                    low(e + 1, 3)
                with dve.If(n < 1):
                    down_parts(e)
                h_low(b)

            turned(0)
            for p in range(GU):
                low(0, p)
            each_block(dve, plain, last_of)


def stage_final(g, x, m):
    nc = g.nc
    RING = 3
    with ExitStack() as ctx:
        a = g.sb("f_first", [P, RING, D], ctx=ctx)
        b = g.sb("f_second", [P, RING, D], ctx=ctx)
        y = g.sb("f_y", [P, RING, D], ctx=ctx)
        junk = g.sb("f_junk", [P, D], ctx=ctx)
        gf = g.sb("f_gain", [P, D], ctx=ctx)
        ss = g.sb("f_ss", [P, NT], ctx=ctx)
        s_g = g.sem("f_gain_loaded")
        s_l = [g.sem(f"f_gathered{i}") for i in range(RING)]
        s_a, s_x, s_ss, s_ms, s_rs, s_y = (g.sem("f_" + x_) for x_ in (
            "first_added", "x_ready", "squares", "mean", "rstd", "y_ready"))
        s_o = [g.sem(f"f_stored{i}") for i in range(RING)]
        block = ctx.enter_context(nc.Block("final"))

        def rows(c):
            return P if c < NC else NS

        @block.sync
        def _(sp):
            sp.dma_start(gf[:], g.flat["norm_final"].partition_broadcast(P)).then_inc(s_g, 16)
            for c in range(NT):
                sp.wait_ge(s_y, c + 1)
                dst = g.out["y_p"][c * P:(c + 1) * P, :] if c < NC else g.out["y_s"]
                sp.dma_start(dst, y[0:rows(c), c % RING, :]).then_inc(s_o[c % RING], 16)
            for q in range(RING):
                sp.wait_ge(s_o[q], 16 * (NT // RING))

        @block.gpsimd
        def _(pool):
            def gather(c):
                n, q = rows(c), c % RING
                for k, dst in enumerate((a, b)):
                    nc.gpsimd.indirect_dma_start(
                        out=dst[0:n, q, :], out_offset=None, in_=g.moe_scr,
                        in_offset=bass.IndirectOffsetOnAxis(ap=m.slot[0:n, k, c:c + 1], axis=0)).then_inc(s_l[q], 16)

            for c in range(RING):
                gather(c)
            for c in range(NT):
                n = rows(c)
                pool.wait_ge(s_ss, c + 1)
                nc.gpsimd.tensor_scalar(ss[0:n, c:c + 1], ss[0:n, c:c + 1], 1.0 / D, EPS, ALU.mult, ALU.add).then_inc(s_ms, 1)
                pool.wait_ge(s_ms, c + 1)
                nc.gpsimd.tensor_tensor(ss[0:n, c:c + 1], ss[0:n, c:c + 1], g.mhalf[0:n, 0:1], ALU.pow).then_inc(s_rs, 1)
                if c + RING < NT:
                    gather(c + RING)

        @block.scalar
        def _(act):
            for c in range(NT):
                n = rows(c)
                act.wait_ge(s_x, c + 1)
                act.wait_ge(s_ss, c)
                nc.scalar.activation(junk[0:n, :], x[0:n, c, :], ACT.Square, accum_out=ss[0:n, c:c + 1]).then_inc(s_ss, 1)

        @block.vector
        def _(dve):
            def add(c):
                n, q = rows(c), c % RING
                xc = x[0:n, c, :]
                dve.wait_ge(s_l[q], 32 * (c // RING + 1))
                nc.vector.scalar_tensor_tensor(xc, a[0:n, q, :], m.wt[0:n, 0, c:c + 1], xc, ALU.mult, ALU.add).then_inc(s_a, 1)
                dve.wait_ge(s_a, c + 1)
                nc.vector.scalar_tensor_tensor(xc, b[0:n, q, :], m.wt[0:n, 1, c:c + 1], xc, ALU.mult, ALU.add).then_inc(s_x, 1)

            dve.wait_ge(s_g, 16)
            add(0)
            for c in range(NT):
                n, q = rows(c), c % RING
                if c + 1 < NT:
                    add(c + 1)
                dve.wait_ge(s_rs, c + 1)
                if c >= RING:
                    dve.wait_ge(s_o[q], 16 * (c // RING))
                nc.vector.scalar_tensor_tensor(y[0:n, q, :], x[0:n, c, :], ss[0:n, c:c + 1], gf[0:n, :],
                                               ALU.mult, ALU.mult).then_inc(s_y, 1)


class Tables:

    def __init__(self, g, ctx):
        self.wt = g.sb("wt", [P, 2, NT], ctx=ctx)
        self.slot = g.sb("slot", [P, 2, NT], U32, ctx=ctx)
        self.start = g.sb("start", [P, NE], I32, ctx=ctx)
        self.more = g.sb("more", [P, NE], I32, ctx=ctx)


def build(nc, d, out, stages=99):
    g = Prog(nc, d, out, stages)
    flat = {}
    for n in ("conv_w", "conv_b", "norm_mix", "norm_mem", "norm_memkv", "norm_ffn", "b_gate", "ssm_norm",
              "dt_bias", "d_skip", "gm_ln_g", "gm_ln_b", "gm_bs", "b_router_group", "b_router_expert", "norm_final"):
        a = d[n]
        names = " ".join("abcd"[:len(a.shape)])
        flat[n] = a.rearrange(f"{names} -> ({names})") if len(a.shape) > 1 else a
    g.flat = flat
    g.x_scr = nc.dram_tensor("x_scr", [NC, P, CF, P], F32, kind="Internal").ap()
    g.z_scr = nc.dram_tensor("z_scr", [NT, P, DI], F32, kind="Internal").ap()
    g.h_scr = nc.dram_tensor("h_scr", [TP, D], F32, kind="Internal").ap()
    g.moe_scr = nc.dram_tensor("moe_scr", [NSLOT, D], F32, kind="Internal").ap()
    g.gate_scr = nc.dram_tensor("gate_scr", [2 * DK, P, T], F32, kind="Internal").ap()
    g.merged_scr = nc.dram_tensor("merged_scr", [DK, P, T], F32, kind="Internal").ap()
    res_scr = nc.dram_tensor("res_scr", [TP, D], F32, kind="Internal").ap()
    g.tok_scr = nc.dram_tensor("tok_scr", [NSLOT + P, 1], U32, kind="Internal").ap()
    with g.ctx as top:
        g.psum = top.enter_context(nc.psum_tensor("psum", [P, 8, BANK], F32))
        g.ident = g.sb("ident", [P, P])
        g.ones = g.sb("ones", [P, P])
        g.tri = g.sb("tri", [P, P])
        g.stri = g.sb("stri", [P, P])
        g.same = g.sb("same", [NS, NS])
        g.btri = g.sb("btri", [NS, NS])
        g.colmask = g.sb("colmask", [P, NB, NS])
        g.rowmask = g.sb("rowmask", [NS, NB])
        g.mhalf = g.sb("mhalf", [P, 16])
        g.eps = g.sb("eps", [P, 1])
        g.veca = g.sb("veca", [P, VEC_A])
        g.vecb = g.sb("vecb", [P, VEC_B])
        g.s_out = nc.alloc_semaphore("outputs_stored")
        g.big, big_at = g.sb_at("big", [P, 2 * NT * D])
        big1, big2 = g.big[:, 0:NT * D], g.big[:, NT * D:]
        g.R1, g.R2 = (b.rearrange("p (t n) -> p t n", n=D) for b in (big1, big2))
        g.R1T, g.R2T = (b.rearrange("p (k t) -> p k t", t=TP) for b in (big1, big2))

        g.R1_low = g.alias("R1_low", [P, DK, TP], big_at)
        g.hT_high = g.alias("hT_high", [P, DK, TP], big_at)
        g.hT_low = g.alias("hT_low", [P, DK, TP], big_at + NT * D * 4)

        def gain(name):
            return g.vecb[:, VEC[name]:VEC[name] + DK]

        def x_load(x):
            return [(x[:, 0:NC, :], d["x_prompt"][0].rearrange("(t p) n -> p t n", p=P)),
                    (x[0:NS, NC, :], d["x_sample"].rearrange("b t n -> (b t) n"))]

        def residual(x):
            return [(x[:, 0:NC, :], res_scr[0:SEQ, :].rearrange("(t p) n -> p t n", p=P)),
                    (x[0:NS, NC, :], res_scr[SEQ:T, :])]
        g.residual = residual

        with ExitStack() as mix:
            g.dtb = g.sb("dtb", [P, H], ctx=mix)
            g.dskip = g.sb("dskip", [P, H], ctx=mix)
            g.aneg = g.sb("aneg", [P, H], ctx=mix)
            g.dt = g.sb("dt", [P, NT, H], ctx=mix)
            g.dta = g.sb("dta", [P, NT, H], ctx=mix)
            g.acs = g.sb("acs", [P, NT, H], ctx=mix)
            g.eacs = g.sb("eacs", [P, NT, H], ctx=mix)
            g.etot = g.sb("etot", [P, NT, H], ctx=mix)
            g.dte = g.sb("dte", [P, NT, H], ctx=mix)
            g.xbs = g.sb("xbs", [P, CF, NS], ctx=mix)
            g.uT, u_at = g.sb_at("uT", [P, GMF, T], ctx=mix)
            with ExitStack() as vs:
                g.v = g.sb("v", [P, NT, GM], ctx=vs)
                g.lng = g.sb("lng", [P, GM], ctx=vs)
                g.lnb = g.sb("lnb", [P, GM], ctx=vs)
                g.bs = g.sb("bs", [P, G, P], ctx=vs)
                g.cst = g.sb("cst", [P, CF, 3 * NB], ctx=vs)
                g.lasts = g.sb("lasts", [P, CF, 27], ctx=vs)
                stage_constants(g)
                stage_norm(g, "norm_mix", g.R1, gain("norm_mix"), g.R2T, NT, x_dram=x_load(g.R1))
                if stages < 2:
                    return
                stage_rows(g)
                with ExitStack() as lr:
                    g.lrow = g.sb("lrow", [27, CD], ctx=lr)
                    stage_turned(g)
                if stages < 3:
                    return
                stage_gmlp(g)
            g.renew_semaphores()
            g.yT, y_at = g.sb_at("yT", [P, XF, T], ctx=mix)
            g.y_parts = (g.alias("yT_high", [P, XF, T], big_at), g.alias("yT_low", [P, XF, T], y_at))
            g.u_parts = (g.alias("uT_high", [P, GMF, T], big_at + XF * T * 4), g.alias("uT_low", [P, GMF, T], u_at))
            stage_ssd(g)
            stage_ssd_sample(g)
            if stages < 4:
                return
            stage_merge(g)
        stage_add_rows(g, "w_out", g.R1T, d["w_out"][0], g.R2, x_load(g.R2), g.merged_scr)
        if stages < 5:
            return
        g.renew_semaphores()
        with ExitStack() as at:
            qT = g.sb("qT", [P, DK, T], ctx=at)
            kT = g.sb("kT", [P, DK, ML], ctx=at)
            vr = g.sb("vr", [P, MT, D], ctx=at)
            stage_norm(g, "norm_mem", g.R2, gain("norm_mem"), g.R1T, NT)
            stage_query(g, g.R1T, qT)
            with ExitStack() as me:
                mr = g.sb("mr", [P, MT, D], ctx=me)
                mT = g.sb("mT", [P, DK, ML], ctx=me)
                stage_norm(g, "norm_memkv", mr, gain("norm_memkv"), mT, MT,
                           x_dram=[(mr[:], d["mem_prompt"][0].rearrange("(t p) n -> p t n", p=P))])
                stage_mem_kv(g, mT, kT, vr)
            stage_attention(g, qT, kT, vr, g.R1T)
            stage_attention_sample(g, qT, g.R1T)
        stage_add_rows(g, "w_mem_o", g.R1T, d["w_mem_o"][0], g.R2)
        if stages < 6:
            return
        g.renew_semaphores()
        with ExitStack() as mo:
            m = Tables(g, mo)
            with ExitStack() as gr:
                row = g.sb("ffn_gain_row", [P, D], ctx=gr)
                stage_row_gain(g, row)
                stage_norm(g, "norm_ffn", g.R2, gain("norm_ffn"), g.R1T, NT, rows_dram=(g.h_scr, row))
            place_pieces(g)
            stage_router(g, g.R1T, m)
            if stages < 7:
                return
            stage_experts(g, m)
            stage_final(g, g.R2, m)


def stage_row_gain(g, row):
    nc = g.nc
    s = g.sem("ffn_gain_loaded")
    with nc.Block("row_gain") as block:
        @block.sync
        def _(sp):
            sp.dma_start(row[:], g.flat["norm_ffn"].partition_broadcast(P)).then_inc(s, 16)
            sp.wait_ge(s, 16)


_OUTS = [("y_p", (1, SEQ, D)), ("y_s", (NB, LS, D)), ("ssm_p", (1, 1, H, HD, N)), ("conv_p", (1, 1, CONV - 1, CD)),
         ("mk", (1, 1, ML, MH, MD)), ("mv", (1, 1, ML, MH, MD)), ("ssm_s", (1, NB, H, HD, N)),
         ("conv_s", (1, NB, CONV - 1, CD)), ("gv", (1, NB, LS, GM))]
STAGES = 99


def kernel(**inputs):
    import concourse.bacc as bacc
    from concourse.bass_utils import run_bass_kernel_spmd

    nc = bacc.Bacc("TRN2", target_bir_lowering=False, num_devices=1)
    arrays, d = {}, {}
    for name, a in inputs.items():
        a = np.ascontiguousarray(a)
        arrays["in_" + name] = a
        d[name] = nc.dram_tensor("in_" + name, a.shape, mybir.dt.from_np(a.dtype), kind="ExternalInput").ap()
    o = {n: nc.dram_tensor("out_" + n, shape, F32, kind="ExternalOutput").ap() for n, shape in _OUTS}
    out = {
        "y_p": o["y_p"][0], "y_s": o["y_s"].rearrange("b t n -> (b t) n"),
        "ssm_p": o["ssm_p"][0, 0].rearrange("h p n -> (h p) n").rearrange("(j p) n -> p j n", p=P),
        "conv_p": o["conv_p"][0, 0], "mk": o["mk"][0, 0].rearrange("m h e -> m (h e)"),
        "mv": o["mv"][0, 0].rearrange("m h e -> m (h e)"),
        "ssm_s": o["ssm_s"][0].rearrange("b h p n -> b (h p) n"),
        "conv_s": o["conv_s"][0].rearrange("b r c -> (b r) c"), "gv": o["gv"][0].rearrange("b t n -> (b t) n"),
    }
    build(nc, d, out, STAGES)
    r = run_bass_kernel_spmd(nc, [arrays], core_ids=[0])
    return tuple(r.results[0]["out_" + n] for n, _ in _OUTS)
```
